# Optimizing a Trainium2 kernel written in Bass

```python
import math
import functools
import jax
import jax.numpy as jnp
from jax import lax
import numpy as np
import jax, jax.numpy as jnp

D_MODEL = 1024
BATCH = 1
SEQ = 256
DEPTH = 1

N_MIXERS = 4
CHUNK = 64
CONV_K = 5
PLE_DIM = 256

GDN_QK_HEADS = 8
GDN_V_HEADS = 16
GDN_HEAD_DIM = 128
GDN_KEY_WIDTH = GDN_QK_HEADS * GDN_HEAD_DIM
GDN_VAL_WIDTH = GDN_V_HEADS * GDN_HEAD_DIM
GDN_CONV_CH = 2 * GDN_KEY_WIDTH + GDN_VAL_WIDTH
GDN_IN = GDN_CONV_CH + GDN_VAL_WIDTH + 4 * GDN_V_HEADS

M2_D_INNER = 2 * D_MODEL
M2_HEAD_DIM = 64
M2_HEADS = M2_D_INNER // M2_HEAD_DIM
M2_GROUPS = 4
M2_HEADS_PER_GROUP = M2_HEADS // M2_GROUPS
M2_STATE = 128
M2_CONV_CH = M2_D_INNER + 2 * M2_GROUPS * M2_STATE
M2_IN = M2_D_INNER + M2_CONV_CH + 2 * M2_HEADS

HG_EXPAND = 128
HG_HEADS = D_MODEL // HG_EXPAND
HG_WIDTH = HG_HEADS * HG_EXPAND
HG_IN = 5 * HG_WIDTH

GLA_HEADS = 4
GLA_KEY_WIDTH = D_MODEL // 2
GLA_VAL_WIDTH = D_MODEL
GLA_K = GLA_KEY_WIDTH // GLA_HEADS
GLA_V = GLA_VAL_WIDTH // GLA_HEADS
GLA_GATE_RANK = 16
GLA_GATE_TEMP = 16.0
GLA_IN = 2 * GLA_KEY_WIDTH + 2 * GLA_VAL_WIDTH + 2 * GLA_GATE_RANK

MOE_GROUPS = 4
MOE_EXPERTS_PER_GROUP = 8
MOE_EXPERTS = MOE_GROUPS * MOE_EXPERTS_PER_GROUP
MOE_TOPK = 2
MOE_HIDDEN = 256

DEEPNORM_ALPHA = (2 * DEPTH) ** 0.25
DEEPNORM_BETA = (8 * DEPTH) ** -0.25
LN_EPS = 1e-5
NORM_EPS = 1e-6
F32 = jnp.float32


def _n_uses(m):
    return (DEPTH - m + N_MIXERS - 1) // N_MIXERS

def _layernorm(t, g, b):
    tf = t.astype(F32)
    mu = jnp.mean(tf, axis=-1, keepdims=True)
    var = jnp.mean(jnp.square(tf - mu), axis=-1, keepdims=True)
    return ((tf - mu) * lax.rsqrt(var + LN_EPS) * g.astype(F32) + b.astype(F32)).astype(t.dtype)

def _rms(t):
    tf = t.astype(F32)
    return tf * lax.rsqrt(jnp.mean(tf * tf, axis=-1, keepdims=True) + NORM_EPS)

def _l2norm(t):
    tf = t.astype(F32)
    return tf * lax.rsqrt(jnp.sum(tf * tf, axis=-1, keepdims=True) + NORM_EPS)

def _dwconv(t, w):
    return lax.conv_general_dilated(
        t, w[:, None, :].astype(t.dtype), window_strides=(1,),
        padding=[(CONV_K // 2, CONV_K // 2)],
        dimension_numbers=("NWC", "WIO", "NWC"),
        feature_group_count=t.shape[-1])

def _rev(t):
    return jnp.flip(t, axis=1)

def _chunks(t):
    bsz, seq = t.shape[:2]
    t = t.reshape(bsz, seq // CHUNK, CHUNK, *t.shape[2:])
    return jnp.swapaxes(jnp.swapaxes(t, 0, 1), 2, 3)

def _unchunks(t):
    t = jnp.swapaxes(jnp.swapaxes(t, 2, 3), 0, 1)
    return t.reshape(t.shape[0], t.shape[1] * t.shape[2], *t.shape[3:])

def _gated_delta_rule(q, k, v, beta, g):
    q, k, v, beta, g = (_chunks(t.astype(F32)) for t in (q, k, v, beta, g))
    gc = jnp.cumsum(g, axis=-1)
    incl = jnp.tril(jnp.ones((CHUNK, CHUNK), dtype=bool))
    decay = jnp.exp(jnp.where(incl, gc[..., :, None] - gc[..., None, :], -jnp.inf))
    eye = jnp.eye(CHUNK, dtype=F32)
    kb = k * beta[..., None]
    lhs = eye + jnp.einsum("nbhik,nbhjk->nbhij", kb, k) * decay * (1.0 - eye)
    solve = functools.partial(lax.linalg.triangular_solve, left_side=True, lower=True,
                              unit_diagonal=True)
    u = solve(lhs, v * beta[..., None])
    w = solve(lhs, kb * jnp.exp(gc)[..., None])
    attn = jnp.einsum("nbhik,nbhjk->nbhij", q, k) * decay
    q_dec = q * jnp.exp(gc)[..., None]
    k_dec = k * jnp.exp(gc[..., -1:] - gc)[..., None]
    g_last = jnp.exp(gc[..., -1])

    def step(state, inp):
        attn_c, q_c, k_c, u_c, w_c, gl = inp
        v_new = u_c - jnp.einsum("bhck,bhkv->bhcv", w_c, state)
        o = jnp.einsum("bhck,bhkv->bhcv", q_c, state) + jnp.einsum("bhij,bhjv->bhiv", attn_c, v_new)
        state = state * gl[..., None, None] + jnp.einsum("bhck,bhcv->bhkv", k_c, v_new)
        return state, o

    s0 = jnp.zeros(q.shape[1:3] + (q.shape[-1], v.shape[-1]), F32)
    _, o = lax.scan(step, s0, (attn, q_dec, k_dec, u, w, g_last))
    return _unchunks(o)

def _ssd_grouped(c, b, u, g):
    c, b, u, g = (_chunks(t.astype(F32)) for t in (c, b, u, g))
    gc = jnp.cumsum(g, axis=3)
    tril = jnp.tril(jnp.ones((CHUNK, CHUNK), dtype=bool))[:, :, None]
    seg = gc[:, :, :, :, None, :] - gc[:, :, :, None, :, :]
    decay = jnp.exp(jnp.where(tril, seg, -jnp.inf))
    scores = jnp.einsum("nbgis,nbgjs->nbgij", c, b)[..., None] * decay
    y_intra = jnp.einsum("nbgijr,nbgjrp->nbgirp", scores, u)

    def step(state, inp):
        c_c, b_c, u_c, gc_c = inp
        y = jnp.exp(gc_c)[..., None] * jnp.einsum("bgis,bgrsp->bgirp", c_c, state)
        g_last = gc_c[:, :, -1]
        u_dec = u_c * jnp.exp(g_last[:, :, None] - gc_c)[..., None]
        state = state * jnp.exp(g_last)[..., None, None] + jnp.einsum("bgjs,bgjrp->bgrsp", b_c, u_dec)
        return state, y

    s0 = jnp.zeros((c.shape[1], c.shape[2], u.shape[4], c.shape[4], u.shape[5]), F32)
    _, y_inter = lax.scan(step, s0, (c, b, u, gc))
    return _unchunks(y_intra + y_inter)

def _gla_chunked(q, k, v, g):
    q, k, v, g = (_chunks(t.astype(F32)) for t in (q, k, v, g))
    gc = jnp.cumsum(g, axis=3)
    tril = jnp.tril(jnp.ones((CHUNK, CHUNK), dtype=bool))[:, :, None]

    def step(state, inp):
        q_c, k_c, v_c, gc_c = inp
        seg = gc_c[:, :, :, None, :] - gc_c[:, :, None, :, :]
        decay = jnp.exp(jnp.where(tril, seg, -jnp.inf))
        attn = jnp.einsum("bhijk,bhjk->bhij", decay * q_c[:, :, :, None, :], k_c)
        g_last = gc_c[:, :, -1]
        o = (jnp.einsum("bhij,bhjv->bhiv", attn, v_c)
             + jnp.einsum("bhik,bhkv->bhiv", q_c * jnp.exp(gc_c), state))
        state = (state * jnp.exp(g_last)[..., None]
                 + jnp.einsum("bhjk,bhjv->bhkv", k_c * jnp.exp(g_last[:, :, None] - gc_c), v_c))
        return state, o

    s0 = jnp.zeros(q.shape[1:3] + (q.shape[-1], v.shape[-1]), F32)
    _, o = lax.scan(step, s0, (q, k, v, gc))
    return _unchunks(o)

def _gdn_mixer(x, w_in, conv_w, a_log, dt_bias, norm_w, w_out):
    bsz, seq, _ = x.shape
    qkv, z, ab = jnp.split(x @ w_in, [GDN_CONV_CH, GDN_CONV_CH + GDN_VAL_WIDTH], axis=-1)
    qkv = jax.nn.silu(_dwconv(qkv, conv_w))
    q, k, v = jnp.split(qkv, [GDN_KEY_WIDTH, 2 * GDN_KEY_WIDTH], axis=-1)
    rep = GDN_V_HEADS // GDN_QK_HEADS
    qk_shape = (bsz, seq, GDN_QK_HEADS, GDN_HEAD_DIM)
    q = jnp.repeat(_l2norm(q.reshape(qk_shape)), rep, axis=2) * GDN_HEAD_DIM ** -0.5
    k = jnp.repeat(_l2norm(k.reshape(qk_shape)), rep, axis=2)
    v = v.reshape(bsz, seq, GDN_V_HEADS, GDN_HEAD_DIM).astype(F32)
    ab = ab.astype(F32).reshape(bsz, seq, 2, 2, GDN_V_HEADS)
    g = -jnp.exp(a_log.astype(F32)) * jax.nn.softplus(ab[:, :, 0] + dt_bias.astype(F32))
    beta = jax.nn.sigmoid(ab[:, :, 1])
    o = (_gated_delta_rule(q, k, v, beta[:, :, 0], g[:, :, 0])
         + _rev(_gated_delta_rule(_rev(q), _rev(k), _rev(v), _rev(beta[:, :, 1]), _rev(g[:, :, 1]))))
    o = _rms(o) * norm_w.astype(F32) * jax.nn.silu(
        z.astype(F32).reshape(bsz, seq, GDN_V_HEADS, GDN_HEAD_DIM))
    return o.reshape(bsz, seq, GDN_VAL_WIDTH).astype(x.dtype) @ w_out

def _mamba2_mixer(x, w_in, conv_w, conv_b, a_log, dt_bias, d_skip, norm_w, w_out):
    bsz, seq, _ = x.shape
    z, xbc, dt = jnp.split(x @ w_in, [M2_D_INNER, M2_D_INNER + M2_CONV_CH], axis=-1)
    xbc = jax.nn.silu(_dwconv(xbc, conv_w) + conv_b).astype(F32)
    xs, b_in, c_out = jnp.split(xbc, [M2_D_INNER, M2_D_INNER + M2_GROUPS * M2_STATE], axis=-1)
    xs = xs.reshape(bsz, seq, M2_GROUPS, M2_HEADS_PER_GROUP, M2_HEAD_DIM)
    b_in = b_in.reshape(bsz, seq, M2_GROUPS, M2_STATE)
    c_out = c_out.reshape(bsz, seq, M2_GROUPS, M2_STATE)
    hshape = (2, M2_GROUPS, M2_HEADS_PER_GROUP)
    dt = jax.nn.softplus(dt.astype(F32).reshape(bsz, seq, *hshape) + dt_bias.astype(F32).reshape(hshape))
    g = -jnp.exp(a_log.astype(F32)).reshape(hshape) * dt
    u_f = xs * dt[:, :, 0, :, :, None]
    u_b = xs * dt[:, :, 1, :, :, None]
    y = (_ssd_grouped(c_out, b_in, u_f, g[:, :, 0])
         + _rev(_ssd_grouped(_rev(c_out), _rev(b_in), _rev(u_b), _rev(g[:, :, 1]))))
    y = y + d_skip.astype(F32).reshape(M2_GROUPS, M2_HEADS_PER_GROUP, 1) * xs
    y = y.reshape(bsz, seq, M2_GROUPS, -1) * jax.nn.silu(z.astype(F32).reshape(bsz, seq, M2_GROUPS, -1))
    y = _rms(y) * norm_w.astype(F32).reshape(M2_GROUPS, -1)
    return y.reshape(bsz, seq, M2_D_INNER).astype(x.dtype) @ w_out

def _hgrn2_mixer(x, w_in, lb, norm_w, w_out):
    bsz, seq, _ = x.shape
    hs = (bsz, seq, HG_HEADS, HG_EXPAND)
    q, f_fwd, f_bwd, i_in, gate = jnp.split((x @ w_in).astype(F32), 5, axis=-1)
    q = jax.nn.silu(q).reshape(hs)
    i_in = i_in.reshape(hs)
    lb = lb.reshape(HG_HEADS, HG_EXPAND)

    def forget(f):
        f = f.reshape(hs)
        log_f = jnp.logaddexp(jnp.log(lb), jnp.log1p(-lb) + jax.nn.log_sigmoid(f))
        return (1.0 - lb) * jax.nn.sigmoid(-f), log_f

    k_f, g_f = forget(f_fwd)
    k_b, g_b = forget(f_bwd)
    o = (_gla_chunked(q, k_f, i_in, g_f)
         + _rev(_gla_chunked(_rev(q), _rev(k_b), _rev(i_in), _rev(g_b))))
    o = _rms(o) * norm_w.astype(F32) * jax.nn.silu(gate.reshape(hs))
    return o.reshape(bsz, seq, HG_WIDTH).astype(x.dtype) @ w_out

def _gla_mixer(x, w_in, w_gk, b_gk, norm_w, w_out):
    bsz, seq, _ = x.shape
    splits = [GLA_KEY_WIDTH, 2 * GLA_KEY_WIDTH, 2 * GLA_KEY_WIDTH + GLA_VAL_WIDTH,
              2 * GLA_KEY_WIDTH + 2 * GLA_VAL_WIDTH]
    q, k, v, gate, r = jnp.split((x @ w_in).astype(F32), splits, axis=-1)
    ks = (bsz, seq, GLA_HEADS, GLA_K)
    vs = (bsz, seq, GLA_HEADS, GLA_V)
    q = q.reshape(ks) * GLA_K ** -0.5
    k = k.reshape(ks)
    v = v.reshape(vs)
    r = r.reshape(bsz, seq, 2, GLA_GATE_RANK)
    gk = jax.nn.log_sigmoid(jnp.einsum("blzr,zrk->blzk", r, w_gk.astype(F32))
                            + b_gk.astype(F32)) / GLA_GATE_TEMP
    g_f = gk[:, :, 0].reshape(ks)
    g_b = gk[:, :, 1].reshape(ks)
    o = (_gla_chunked(q, k, v, g_f)
         + _rev(_gla_chunked(_rev(q), _rev(k), _rev(v), _rev(g_b))))
    o = _rms(o) * norm_w.astype(F32) * jax.nn.silu(gate.reshape(vs))
    return o.reshape(bsz, seq, GLA_VAL_WIDTH).astype(x.dtype) @ w_out

def _hier_moe(x, w_group, b_group, w_router, b_router, w_gate, w_up, w_down):
    bsz, seq, d = x.shape
    xt = x.reshape(bsz * seq, d)
    g_logits = (xt @ w_group).astype(F32) + b_group.astype(F32)
    g_onehot = jax.nn.one_hot(jnp.argmax(g_logits, axis=-1), MOE_GROUPS, dtype=F32)
    g_prob = jnp.sum(jax.nn.softmax(g_logits, axis=-1) * g_onehot, axis=-1)
    e_logits = ((xt @ w_router).astype(F32) + b_router.astype(F32)).reshape(
        -1, MOE_GROUPS, MOE_EXPERTS_PER_GROUP)
    e_logits = jnp.einsum("tge,tg->te", e_logits, g_onehot)
    top_val, top_idx = lax.top_k(e_logits, MOE_TOPK)
    top_w = jax.nn.softmax(top_val, axis=-1) * g_prob[:, None]
    within = jnp.einsum("tk,tke->te", top_w,
                        jax.nn.one_hot(top_idx, MOE_EXPERTS_PER_GROUP, dtype=F32))
    comb = (g_onehot[:, :, None] * within[:, None, :]).astype(x.dtype)
    out = jnp.zeros_like(xt)
    for grp in range(MOE_GROUPS):
        h = (jax.nn.silu(jnp.einsum("td,edf->tef", xt, w_gate[grp]))
             * jnp.einsum("td,edf->tef", xt, w_up[grp]))
        out = out + jnp.einsum("tef,efd->td", h * comb[:, grp, :, None], w_down[grp])
    return out.reshape(bsz, seq, d)

def first_inputs(seed: int = 0) -> dict:
    key = jax.random.key(seed)
    ks = iter(jax.random.split(key, 48))

    def nrm(shape, scale):
        return jax.random.normal(next(ks), shape, F32) * scale

    def a_log(shape):
        return jnp.log(jax.random.uniform(next(ks), shape, F32, 1.0, 16.0))

    def dt_bias(shape):
        dt = jnp.exp(jax.random.uniform(next(ks), shape, F32, math.log(1e-3), math.log(1e-1)))
        return dt + jnp.log(-jnp.expm1(-dt))

    na, nb, nc, nd = (_n_uses(m) for m in range(N_MIXERS))
    D = D_MODEL
    sd = D ** -0.5
    beta = DEEPNORM_BETA
    return {
        "x": nrm((BATCH, SEQ, D), 1.0),
        "p": nrm((DEPTH, BATCH, SEQ, PLE_DIM), 1.0),
        "gdn_w_in": nrm((na, D, GDN_IN), sd),
        "gdn_conv_w": nrm((na, CONV_K, GDN_CONV_CH), CONV_K ** -0.5),
        "gdn_a_log": a_log((na, 2, GDN_V_HEADS)),
        "gdn_dt_bias": dt_bias((na, 2, GDN_V_HEADS)),
        "gdn_norm_w": 1.0 + nrm((na, GDN_HEAD_DIM), 0.02),
        "gdn_w_out": nrm((na, GDN_VAL_WIDTH, D), GDN_VAL_WIDTH ** -0.5 * beta),
        "m2_w_in": nrm((nb, D, M2_IN), sd),
        "m2_conv_w": nrm((nb, CONV_K, M2_CONV_CH), CONV_K ** -0.5),
        "m2_conv_b": nrm((nb, M2_CONV_CH), 0.02),
        "m2_a_log": a_log((nb, 2, M2_HEADS)),
        "m2_dt_bias": dt_bias((nb, 2, M2_HEADS)),
        "m2_d": 1.0 + nrm((nb, M2_HEADS), 0.1),
        "m2_norm_w": 1.0 + nrm((nb, M2_D_INNER), 0.02),
        "m2_w_out": nrm((nb, M2_D_INNER, D), M2_D_INNER ** -0.5 * beta),
        "hg_w_in": nrm((nc, D, HG_IN), sd),
        "hg_lb_logits": nrm((DEPTH, HG_WIDTH), 0.1),
        "hg_norm_w": 1.0 + nrm((nc, HG_EXPAND), 0.02),
        "hg_w_out": nrm((nc, HG_WIDTH, D), HG_WIDTH ** -0.5 * beta),
        "gla_w_in": nrm((nd, D, GLA_IN), sd),
        "gla_w_gk": nrm((nd, 2, GLA_GATE_RANK, GLA_KEY_WIDTH), GLA_GATE_RANK ** -0.5),
        "gla_b_gk": nrm((nd, 2, GLA_KEY_WIDTH), 0.1),
        "gla_norm_w": 1.0 + nrm((nd, GLA_V), 0.02),
        "gla_w_out": nrm((nd, GLA_VAL_WIDTH, D), GLA_VAL_WIDTH ** -0.5 * beta),
        "ln_g": 1.0 + nrm((DEPTH, 2, D), 0.02),
        "ln_b": nrm((DEPTH, 2, D), 0.02),
        "moe_w_group": nrm((DEPTH, D, MOE_GROUPS), sd),
        "moe_b_group": nrm((DEPTH, MOE_GROUPS), 0.01),
        "moe_w_router": nrm((DEPTH, D, MOE_EXPERTS), sd),
        "moe_b_router": nrm((DEPTH, MOE_EXPERTS), 0.01),
        "moe_w_gate": nrm((DEPTH, MOE_GROUPS, MOE_EXPERTS_PER_GROUP, D, MOE_HIDDEN), sd),
        "moe_w_up": nrm((DEPTH, MOE_GROUPS, MOE_EXPERTS_PER_GROUP, D, MOE_HIDDEN), sd),
        "moe_w_down": nrm((DEPTH, MOE_GROUPS, MOE_EXPERTS_PER_GROUP, MOE_HIDDEN, D),
                          MOE_HIDDEN ** -0.5 * beta),
        "pe_w_gate": nrm((DEPTH, D, D), sd),
        "pe_w_proj": nrm((DEPTH, PLE_DIM, D), PLE_DIM ** -0.5 * beta),
    }

def first_block(x, p, gdn_w_in, gdn_conv_w, gdn_a_log, gdn_dt_bias, gdn_norm_w, gdn_w_out,
              m2_w_in, m2_conv_w, m2_conv_b, m2_a_log, m2_dt_bias, m2_d, m2_norm_w, m2_w_out,
              hg_w_in, hg_lb_logits, hg_norm_w, hg_w_out,
              gla_w_in, gla_w_gk, gla_b_gk, gla_norm_w, gla_w_out,
              ln_g, ln_b, moe_w_group, moe_b_group, moe_w_router, moe_b_router,
              moe_w_gate, moe_w_up, moe_w_down, pe_w_gate, pe_w_proj):
    lb_all = jnp.cumsum(jax.nn.softmax(hg_lb_logits.astype(F32), axis=0), axis=0)
    lb_all = lb_all - lb_all[0]
    for i in range(DEPTH):
        m, j = i % N_MIXERS, i // N_MIXERS
        if m == 0:
            h = _gdn_mixer(x, gdn_w_in[j], gdn_conv_w[j], gdn_a_log[j], gdn_dt_bias[j],
                           gdn_norm_w[j], gdn_w_out[j])
        elif m == 1:
            h = _mamba2_mixer(x, m2_w_in[j], m2_conv_w[j], m2_conv_b[j], m2_a_log[j],
                              m2_dt_bias[j], m2_d[j], m2_norm_w[j], m2_w_out[j])
        elif m == 2:
            h = _hgrn2_mixer(x, hg_w_in[j], lb_all[i], hg_norm_w[j], hg_w_out[j])
        else:
            h = _gla_mixer(x, gla_w_in[j], gla_w_gk[j], gla_b_gk[j], gla_norm_w[j], gla_w_out[j])
        x = _layernorm(DEEPNORM_ALPHA * x + h, ln_g[i, 0], ln_b[i, 0])
        h = _hier_moe(x, moe_w_group[i], moe_b_group[i], moe_w_router[i], moe_b_router[i],
                      moe_w_gate[i], moe_w_up[i], moe_w_down[i])
        x = _layernorm(DEEPNORM_ALPHA * x + h, ln_g[i, 1], ln_b[i, 1])
        x = x + jax.nn.sigmoid(x @ pe_w_gate[i]) * (p[i].astype(x.dtype) @ pe_w_proj[i])
    return x


DEPTH_2 = 2

A_HEADS = 4
A_HEAD_DIM = 256
A_WIDTH = A_HEADS * A_HEAD_DIM
A_CHUNK = 64
CONV_WIDTH = 4
B_GROUPS = 4
B_GROUP_DIM = 256
B_WIDTH = B_GROUPS * B_GROUP_DIM
POOL_WINDOWS = (2, 4, 8, 16)
C_HEADS = 16
C_HEAD_DIM = 64
C_WIDTH = C_HEADS * C_HEAD_DIM
KV_RANK = 256
IDX_HEADS = 4
IDX_DIM = 64
TOP_K_MAX = 256
Q_BLOCK = 128
NUM_BUCKETS = 32
MAX_DISTANCE = 128
EPS = 1e-6

N_EVEN = (DEPTH_2 + 1) // 2
N_ODD = DEPTH_2 // 2
EVEN_SPLITS = (A_WIDTH, A_WIDTH, A_WIDTH, A_WIDTH, A_WIDTH, 2 * A_HEADS, B_WIDTH, B_WIDTH)
EVEN_IN = sum(EVEN_SPLITS)
ODD_SPLITS = (C_WIDTH, KV_RANK, IDX_HEADS * IDX_DIM, IDX_DIM, IDX_HEADS, C_WIDTH)
ODD_IN = sum(ODD_SPLITS)


def _split(p, sizes):
    pts = [int(v) for v in np.cumsum(sizes)[:-1]]
    return jnp.split(p, pts, axis=-1)

def rmsnorm(x, g):
    xf = x.astype(jnp.float32)
    y = xf * lax.rsqrt(jnp.mean(xf * xf, axis=-1, keepdims=True) + EPS)
    return (y * g.astype(jnp.float32)).astype(x.dtype)

def causal_conv(u, w):
    n_taps = w.shape[0]
    s_len = u.shape[1]
    up = jnp.pad(u, ((0, 0), (n_taps - 1, 0), (0, 0)))
    out = w[0] * up[:, 0:s_len]
    for j in range(1, n_taps):
        out = out + w[j] * up[:, j:j + s_len]
    return out

def mlstm_chunkwise(q, k, v, i_pre, f_pre):
    bsz, s_len, nh, dh = q.shape
    nc = s_len // A_CHUNK
    f32 = jnp.float32

    def to_chunks(a):
        return a.astype(f32).reshape(bsz, nc, A_CHUNK, nh, -1).transpose(1, 0, 3, 2, 4)

    def gate_chunks(a):
        return a.astype(f32).reshape(bsz, nc, A_CHUNK, nh).transpose(1, 0, 3, 2)

    qc = to_chunks(q)
    kc = to_chunks(k) * (dh ** -0.5)
    vc = to_chunks(v)
    ic = gate_chunks(i_pre)
    fc = gate_chunks(f_pre)
    causal = jnp.tril(jnp.ones((A_CHUNK, A_CHUNK), dtype=bool))

    def step(carry, inp):
        c_mat, n_vec, m_prev = carry
        qb, kb, vb, ib, fb = inp
        b = jnp.cumsum(jax.nn.log_sigmoid(fb), axis=-1)
        dmat = jnp.where(causal, b[..., :, None] - b[..., None, :] + ib[..., None, :], -jnp.inf)
        inter = b + m_prev[..., None]
        m_t = jnp.maximum(inter, jnp.max(dmat, axis=-1))
        w = jnp.exp(dmat - m_t[..., None]) * jnp.einsum('bhtd,bhsd->bhts', qb, kb)
        a_inter = jnp.exp(inter - m_t)
        num = a_inter[..., None] * jnp.einsum('bhvk,bhtk->bhtv', c_mat, qb) + jnp.einsum('bhts,bhsv->bhtv', w, vb)
        nq = a_inter * jnp.einsum('bhk,bhtk->bht', n_vec, qb) + jnp.sum(w, axis=-1)
        den = jnp.maximum(jnp.abs(nq), jnp.exp(-m_t))
        h = num / den[..., None]
        b_last = b[..., -1]
        g = b_last[..., None] - b + ib
        m_new = jnp.maximum(b_last + m_prev, jnp.max(g, axis=-1))
        decay = jnp.exp(b_last + m_prev - m_new)
        sw = jnp.exp(g - m_new[..., None])
        c_new = decay[..., None, None] * c_mat + jnp.einsum('bhs,bhsv,bhsk->bhvk', sw, vb, kb)
        n_new = decay[..., None] * n_vec + jnp.einsum('bhs,bhsk->bhk', sw, kb)
        return (c_new, n_new, m_new), h

    init = (jnp.zeros((bsz, nh, dh, dh), f32), jnp.zeros((bsz, nh, dh), f32), jnp.zeros((bsz, nh), f32))
    _, hs = lax.scan(step, init, (qc, kc, vc, ic, fc))
    return hs.transpose(1, 0, 3, 2, 4).reshape(bsz, s_len, nh, dh)

def multiscale_pool(u):
    bsz, s_len, _ = u.shape
    uf = u.astype(jnp.float32)
    cs = jnp.concatenate([jnp.zeros((bsz, 1, B_WIDTH), jnp.float32), jnp.cumsum(uf, axis=1)], axis=1)
    pos = jnp.arange(s_len)
    outs = []
    for gi, win in enumerate(POOL_WINDOWS):
        sl = slice(gi * B_GROUP_DIM, (gi + 1) * B_GROUP_DIM)
        cg = cs[:, :, sl]
        hi = cg[:, 1:]
        lo = jnp.concatenate([jnp.zeros((bsz, win - 1, B_GROUP_DIM), jnp.float32), cg[:, :s_len - win + 1]], axis=1)
        cnt = jnp.minimum(pos + 1, win).astype(jnp.float32)
        outs.append((hi - lo) / cnt[None, :, None] - uf[:, :, sl])
    return jnp.stack(outs, axis=2)

def t5_bucket(rel):
    rel = jnp.maximum(rel, 0)
    max_exact = NUM_BUCKETS // 2
    rel_f = jnp.maximum(rel, 1).astype(jnp.float32)
    large = max_exact + (jnp.log(rel_f / max_exact) / math.log(MAX_DISTANCE / max_exact)
                         * (NUM_BUCKETS - max_exact)).astype(jnp.int32)
    large = jnp.minimum(large, NUM_BUCKETS - 1)
    return jnp.where(rel < max_exact, rel, large)

def even_layer(x, g_norm, w_in, conv_w, b_if, g_head, w_pool, s_pool, w_out):
    bsz, s_len, _ = x.shape
    xn = rmsnorm(x, g_norm)
    p = xn @ w_in
    q, k, v, o, z_a, gates, u, z_b = _split(p, EVEN_SPLITS)
    qk = jax.nn.silu(causal_conv(jnp.concatenate([q, k], axis=-1), conv_w))
    q, k = qk[..., :A_WIDTH], qk[..., A_WIDTH:]
    gates = gates + b_if
    i_pre, f_pre = gates[..., :A_HEADS], gates[..., A_HEADS:]
    hd = (bsz, s_len, A_HEADS, A_HEAD_DIM)
    h = mlstm_chunkwise(q.reshape(hd), k.reshape(hd), v.reshape(hd), i_pre, f_pre)
    h = jax.nn.sigmoid(o.astype(jnp.float32)).reshape(hd) * h
    h = rmsnorm(h, g_head).reshape(bsz, s_len, A_WIDTH).astype(x.dtype)
    y_a = h * jax.nn.silu(z_a)
    pooled = multiscale_pool(u).astype(x.dtype)
    y_b = jnp.einsum('bsgc,gcd->bsgd', pooled, w_pool).reshape(bsz, s_len, B_WIDTH)
    y_b = y_b * s_pool * jax.nn.silu(z_b)
    return x + jnp.concatenate([y_a, y_b], axis=-1) @ w_out

def odd_layer(x, g_norm, w_in, g_kv, w_uk, w_uv, g_q, g_k, w_out, rel_bias):
    bsz, s_len, _ = x.shape
    xn = rmsnorm(x, g_norm)
    p = xn @ w_in
    q, ckv, qi, ki, wi, z = _split(p, ODD_SPLITS)
    hd = (bsz, s_len, C_HEADS, C_HEAD_DIM)
    q = rmsnorm(q.reshape(hd), g_q)
    ckv = rmsnorm(ckv, g_kv)
    k = rmsnorm((ckv @ w_uk).reshape(hd), g_k)
    v = (ckv @ w_uv).reshape(hd)
    qi = qi.reshape(bsz, s_len, IDX_HEADS, IDX_DIM).astype(jnp.float32) * (IDX_DIM ** -0.5)
    ki = ki.astype(jnp.float32)
    wi = wi.astype(jnp.float32) * (IDX_HEADS ** -0.5)
    top_k = min(TOP_K_MAX, s_len // 4)
    n_blocks = s_len // Q_BLOCK
    key_pos = jnp.arange(s_len)

    def block(start):
        qb = lax.dynamic_slice_in_dim(q, start, Q_BLOCK, axis=1)
        qib = lax.dynamic_slice_in_dim(qi, start, Q_BLOCK, axis=1)
        wib = lax.dynamic_slice_in_dim(wi, start, Q_BLOCK, axis=1)
        t = start + jnp.arange(Q_BLOCK)
        score = jnp.einsum('bqh,bqhs->bqs', wib, jax.nn.relu(jnp.einsum('bqhd,bsd->bqhs', qib, ki)))
        score = jnp.where((key_pos[None, :] <= t[:, None])[None], score, -jnp.inf)
        _, idx = lax.top_k(score, top_k)
        valid = idx <= t[None, :, None]
        ksel = jax.vmap(lambda kk, ii: kk[ii])(k, idx)
        vsel = jax.vmap(lambda vv, ii: vv[ii])(v, idx)
        logits = jnp.einsum('bqhd,bqkhd->bqhk', qb, ksel).astype(jnp.float32) * (C_HEAD_DIM ** -0.5)
        bias = rel_bias[t5_bucket(t[None, :, None] - idx)].astype(jnp.float32)
        logits = logits + bias.transpose(0, 1, 3, 2)
        logits = jnp.where(valid[:, :, None, :], logits, -jnp.inf)
        probs = jax.nn.softmax(logits, axis=-1).astype(v.dtype)
        return jnp.einsum('bqhk,bqkhd->bqhd', probs, vsel)

    out = lax.map(block, jnp.arange(n_blocks) * Q_BLOCK)
    out = out.transpose(1, 0, 2, 3, 4).reshape(bsz, s_len, C_WIDTH)
    return x + (out * jax.nn.silu(z)) @ w_out

def second_inputs(seed: int = 0) -> dict:
    key = jax.random.key(seed)
    ks = jax.random.split(key, 20)
    nrm = jax.random.normal
    f32 = jnp.float32
    b_i = 0.1 * nrm(ks[4], (N_EVEN, A_HEADS), f32)
    b_f = jnp.linspace(3.0, 6.0, A_HEADS, dtype=f32)[None] + 0.1 * nrm(ks[5], (N_EVEN, A_HEADS), f32)
    return {
        'x': nrm(ks[0], (BATCH, SEQ, D_MODEL), f32),
        'e_norm': 1.0 + 0.02 * nrm(ks[1], (N_EVEN, D_MODEL), f32),
        'e_w_in': nrm(ks[2], (N_EVEN, D_MODEL, EVEN_IN), f32) * D_MODEL ** -0.5,
        'e_conv': nrm(ks[3], (N_EVEN, CONV_WIDTH, 2 * A_WIDTH), f32) * CONV_WIDTH ** -0.5,
        'e_b_if': jnp.concatenate([b_i, b_f], axis=-1),
        'e_g_head': 1.0 + 0.02 * nrm(ks[6], (N_EVEN, A_HEADS, A_HEAD_DIM), f32),
        'e_w_pool': nrm(ks[7], (N_EVEN, B_GROUPS, B_GROUP_DIM, B_GROUP_DIM), f32) * B_GROUP_DIM ** -0.5,
        'e_s_pool': 1.0 + 0.02 * nrm(ks[8], (N_EVEN, B_WIDTH), f32),
        'e_w_out': nrm(ks[9], (N_EVEN, A_WIDTH + B_WIDTH, D_MODEL), f32) * (A_WIDTH + B_WIDTH) ** -0.5,
        'o_norm': 1.0 + 0.02 * nrm(ks[10], (N_ODD, D_MODEL), f32),
        'o_w_in': nrm(ks[11], (N_ODD, D_MODEL, ODD_IN), f32) * D_MODEL ** -0.5,
        'o_g_kv': 1.0 + 0.02 * nrm(ks[12], (N_ODD, KV_RANK), f32),
        'o_w_uk': nrm(ks[13], (N_ODD, KV_RANK, C_WIDTH), f32) * KV_RANK ** -0.5,
        'o_w_uv': nrm(ks[14], (N_ODD, KV_RANK, C_WIDTH), f32) * KV_RANK ** -0.5,
        'o_g_q': 1.0 + 0.02 * nrm(ks[15], (N_ODD, C_HEAD_DIM), f32),
        'o_g_k': 1.0 + 0.02 * nrm(ks[16], (N_ODD, C_HEAD_DIM), f32),
        'o_w_out': nrm(ks[17], (N_ODD, C_WIDTH, D_MODEL), f32) * C_WIDTH ** -0.5,
        'rel_bias': 0.5 * nrm(ks[18], (NUM_BUCKETS, C_HEADS), f32),
    }

def second_block(x, e_norm, e_w_in, e_conv, e_b_if, e_g_head, e_w_pool, e_s_pool, e_w_out,
              o_norm, o_w_in, o_g_kv, o_w_uk, o_w_uv, o_g_q, o_g_k, o_w_out, rel_bias):
    h = x
    for layer in range(DEPTH_2):
        j = layer // 2
        if layer % 2 == 0:
            h = even_layer(h, e_norm[j], e_w_in[j], e_conv[j], e_b_if[j], e_g_head[j],
                           e_w_pool[j], e_s_pool[j], e_w_out[j])
        else:
            h = odd_layer(h, o_norm[j], o_w_in[j], o_g_kv[j], o_w_uk[j], o_w_uv[j],
                          o_g_q[j], o_g_k[j], o_w_out[j], rel_bias)
    return h


def setup_inputs(seed=0):
    out = dict(first_inputs(seed))
    for name, value in second_inputs(seed + 1).items():
        if name != "x":
            out[name + "_2"] = value
    return out


def reference(
    x, p, gdn_w_in, gdn_conv_w, gdn_a_log, gdn_dt_bias, gdn_norm_w, gdn_w_out, m2_w_in,
    m2_conv_w, m2_conv_b, m2_a_log, m2_dt_bias, m2_d, m2_norm_w, m2_w_out, hg_w_in,
    hg_lb_logits, hg_norm_w, hg_w_out, gla_w_in, gla_w_gk, gla_b_gk, gla_norm_w, gla_w_out,
    ln_g, ln_b, moe_w_group, moe_b_group, moe_w_router, moe_b_router, moe_w_gate, moe_w_up,
    moe_w_down, pe_w_gate, pe_w_proj, e_norm_2, e_w_in_2, e_conv_2, e_b_if_2, e_g_head_2,
    e_w_pool_2, e_s_pool_2, e_w_out_2, o_norm_2, o_w_in_2, o_g_kv_2, o_w_uk_2, o_w_uv_2,
    o_g_q_2, o_g_k_2, o_w_out_2, rel_bias_2,
):
    x = first_block(
        x, p, gdn_w_in, gdn_conv_w, gdn_a_log, gdn_dt_bias, gdn_norm_w, gdn_w_out, m2_w_in,
        m2_conv_w, m2_conv_b, m2_a_log, m2_dt_bias, m2_d, m2_norm_w, m2_w_out, hg_w_in,
        hg_lb_logits, hg_norm_w, hg_w_out, gla_w_in, gla_w_gk, gla_b_gk, gla_norm_w, gla_w_out,
        ln_g, ln_b, moe_w_group, moe_b_group, moe_w_router, moe_b_router, moe_w_gate, moe_w_up,
        moe_w_down, pe_w_gate, pe_w_proj,
    )
    return second_block(
        x, e_norm_2, e_w_in_2, e_conv_2, e_b_if_2, e_g_head_2, e_w_pool_2, e_s_pool_2,
        e_w_out_2, o_norm_2, o_w_in_2, o_g_kv_2, o_w_uk_2, o_w_uv_2, o_g_q_2, o_g_k_2,
        o_w_out_2, rel_bias_2,
    )


_drawn_inputs = setup_inputs


def setup_inputs(seed=0):
    import zlib

    import numpy as np

    out = dict(_drawn_inputs(seed))
    spreads = {}
    factors = {'gdn_norm_w': 2.805,
     'moe_b_group': 8.0,
     'moe_b_router': 4.663,
     'e_norm_2': 2.729,
     'e_g_head_2': 4.725,
     'e_s_pool_2': 5.519,
     'o_norm_2': 3.845,
     'o_g_kv_2': 8.0,
     'o_g_q_2': 8.0,
     'o_g_k_2': 8.0}
    for name, (base, spread) in spreads.items():
        noise = np.random.default_rng([zlib.crc32(name.encode()), seed]).standard_normal(out[name].shape)
        drawn = base * np.exp(spread * noise) if base else spread * noise
        out[name] = jnp.asarray(drawn.astype(out[name].dtype))
    for name, factor in factors.items():
        out[name] = (out[name] * factor).astype(out[name].dtype)
    return out
```

```python
from contextlib import contextmanager

import numpy as np

import concourse.bass as bass
from concourse import mybir

F32 = mybir.dt.float32
ALU = mybir.AluOpType
ACT = mybir.ActivationFunctionType
AX = mybir.AxisListType.X

P = 128
T = 256
NT = T // P
D = 1024
KT = D // P
UC = 256
CHUNK = 64
QKH, VH, HD = 8, 16, 128
REP = VH // QKH
TAPS = 5
EXPERTS, TOPK, HID, GROUPS = 32, 2, 256, 4
EPG = EXPERTS // GROUPS
AH, AD = 4, 256
POOL_WINDOWS = (2, 4, 8, 16)
CH, CD = 16, 64
IH, IDIM = 4, 64
SEL = 64
BUCKETS, MAXDIST = 32, 128
ALPHA = 2.0 ** 0.25
BIG = 1e30
LEVELS = (1, 2, 4, 8, 16, 32)
NSLOT = 6
TAKEN = -2.0 ** 126
ARENA = 27500

U_GDN = 0
U_GOUT = U_GDN + 3 * QKH
U_MOE = U_GOUT + 8
U_PE = U_MOE + 3 * EXPERTS
U_POOL = U_PE + 5
U_EIN = U_POOL + 1
U_EOUT = U_EIN + 28
U_OIN = U_EOUT + 8
U_UK = U_OIN + 10
U_OOUT = U_UK + 2
UNITS = U_OOUT + 4
F_ENORM, F_ONORM, F_HEAD, F_POOL, F_KV, F_Q, F_K = 0, 8, 16, 24, 32, 34, 35
FEATS = 36


class Point:

    def __init__(self, line, value, loop):
        self.line, self.value, self.loop = line, value, loop

    def before(self):
        return Point(self.line, self.value - self.loop.per[self.line.name], self.loop)

    def at(self):
        if self.loop is None:
            return self.value
        per = self.loop.per.get(self.line.name, 0)
        if self.loop.open:
            return self.loop.i * per + self.value if per else self.value
        return self.value + (self.loop.n - 1) * per


class Loop:
    def __init__(self, n, i, per):
        self.n, self.i, self.per, self.open = n, i, per, True


class Line:

    def __init__(self, prog, name, step=1):
        self.prog, self.name, self.step, self.count = prog, name, step, 0
        self.sem = prog.nc.alloc_semaphore(name)
        prog.lines.append(self)

    def mark(self, ins):
        ins.then_inc(self.sem, self.step)
        self.count += self.step
        return Point(self, self.count, self.prog.loop)

    def now(self):
        return Point(self, self.count, self.prog.loop)


class Prog:

    def __init__(self, nc, per):
        self.nc, self.per, self.loop, self.lines, self.found, self.seen = nc, per, None, [], {}, {}
        self.pe, self.act, self.dve, self.pool = (Line(self, n) for n in ("pe", "act", "dve", "pool"))

    def need(self, engine, *points):
        for p in points:
            if p is None:
                continue
            key = (engine.engine, p.line.name, id(p.loop))
            if self.seen.get(key, -1) >= p.value:
                continue
            self.seen[key] = p.value
            engine.wait_ge(p.line.sem, p.at())

    def barrier(self):
        for e in (self.nc.tensor, self.nc.scalar, self.nc.vector, self.nc.gpsimd):
            self.need(e, *(l.now() for l in (self.pe, self.act, self.dve, self.pool)))

    @contextmanager
    def fori(self, name, n):
        starts = self.starts = {l.name: l.count for l in self.lines}
        per = self.per.get(name, {})
        with self.nc.Fori(0, n, 1) as i:
            self.loop = Loop(n, i, per)
            self.seen = {}
            yield i
            self.loop.open = False
        self.found[name] = {l.name: l.count - starts[l.name] for l in self.lines}
        for l in self.lines:
            l.count = starts[l.name] + n * (l.count - starts[l.name])
        self.loop = None
        self.seen = {}


def constants():
    r = np.arange(P)
    i, j = r[:, None], r[None, :]
    same = (i // CHUNK) == (j // CHUNK)
    eye = (i == j).astype(np.float32)
    upto = [(same & (i <= j)), (same & (i >= j))]
    behind = [(same & (i > j)), (same & (i < j))]
    keep = [(same & (i >= j)), (same & (i <= j))]

    def level(b):
        return (i // (2 * b) == j // (2 * b)) & ((i // b) % 2 == 1) & ((j // b) % 2 == 0)

    def four(fwd, bwd):
        return np.stack([fwd, fwd, bwd, bwd], 1).astype(np.float32)

    t = np.arange(T)
    late = np.stack([t[None, :] > P * n + r[:, None] for n in range(NT)], 1)
    window = []
    for w in POOL_WINDOWS:
        back = t[None, :] - t[:, None]
        window.append(((back >= 0) & (back < w)) / np.minimum(t + 1, w)[None, :] - (back == 0))
    window = np.stack(window).reshape(len(POOL_WINDOWS), NT, P, T).transpose(2, 0, 1, 3)
    dist = np.maximum(np.arange(2 * T) - (T - 1), 0)
    half = BUCKETS // 2
    far = half + (np.log(np.maximum(dist, 1).astype(np.float32) / np.float32(half))
                  / np.float32(np.log(MAXDIST / half)) * np.float32(BUCKETS - half)).astype(np.int32)
    bucket = np.where(dist < half, dist, np.minimum(far, BUCKETS - 1))
    onehot = np.zeros((P, 2 * T))
    onehot[bucket, np.arange(2 * T)] = 1
    common = {
        "ident": eye, "ones": np.ones((P, P)), "upto_all": i <= j,
        "columns": np.tile(np.array([1e-6, 1e-5, 0.5 * -np.log(HD), 1.0, -1.0, 0, 0, 0]), (P, 1)),
        "rank4": np.tile(np.arange(4, 0, -1), (P, NT)), "rank8": np.tile(np.arange(8, 0, -1), (P, NT)),
    }
    delta = {
        "upto": np.stack(upto, 1), "behind": np.stack(behind, 1),
        "bars": four(~keep[0], ~keep[1]) * BIG,
        "levels_t": np.stack([four(level(b).T, level(b)) for b in LEVELS], 1),
        "level1": four(level(1), level(1).T),
        "ident4": four(eye, eye),
    }
    late = {"late": late * BIG, "onehot": onehot}
    flat = lambda g: {k: np.ascontiguousarray(v.reshape(P, -1).astype(np.float32)) for k, v in g.items()}
    return {"common": flat(common), "delta": flat(delta), "late": flat(late), "pool": flat({"window": window})}


def const_map(group):
    at, out = 0, {}
    for k, v in constants()[group].items():
        out[k] = (at, v.shape[1])
        at += v.shape[1]
    return out, at


class Build:
    def __init__(self, nc, ins, out, per, upto=99, dbg=None):
        self.nc, self.ins, self.out, self.dbg = nc, ins, out, dbg
        self.p = p = Prog(nc, per)
        self.pe, self.act, self.dve, self.pool = p.pe, p.act, p.dve, p.pool
        self.need = p.need
        nc.tensor.sem_inc(self.pe.sem, 1024)
        self.pe.count = 1024
        nc.gpsimd.sem_inc(self.pool.sem, 64)
        self.pool.count = 64
        self.ps = nc.alloc_psum_tensor("ps", [P, 8, 512], F32)
        self.slots = nc.alloc_sbuf_tensor("slots", [P, NSLOT, KT, UC], F32)
        self.arrived = [Line(p, f"slot{s}_arrived", 16) for s in range(NSLOT)]
        self.small = Line(p, "small_arrived", 16)
        self.scratch_done = Line(p, "bias_rows_stored", 16)
        self.stored = Line(p, "output_stored", 16)
        self.bias_rows = nc.dram_tensor("bias_rows", (CH, 2 * T), F32, kind="Internal").ap()
        self.x = nc.alloc_sbuf_tensor("x", [P, NT, D], F32)
        self.xt = nc.alloc_sbuf_tensor("xt", [P, KT, T], F32)
        self.yt = nc.alloc_sbuf_tensor("yt", [P, 16, T], F32)
        cm, n = const_map("common")
        self.cst = nc.alloc_sbuf_tensor("cst", [P, n], F32)
        self.c = {k: self.cst[:, a:a + m] for k, (a, m) in cm.items()}
        self.arena = nc.alloc_sbuf_tensor("arena", [P, ARENA], F32)
        self.top = 0
        self.stages(upto)

    def alloc(self, name, shape):
        n = int(np.prod(shape[1:]))
        v = self.arena[:shape[0], self.top:self.top + n]
        self.top += n
        assert self.top <= ARENA, (name, self.top)
        if len(shape) > 2:
            names = "abcd"[:len(shape) - 1]
            v = v.rearrange(f"p ({' '.join(names)}) -> p {' '.join(names)}",
                            **{k: m for k, m in zip(names, shape[1:])})
        return v

    def fresh(self):
        self.p.barrier()
        self.top = 0

    def consts(self, group, at=None):
        cm, n = const_map(group)
        v = self.alloc(group, [P, n]) if at is None else at[:, 0:n]
        self.load(v, self.ins["c_" + group])
        self.c.update({k: v[:, a:a + m] for k, (a, m) in cm.items()})

    def load(self, dst, src, queue=None):
        return self.small.mark((queue or self.nc.scalar).dma_start(dst, src))

    def bank(self, b, n=512, at=0):
        return self.ps[:, b, at:at + n]

    def refill(self, slot, unit, point):
        self.need(self.nc.sync, point)
        return self.arrived[slot].mark(self.nc.sync.dma_start(self.slots[:, slot], self.ins["wu"][unit]))

    def stages(self, upto):
        I = self.ins
        self.load(self.cst[:, :], I["c_common"])
        self.load(self.xt[:, :, :], I["xt"])
        for s in range(3):
            self.refill(s, U_GDN + s, None)
        self.refill(3, U_GOUT + 3, None)
        self.load(self.x[:, :, :], I["x"].rearrange("a (n p) d -> p (a n) d", p=P))
        self.gdn()
        if upto <= 1:
            return self.finish_debug(self.yt)
        self.moe()
        if upto <= 2:
            return self.finish_debug(self.x)
        self.embed()
        if upto <= 3:
            return self.finish_debug(self.x)
        self.even()
        if upto <= 4:
            return self.finish_debug(self.x)
        self.odd()
        if self.dbg is not None:
            self.finish_debug(self.x)

    def gdn(self):
        nc, I, p, need, c = self.nc, self.ins, self.p, self.need, self.c
        pe, act, dve, pool = self.pe, self.act, self.dve, self.pool
        A, V, G, M = nc.scalar, nc.vector, nc.gpsimd, nc.tensor
        al = self.alloc
        self.consts("delta")
        wab = al("wab", [P, KT, 64])
        alog = al("alog", [P, 32])
        dtb = al("dtb", [P, 32])
        cw = al("cw", [P, QKH, 4 * TAPS])
        nw = al("gdn_nw", [P, 1])
        self.load(wab[:, :, :], I["wab"])
        self.load(alog[:, :], I["gdn_a_log"].rearrange("a d h -> a (d h)").to_broadcast([P, 32]))
        self.load(dtb[:, :], I["gdn_dt_bias"].rearrange("a d h -> a (d h)").to_broadcast([P, 32]))
        self.load(cw[:, :, :], I["cw"])
        ready = self.load(nw[:, :], I["gdn_norm_w"].rearrange("a (p b) -> (a p) b", b=1))
        need(M, ready)
        for t in range(NT):
            for k in range(KT):
                q = M.matmul(self.bank(0, 64, 64 * t), self.xt[:, k, t * P:(t + 1) * P], wab[:, k, :],
                             start=(k == 0), stop=(k == KT - 1), skip_group_check=True)
        q = pe.mark(q)
        ab = self.bank(0, 128).rearrange("p (t z n) -> p t z n", t=NT, z=2)
        GC, BE, BG, GS = range(4)
        gate = al("gate", [P, 4, NT, 32])
        g = al("g", [P, NT, 32])
        s1 = al("gate_s1", [P, NT, 32])
        s2 = al("gate_s2", [P, NT, 32])
        need(V, q, ready)
        a = dve.mark(V.tensor_tensor(s1[:, :, :], ab[:, :, 0, :],
                                     dtb[:, :].unsqueeze(1).to_broadcast([P, NT, 32]), ALU.add))
        need(V, a)
        b = dve.mark(V.scalar_tensor_tensor(s2[:, :, :], s1[:, :, :], -1.0, s1[:, :, :], ALU.mult, ALU.max))
        need(A, b)
        b = act.mark(A.activation(s2[:, :, :], s2[:, :, :], ACT.Exp, scale=-1.0))
        need(A, b)
        b = act.mark(A.activation(s2[:, :, :], s2[:, :, :], ACT.Ln, bias=1.0))
        need(A, ready)
        e = act.mark(A.activation(alog[:, :], alog[:, :], ACT.Exp))
        need(V, b, e)
        b = dve.mark(V.scalar_tensor_tensor(s1[:, :, :], s1[:, :, :], 0.0, s2[:, :, :], ALU.max, ALU.add))
        need(V, b)
        b = dve.mark(V.scalar_tensor_tensor(g[:, :, :], s1[:, :, :], -1.0,
                                            alog[:, :].unsqueeze(1).to_broadcast([P, NT, 32]),
                                            ALU.mult, ALU.mult))
        need(A, q)
        e = act.mark(A.activation(gate[:, BE], ab[:, :, 1, :], ACT.Exp, scale=-1.0))
        need(V, e)
        e = dve.mark(V.tensor_scalar(gate[:, BE], gate[:, BE], 1.0, None, ALU.add))
        need(V, e)
        be = dve.mark(V.reciprocal(gate[:, BE], gate[:, BE]))
        need(M, b, be)
        up = c["upto"].rearrange("p (d i) -> p d i", d=2)
        bh = c["behind"].rearrange("p (d i) -> p d i", d=2)
        for t in range(NT):
            for d in range(2):
                o = 32 * t + 16 * d
                M.matmul(self.bank(1, 16, o), up[:, d], g[:, t, 16 * d:16 * d + 16],
                         start=True, stop=True, skip_group_check=True)
                q = M.matmul(self.bank(2, 16, o), bh[:, d], g[:, t, 16 * d:16 * d + 16],
                             start=True, stop=True, skip_group_check=True)
        q = pe.mark(q)
        need(A, q)
        gcs = self.bank(1, 64).rearrange("p (t n) -> p t n", t=NT)
        act.mark(A.activation(gate[:, GC], gcs, ACT.Copy))
        act.mark(A.activation(gate[:, GS], self.bank(2, 64).rearrange("p (t n) -> p t n", t=NT), ACT.Exp))
        e = act.mark(A.activation(s2[:, :, :], gcs, ACT.Exp))
        need(V, e)
        dve.mark(V.tensor_tensor(gate[:, BG], gate[:, BE], s2[:, :, :], ALU.mult))

        NI = 4
        raw = al("raw", [P, 4, T + TAPS - 1])
        cv = al("cv", [P, 4, T])
        zs = al("zs", [P, REP, T])
        sq = al("sq", [P, 2, T])
        rn = al("rn", [P, 2, T])
        cwh = al("cwh", [P, 4 * TAPS])
        sc = al("sc", [P, 4, NT, NI])
        gb = al("gb", [P, NT, NI, P])
        er = al("er", [P, NT, NI, P])
        dm = al("dm", [P, NT, NI, P])
        am = al("am", [P, NT, NI, P])
        an = al("an", [P, NT, NI, P])
        att = al("att", [P, NT, NI, P])
        mt = al("mt", [P, NT, NI, P])
        X = al("X", [P, NT, NI, P])
        XT = al("XT", [P, NT, NI, P])
        ktm = al("ktm", [P, NT, P])
        vtm = al("vtm", [P, NT, REP, P])
        S = al("S", [P, NI, P])
        vn = al("vn", [P, 2, P])
        Y, vb, kbe, kdec = gb, er, dm, gb
        kbe = am
        qd = al("qd", [P, NT, NI, P])
        kdec = al("kdec", [P, NT, NI, P])
        vb = dm
        nwt = an
        z = dve.mark(V.memset(raw[:, :, :], 0.0))
        bars = c["bars"].rearrange("p (n j) -> p n j", n=NI)
        lvt = c["levels_t"].rearrange("p (l n j) -> p l n j", l=len(LEVELS), n=NI)
        l1 = c["level1"].rearrange("p (n j) -> p n j", n=NI)
        id4 = c["ident4"].rearrange("p (n j) -> p n j", n=NI)
        ident = c["ident"]
        four = lambda b: self.bank(b).rearrange("p (n j) -> p n j", n=NI)

        with p.fori("delta", QKH) as i:
            p.barrier()
            proj = []
            for s in range(3):
                need(M, self.arrived[s].now())
                for n in range(2):
                    for k in range(KT):
                        q = M.matmul(self.bank(s, T, T * n), self.slots[:, s, k, n * P:(n + 1) * P],
                                     self.xt[:, k, :], start=(k == 0), stop=(k == KT - 1),
                                     skip_group_check=True)
                proj.append(pe.mark(q))
            for s in range(3):
                self.refill(s, i * 3 + (U_GDN + 3 + s), proj[s])
            t1 = dve.mark(V.tensor_copy(cwh[:, :], cw[:, i, :]))
            for h in range(4):
                t2 = dve.mark(V.tensor_copy(
                    sc[:, h].rearrange("p t (d v) -> p (t d) v", d=2),
                    gate[:, h].rearrange("p t (d n) -> p (t d) n", d=2)[:, :, bass.ds(i * 2, 2)]))
            need(G, t2)
            gview = g[:, :, :].rearrange("p t (d n) -> p (t d) n", d=2)
            t3 = dve.mark(V.tensor_copy(
                gb[:, :, :, :].rearrange("p t (d v) j -> p (t d) v j", d=2),
                gview[:, :, bass.ds(i * 2, 2)].unsqueeze(3).to_broadcast([P, NT * 2, REP, P])))
            need(M, t3)
            for t in range(NT):
                for n in range(NI):
                    q = M.matmul(self.bank(6 + t, P, n * P), gb[:, t, n, :], up[:, n // 2],
                                 start=True, stop=True, skip_group_check=True)
            rows = pe.mark(q)
            for s, b in ((0, 0), (2, 1)):
                need(A, proj[b])
                cp = act.mark(A.activation(raw[:, s:s + 2, 2:2 + T],
                                           self.bank(b).rearrange("p (n t) -> p n t", n=2), ACT.Copy))
            need(V, cp, t1)
            last = [None] * 4
            for tap in range(TAPS):
                for s in range(4):
                    src, w = raw[:, s, tap:tap + T], cwh[:, s * TAPS + tap:s * TAPS + tap + 1]
                    if tap == 0:
                        last[s] = dve.mark(V.tensor_scalar(cv[:, s], src, w, None, ALU.mult))
                    else:
                        need(V, last[s])
                        last[s] = dve.mark(V.scalar_tensor_tensor(cv[:, s], src, w, cv[:, s],
                                                                  ALU.mult, ALU.add))
            need(A, last[3], proj[2])
            act.mark(A.activation(zs[:, :, :], self.bank(2).rearrange("p (n t) -> p n t", n=2), ACT.Silu))
            cs = act.mark(A.activation(cv[:, :, :], cv[:, :, :], ACT.Silu))
            need(V, cs)
            t1 = dve.mark(V.tensor_tensor(sq[:, :, :], cv[:, 0:2], cv[:, 0:2], ALU.mult))
            need(M, t1)
            q = pe.mark(M.matmul(self.bank(5), c["ones"], sq[:, :, :], start=True, stop=True))
            need(A, q)
            t1 = act.mark(A.activation(rn[:, :, :], self.bank(5).rearrange("p (n t) -> p n t", n=2),
                                       ACT.Ln, bias=c["columns"][:, 0:1]))
            need(A, t1)
            act.mark(A.activation(rn[:, 0], rn[:, 0], ACT.Exp, scale=-0.5, bias=c["columns"][:, 2:3]))
            t1 = act.mark(A.activation(rn[:, 1], rn[:, 1], ACT.Exp, scale=-0.5))
            need(V, t1)
            qk = dve.mark(V.tensor_tensor(cv[:, 0:2], cv[:, 0:2], rn[:, :, :], ALU.mult))
            need(M, qk, cp)
            for t in range(NT):
                M.transpose(self.bank(3, P, t * P), cv[:, 1, t * P:(t + 1) * P], ident)
                for v in range(REP):
                    M.transpose(self.bank(4, P, (t * 2 + v) * P), cv[:, 2 + v, t * P:(t + 1) * P], ident)
                ts = slice(t * P, (t + 1) * P)
                M.matmul(self.bank(0, P, t * P), cv[:, 1, ts], cv[:, 1, ts], start=True, stop=True,
                         skip_group_check=True)
                q = M.matmul(self.bank(0, P, (2 + t) * P), cv[:, 0, ts], cv[:, 1, ts], start=True,
                             stop=True, skip_group_check=True)
            kq = pe.mark(q)
            need(A, kq)
            act.mark(A.activation(ktm[:, :, :], self.bank(3, 2 * P).rearrange("p (t j) -> p t j", t=2), ACT.Copy))
            tm = act.mark(A.activation(vtm[:, :, :, :].rearrange("p t v j -> p (t v) j"), four(4), ACT.Copy))
            need(A, rows)
            for t in range(NT):
                ex = act.mark(A.activation(er[:, t], four(6 + t), ACT.Exp))
            need(V, rows, ex)
            for t in range(NT):
                t1 = dve.mark(V.tensor_tensor(dm[:, t], four(6 + t), bars, ALU.add))
            need(A, t1)
            for t in range(NT):
                for n in range(NI):
                    t1 = act.mark(A.activation(dm[:, t, n], dm[:, t, n], ACT.Exp, scale=-1.0,
                                               bias=sc[:, GC, t, n:n + 1]))
            need(V, t1, kq, ex)
            for t in range(NT):
                for n in range(NI):
                    dve.mark(V.scalar_tensor_tensor(am[:, t, n], self.bank(0, P, t * P),
                                                    sc[:, BE, t, n:n + 1], dm[:, t, n], ALU.mult, ALU.mult))
                a2 = dve.mark(V.tensor_tensor(an[:, t], self.bank(0, P, (2 + t) * P).unsqueeze(1)
                                              .to_broadcast([P, NI, P]), dm[:, t], ALU.mult))
            for t in range(NT):
                a3 = dve.mark(V.tensor_tensor(qd[:, t], er[:, t], cv[:, 0, t * P:(t + 1) * P].unsqueeze(1)
                                              .to_broadcast([P, NI, P]), ALU.mult))
            need(M, a2, tm)
            for t in range(NT):
                for n in range(NI):
                    M.transpose(self.bank(1 + t, P, n * P), am[:, t, n], ident)
                    q = M.transpose(self.bank(3 + t, P, n * P), an[:, t, n], ident)
            tr = pe.mark(q)
            need(A, tr)
            for t in range(NT):
                at = act.mark(A.activation(att[:, t], four(3 + t), ACT.Copy))
            need(G, tm, t2, a2, a3)
            for t in range(NT):
                dv = lambda x: x[:, t].rearrange("p (d v) j -> p d v j", d=2)
                bc = lambda q: sc[:, q, t].rearrange("p (d v) -> p d v", d=2).unsqueeze(3).to_broadcast([P, 2, REP, P])
                kv = ktm[:, t].unsqueeze(1).to_broadcast([P, NI, P])
                b4 = lambda q: sc[:, q, t].unsqueeze(2).to_broadcast([P, NI, P])
                for d in range(2):
                    pool.mark(G.tensor_tensor(vb[:, t, 2 * d:2 * d + 2], vtm[:, t],
                                              sc[:, BE, t, 2 * d:2 * d + 2].unsqueeze(2)
                                              .to_broadcast([P, REP, P]), ALU.mult))
                pool.mark(G.tensor_tensor(kdec[:, t], kv, b4(GS), ALU.mult))
            need(V, tr)
            for t in range(NT):
                dve.mark(V.tensor_tensor(X[:, t], am[:, t], l1, ALU.mult))
                t1 = dve.mark(V.tensor_tensor(XT[:, t], four(1 + t), lvt[:, 0], ALU.mult))
            need(V, t1)
            for t in range(NT):
                dve.mark(V.tensor_tensor(X[:, t], id4, X[:, t], ALU.subtract))
                x0 = dve.mark(V.tensor_tensor(XT[:, t], id4, XT[:, t], ALU.subtract))
            need(G, x0, tm)
            for t in range(NT):
                kb = pool.mark(G.tensor_tensor(kbe[:, t], ktm[:, t].unsqueeze(1).to_broadcast([P, NI, P]),
                                               sc[:, BG, t].unsqueeze(2).to_broadcast([P, NI, P]), ALU.mult))
            xs, zy = [x0] * NT, [None] * NT
            for l in range(1, len(LEVELS)):
                lastl = l == len(LEVELS) - 1
                ym = []
                for t in range(NT):
                    need(V, zy[t])
                    m = dve.mark(V.tensor_tensor(mt[:, t], four(1 + t), lvt[:, l], ALU.mult))
                    need(M, m, xs[t])
                    for n in range(NI):
                        q = M.matmul(self.bank(5 + t, P, n * P), mt[:, t, n], X[:, t, n], start=True,
                                     stop=True, skip_group_check=True)
                    ym.append(pe.mark(q))
                yc = []
                for t in range(NT):
                    need(A, ym[t])
                    yc.append(act.mark(A.activation(Y[:, t], four(5 + t), ACT.Copy)))
                for t in range(NT):
                    zb, zt = (7, 0) if t == 0 else (3, 4)
                    need(M, yc[t], at)
                    for n in range(NI):
                        if not lastl:
                            M.matmul(self.bank(zb, P, n * P), XT[:, t, n], Y[:, t, n], start=True,
                                     stop=True, skip_group_check=True)
                        q = M.matmul(self.bank(zt, P, n * P), Y[:, t, n], XT[:, t, n], start=True,
                                     stop=True, skip_group_check=True)
                    zy[t] = pe.mark(q)
                    need(V, zy[t])
                    if not lastl:
                        dve.mark(V.tensor_tensor(X[:, t], X[:, t], four(zb), ALU.subtract))
                    xs[t] = dve.mark(V.tensor_tensor(XT[:, t], XT[:, t], four(zt), ALU.subtract))
            need(M, kb, *xs)
            for t in range(NT):
                for n in range(NI):
                    q = M.matmul(self.bank(1 + t, P, n * P), kbe[:, t, n], XT[:, t, n], start=True,
                                 stop=True, skip_group_check=True)
            w = pe.mark(q)
            need(A, w)
            for t in range(NT):
                wt = act.mark(A.activation(nwt[:, t], four(1 + t), ACT.Copy, scale=-1.0))
            st = dve.mark(V.memset(S[:, :, :], 0.0))
            need(M, wt, st, self.pool.now(), *xs)
            NC = T // CHUNK
            vc, sr = None, None
            for step in range(NC):
                where = []
                for n in range(NI):
                    ch = step if n < 2 else NC - 1 - step
                    where.append((ch // 2, CHUNK * (ch % 2), ch))
                for n in range(NI):
                    t, r, ch = where[n]
                    rs = slice(r, r + CHUNK)
                    o = self.ps[rs, 5, (n % 2) * P:(n % 2 + 1) * P]
                    M.matmul(o, nwt[:, t, n, rs], S[:, n, :], start=True, stop=False, skip_group_check=True)
                    q = M.matmul(o, XT[rs, t, n, rs], vb[rs, t, n, :], start=False, stop=True,
                                 skip_group_check=True)
                vp = pe.mark(q)
                for n in range(NI):
                    t, r, ch = where[n]
                    rs = slice(r, r + CHUNK)
                    o = self.bank(7 if n < 2 else 4, CHUNK, (n % 2) * T + ch * CHUNK)
                    q = M.matmul(o, S[:, n, :], qd[:, t, n, rs], start=(step == 0 and n % 2 == 0),
                                 stop=False, skip_group_check=True)
                sr = pe.mark(q)
                need(A, vp)
                vc = act.mark(A.activation(vn[:, :, :], self.bank(5, 2 * P).rearrange("p (n j) -> p n j", n=2),
                                           ACT.Copy))
                need(M, vc)
                for n in range(NI):
                    t, r, ch = where[n]
                    rs = slice(r, r + CHUNK)
                    if step < NC - 1:
                        q = M.matmul(self.bank(6 if n < 2 else 3, P, n * P), kdec[rs, t, n, :], vn[rs, n % 2, :],
                                     start=True, stop=True, skip_group_check=True)
                if step < NC - 1:
                    sp = pe.mark(q)
                for n in range(NI):
                    t, r, ch = where[n]
                    rs = slice(r, r + CHUNK)
                    o = self.bank(7 if n < 2 else 4, CHUNK, (n % 2) * T + ch * CHUNK)
                    q = M.matmul(o, vn[rs, n % 2, :], att[rs, t, n, rs], start=False, stop=True,
                                 skip_group_check=True)
                op = pe.mark(q)
                if step < NC - 1:
                    need(V, sp, sr)
                    for n in range(NI):
                        t, r, ch = where[n]
                        col = r + CHUNK - 1 if n < 2 else r
                        st = dve.mark(V.scalar_tensor_tensor(S[:, n], S[:, n], er[:, t, n, col:col + 1],
                                                             self.bank(6 if n < 2 else 3, P, n * P), ALU.mult, ALU.add))
                    need(M, st)
            need(A, op)
            t1 = act.mark(A.activation(Y[:, 1], four(4), ACT.Copy))
            need(V, t1)
            osum = dve.mark(V.tensor_tensor(Y[:, 1], Y[:, 1], four(7), ALU.add))
            need(A, osum)
            t1 = act.mark(A.activation(Y[:, 0], Y[:, 1], ACT.Square))
            need(M, t1)
            q = pe.mark(M.matmul(self.bank(0), c["ones"], Y[:, 0], start=True, stop=True))
            need(A, q)
            rr = rn[:, :, :]
            t1 = act.mark(A.activation(rr, self.bank(0).rearrange("p (n t) -> p n t", n=2), ACT.Ln,
                                       scale=1.0 / HD, bias=c["columns"][:, 0:1]))
            need(A, t1)
            t1 = act.mark(A.activation(rr, rr, ACT.Exp, scale=-0.5))
            need(V, t1)
            t1 = dve.mark(V.tensor_tensor(rr, rr, Y[:, 1].rearrange("p (n a) j -> p n (a j)", n=2), ALU.mult))
            need(V, t1)
            dve.mark(V.scalar_tensor_tensor(self.yt[:, bass.ds(i * 2, 2), :], rr, nw[:, 0:1], zs[:, :, :],
                                            ALU.mult, ALU.mult))

    def col(self, k):
        return self.c["columns"][:, k:k + 1]

    def project(self, name, first, units, halves, lhs, evac, skip=0):
        M, pe = self.nc.tensor, self.pe
        groups = 4 // halves
        free = {}

        def body(i):
            for cg in range(groups):
                if free.get(cg) is not None:
                    self.need(M, free[cg])
                for h in range(halves):
                    s = cg * halves + h
                    self.need(M, self.arrived[s].now())
                    for t in range(NT):
                        for k in range(KT):
                            q = M.matmul(self.bank(cg, UC, t * UC), lhs[:, h * KT + k, t * P:(t + 1) * P],
                                         self.slots[:, s, k, :], start=(t == 0 and k == 0 and h == 0),
                                         stop=(k == KT - 1 and h == halves - 1), skip_group_check=True)
                    q = pe.mark(q)
                    if first + 4 + skip < UNITS:
                        self.refill(s, i * 4 + (first + 4 + skip + s), q)
                free[cg] = evac(i * groups + cg, cg, q)

        n = units // 4
        if n == 1:
            body(0)
            return
        with self.p.fori(name, n) as i:
            for cg in range(groups):
                free[cg] = self.behind(name, f"bank{cg}")
            body(i)
            for cg in range(groups):
                self.note(name, f"bank{cg}", free[cg])

    def norm_rows(self, src, sq, width, eps, st, center=False):
        A, V, act, dve = self.nc.scalar, self.nc.vector, self.act, self.dve
        for t in range(NT):
            if center:
                q = dve.mark(V.reduce_sum(st[:, 2 + t:3 + t], src[:, t], AX))
                self.need(V, q)
                q = dve.mark(V.tensor_scalar(st[:, 2 + t:3 + t], st[:, 2 + t:3 + t], 1.0 / width, None, ALU.mult))
                self.need(V, q)
                q = dve.mark(V.tensor_scalar(src[:, t], src[:, t], st[:, 2 + t:3 + t], None, ALU.subtract))
                self.need(A, q)
            q = act.mark(A.activation(sq[:, t], src[:, t], ACT.Square, accum_out=st[:, t:t + 1]))
        self.need(A, q)
        q = act.mark(A.activation(st[:, 0:NT], st[:, 0:NT], ACT.Ln, scale=1.0 / width, bias=self.col(eps)))
        self.need(A, q)
        return act.mark(A.activation(st[:, 0:NT], st[:, 0:NT], ACT.Exp, scale=-0.5))

    def turn(self, src, dst, ktiles, ready, banks, scale=None):
        M, A = self.nc.tensor, self.nc.scalar
        free = [None] * len(banks)
        self.need(M, *ready)
        for g in range(ktiles // 2):
            b = g % len(banks)
            self.need(M, free[b])
            for k in range(2):
                for t in range(NT):
                    q = M.transpose(self.bank(banks[b], P, (2 * k + t) * P),
                                    src[:, t, (2 * g + k) * P:(2 * g + k + 1) * P], self.c["ident"])
            q = self.pe.mark(q)
            self.need(A, q)
            if scale is None:
                free[b] = self.act.mark(A.activation(
                    dst[:, 2 * g:2 * g + 2, :], self.bank(banks[b]).rearrange("p (k t) -> p k t", k=2), ACT.Copy))
            else:
                for k in range(2):
                    free[b] = self.act.mark(A.activation(
                        dst[:, 2 * g + k, :], self.bank(banks[b], T, k * T), ACT.Copy, scale=scale(2 * g + k)))
        return free[b]

    def layer_norm(self, row, st, sq, gb):
        V, dve = self.nc.vector, self.dve
        q = self.norm_rows(self.x, sq, D, 1, st, center=True)
        self.need(V, q, gb[1])
        for t in range(NT):
            q = dve.mark(V.scalar_tensor_tensor(self.x[:, t], self.x[:, t], st[:, t:t + 1], gb[0][:, row],
                                                ALU.mult, ALU.mult))
            self.need(V, q)
            q = dve.mark(V.tensor_tensor(self.x[:, t], self.x[:, t], gb[0][:, 2 + row], ALU.add))
        return q

    def moe(self):
        nc, I, p, need, c = self.nc, self.ins, self.p, self.need, self.c
        pe, act, dve, pool = self.pe, self.act, self.dve, self.pool
        A, V, M = nc.scalar, nc.vector, nc.tensor
        self.fresh()
        al = self.alloc
        rows = al("rows", [P, 4, D])
        wr = al("w_route", [P, KT, GROUPS + EXPERTS])
        br = al("b_route", [P, GROUPS + EXPERTS])
        st = al("st", [P, 4])
        sq = al("sq", [P, NT, D])
        self.load(wr[:, :, :], I["w_route"])
        self.load(br[:, :], I["b_route"].to_broadcast([P, GROUPS + EXPERTS]))
        self.load(rows[:, 0:2], I["ln_g"][0].unsqueeze(0).to_broadcast([P, 2, D]))
        loaded = self.load(rows[:, 2:4], I["ln_b"][0].unsqueeze(0).to_broadcast([P, 2, D]))
        for s in (4, 5):
            self.refill(s, U_MOE + s, None)

        def add(cg, b, q):
            need(V, q)
            cols = bass.ds(cg * UC, UC)
            return dve.mark(V.scalar_tensor_tensor(
                self.x[:, :, cols], self.x[:, :, cols], ALPHA, self.bank(b).rearrange("p (t n) -> p t n", t=NT),
                ALU.mult, ALU.add))

        self.project("delta_out", U_GOUT, 8, 2, self.yt, add)
        need(V, dve.now())
        q = self.layer_norm(0, st, sq, (rows, loaded))
        q = self.turn(self.x, self.xt, KT, [q], [0, 1])

        NG = GROUPS + EXPERTS
        lg = al("lg", [P, NT, NG])
        comb = al("comb", [P, NT, GROUPS, EPG])
        m = al("m", [P, NT, 8])
        g1 = al("g1", [P, NT, GROUPS])
        e1, e2, o1, o2 = (al(n, [P, NT, EPG]) for n in ("e1", "e2", "o1", "o2"))
        need(M, q, loaded)
        for t in range(NT):
            for k in range(KT):
                q = M.matmul(self.bank(2, NG, t * NG), self.xt[:, k, t * P:(t + 1) * P], wr[:, k, :],
                             start=(k == 0), stop=(k == KT - 1), skip_group_check=True)
        q = pe.mark(q)
        need(V, q)

        def v(ins):
            need(V, dve.mark(ins))

        def first_of(o, x, mx, rank, n):
            v(V.tensor_tensor(o, x, mx.to_broadcast([P, NT, n]), ALU.is_equal))
            v(V.tensor_tensor(o, o, rank, ALU.mult))
            v(V.tensor_reduce(m[:, :, 7], o, AX, ALU.max))
            v(V.tensor_tensor(o, o, m[:, :, 7].unsqueeze(2).to_broadcast([P, NT, n]), ALU.is_equal))

        r4 = c["rank4"].rearrange("p (t n) -> p t n", t=NT)
        r8 = c["rank8"].rearrange("p (t n) -> p t n", t=NT)
        gl = lg[:, :, 0:GROUPS]
        v(V.tensor_tensor(lg[:, :, :], self.bank(2, NT * NG).rearrange("p (t n) -> p t n", t=NT),
                          br[:, :].unsqueeze(1).to_broadcast([P, NT, NG]), ALU.add))
        v(V.tensor_reduce(m[:, :, 0], gl, AX, ALU.max))
        v(V.tensor_tensor(e1[:, :, 0:GROUPS], gl, m[:, :, 0].unsqueeze(2).to_broadcast([P, NT, GROUPS]), ALU.subtract))
        q = dve.now()
        need(A, q)
        ex = act.mark(A.activation(e1[:, :, 0:GROUPS], e1[:, :, 0:GROUPS], ACT.Exp))
        first_of(g1[:, :, :], gl, m[:, :, 0].unsqueeze(2), r4, GROUPS)
        need(V, ex)
        v(V.tensor_reduce(m[:, :, 1], e1[:, :, 0:GROUPS], AX, ALU.add))
        v(V.reciprocal(m[:, :, 1], m[:, :, 1]))
        v(V.memset(e1[:, :, :], 0.0))
        el = lg[:, :, GROUPS:].rearrange("p t (g e) -> p t g e", g=GROUPS)
        for g in range(GROUPS):
            v(V.tensor_tensor(e2[:, :, :], el[:, :, g], g1[:, :, g:g + 1].to_broadcast([P, NT, EPG]), ALU.mult))
            v(V.tensor_tensor(e1[:, :, :], e1[:, :, :], e2[:, :, :], ALU.add))
        v(V.tensor_reduce(m[:, :, 2], e1[:, :, :], AX, ALU.max))
        first_of(o1[:, :, :], e1[:, :, :], m[:, :, 2].unsqueeze(2), r8, EPG)
        v(V.scalar_tensor_tensor(e2[:, :, :], o1[:, :, :], -BIG, e1[:, :, :], ALU.mult, ALU.add))
        v(V.tensor_reduce(m[:, :, 3], e2[:, :, :], AX, ALU.max))
        first_of(o2[:, :, :], e2[:, :, :], m[:, :, 3].unsqueeze(2), r8, EPG)
        v(V.tensor_tensor(m[:, :, 4], m[:, :, 3], m[:, :, 2], ALU.subtract))
        need(A, dve.now())
        ex = act.mark(A.activation(m[:, :, 4], m[:, :, 4], ACT.Exp))
        need(V, ex)
        v(V.tensor_scalar(m[:, :, 5], m[:, :, 4], 1.0, None, ALU.add))
        v(V.reciprocal(m[:, :, 5], m[:, :, 5]))
        v(V.tensor_tensor(m[:, :, 5], m[:, :, 5], m[:, :, 1], ALU.mult))
        v(V.tensor_tensor(m[:, :, 6], m[:, :, 5], m[:, :, 4], ALU.mult))
        v(V.tensor_tensor(o1[:, :, :], o1[:, :, :], m[:, :, 5].unsqueeze(2).to_broadcast([P, NT, EPG]), ALU.mult))
        v(V.tensor_tensor(o2[:, :, :], o2[:, :, :], m[:, :, 6].unsqueeze(2).to_broadcast([P, NT, EPG]), ALU.mult))
        v(V.tensor_tensor(o1[:, :, :], o1[:, :, :], o2[:, :, :], ALU.add))
        for g in range(GROUPS):
            v(V.tensor_tensor(comb[:, :, g], o1[:, :, :], g1[:, :, g:g + 1].to_broadcast([P, NT, EPG]), ALU.mult))

        FT = HID // P
        sg = al("sg", [P, 2, NT, HID])
        hh = al("hh", [P, 2, NT, HID])
        ht = al("ht", [P, 2, FT, T])
        cs = al("cs", [P, NT, 2])
        zero = al("zero", [P, P])
        v(V.memset(zero[:, :], 0.0))
        v(V.memset(ht[:, :, :, :], 0.0))
        down = lambda s: self.slots[:, s].rearrange("p a b -> p (a b)").rearrange("p (f n) -> p f n", f=FT)
        need(M, dve.now(), act.now())
        for b in range(4):
            q = M.matmul(self.bank(4 + b), zero[:, :], self.x[:, b // 2, (b % 2) * 512:(b % 2 + 1) * 512],
                         start=True, stop=False, skip_group_check=True)

        def down_product(e, s):
            need(M, self.arrived[s].now())
            for b in range(4):
                for f in range(FT):
                    q = M.matmul(self.bank(4 + b), ht[:, e, f, (b // 2) * P:(b // 2 + 1) * P],
                                 down(s)[:, f, (b % 2) * 512:(b % 2 + 1) * 512], start=False, stop=True,
                                 skip_group_check=True)
            return pe.mark(q)

        combv = comb[:, :, :, :].rearrange("p t g e -> p t (g e)")
        with p.fori("experts", EXPERTS // 2) as i:
            need(V, self.behind("experts", "gate_read1"))
            sc = dve.mark(V.tensor_copy(cs[:, :, :], combv[:, :, bass.ds(i * 2, 2)]))
            need(V, sc)
            for e in range(2):
                gate, up = 3 * e, 3 * e + 1
                need(M, self.arrived[gate].now(), self.arrived[up].now())
                if e == 0:
                    need(M, self.behind("experts", "gate_read1"))
                else:
                    need(M, gu_read)
                gu = []
                for t in range(NT):
                    for n, s in ((0, gate), (1, up)):
                        for k in range(KT):
                            q = M.matmul(self.bank(t, HID, n * HID), self.xt[:, k, t * P:(t + 1) * P],
                                         self.slots[:, s, k, :], start=(n == 0 and k == 0),
                                         stop=(k == KT - 1), skip_group_check=True)
                    gu.append(pe.mark(q))
                self.refill(gate, i * 6 + (U_MOE + 6 + gate), gu[1])
                self.refill(up, i * 6 + (U_MOE + 6 + up), gu[1])
                for t in range(NT):
                    need(A, gu[t], self.behind("experts", f"gate_read{e}"))
                    q = act.mark(A.activation(sg[:, e, t], self.bank(t, HID), ACT.Silu))
                    need(V, q, gu[t], self.behind("experts", f"turned{e}"))
                    gu_read = dve.mark(V.scalar_tensor_tensor(hh[:, e, t], self.bank(t, HID, HID), cs[:, t, e:e + 1],
                                                              sg[:, e, t], ALU.mult, ALU.mult))
                self.note("experts", f"gate_read{e}", gu_read)
                if e == 0:
                    need(M, self.behind("experts", "ht1"))
                    q = down_product(1, 5)
                    self.refill(5, i * 6 + (U_MOE + 5), q)
                else:
                    need(M, hq)
                    q = down_product(0, 2)
                    self.refill(2, i * 6 + (U_MOE + 8), q)
                need(M, gu_read, self.behind("experts", f"ht{e}"))
                for f in range(FT):
                    for t in range(NT):
                        q = M.transpose(self.bank(2 + e, P, (f * NT + t) * P), hh[:, e, t, f * P:(f + 1) * P], c["ident"])
                q = pe.mark(q)
                self.note("experts", f"turned{e}", q)
                need(A, q)
                hq = act.mark(A.activation(ht[:, e], self.bank(2 + e).rearrange("p (f t) -> p f t", f=FT), ACT.Copy))
                self.note("experts", f"ht{e}", hq)
        need(M, hq)
        q = down_product(1, 5)
        self.refill(5, U_POOL, q)
        need(V, q)
        for t in range(NT):
            q = dve.mark(V.scalar_tensor_tensor(
                self.x[:, t].rearrange("p (a n) -> p a n", a=2), self.x[:, t].rearrange("p (a n) -> p a n", a=2),
                ALPHA, self.ps[:, 4 + 2 * t:6 + 2 * t], ALU.mult, ALU.add))
        need(V, q)
        self.layer_norm(1, st, sq, (rows, loaded))

    def chain(self):
        def v(ins):
            q = self.dve.mark(ins)
            self.need(self.nc.vector, q)
            return q
        return v

    def embed(self):
        nc, I, need = self.nc, self.ins, self.need
        pe, act, dve = self.pe, self.act, self.dve
        A, V, M = nc.scalar, nc.vector, nc.tensor
        self.fresh()
        pt = self.alloc("pt", [P, 2, T])
        sg = self.alloc("sg", [P, 4, NT, UC])
        loaded = self.load(pt[:, :, :], I["pt"])
        t = self.turn(self.x, self.xt, KT, [dve.now()], [0, 1])
        need(M, t, loaded, self.arrived[4].now())
        wp = self.slots[:, 4].rearrange("p a b -> p (a b)").rearrange("p (f n) -> p f n", f=2)
        for cg in range(4):
            for t in range(NT):
                for f in range(2):
                    q = M.matmul(self.bank(4 + cg, UC, t * UC), pt[:, f, t * P:(t + 1) * P],
                                 wp[:, f, cg * UC:(cg + 1) * UC], start=(f == 0), stop=(f == 1),
                                 skip_group_check=True)
        pq = pe.mark(q)

        def gate(cg, b, q):
            need(A, q)
            q = act.mark(A.activation(sg[:, cg], self.bank(b).rearrange("p (t n) -> p t n", t=NT), ACT.Sigmoid))
            need(V, q, pq)
            r = dve.mark(V.tensor_tensor(sg[:, cg], sg[:, cg],
                                         self.bank(4 + cg).rearrange("p (t n) -> p t n", t=NT), ALU.mult))
            need(V, r)
            xc = self.x[:, :, cg * UC:(cg + 1) * UC]
            dve.mark(V.tensor_tensor(xc, xc, sg[:, cg], ALU.add))
            return q

        self.project("embed", U_PE, 4, 1, self.xt, gate, skip=2)

    def even(self):
        nc, I, p, need, c = self.nc, self.ins, self.p, self.need, self.c
        pe, act, dve = self.pe, self.act, self.dve
        A, V, M = nc.scalar, nc.vector, nc.tensor
        self.fresh()
        al = self.alloc
        self.consts("pool", self.slots[:, 4].rearrange("p a b -> p (a b)"))
        self.consts("late")
        ecw = al("ecw", [P, 16, 4])
        wif = al("wif", [P, KT, 2 * AH])
        bif = al("bif", [P, 2 * AH])
        feat = al("feat", [P, FEATS])
        self.load(ecw[:, :, :], I["ecw"])
        self.load(wif[:, :, :], I["w_if"])
        self.load(bif[:, :], I["e_b_if_2"].to_broadcast([P, 2 * AH]))
        loaded = self.load(feat[:, :], I["feat"])
        fcol = lambda at: (lambda k: feat[:, at + k:at + k + 1])
        st = al("st", [P, 4])
        qk = al("qk", [P, 16, T])
        pj = al("pj", [P, 5, NT, D])
        mark = self.top
        xn = al("xn", [P, NT, D])
        v = self.chain()
        q = self.norm_rows(self.x, xn, D, 0, st)
        need(V, q)
        for t in range(NT):
            q = dve.mark(V.tensor_scalar(xn[:, t], self.x[:, t], st[:, t:t + 1], None, ALU.mult))
        need(A, loaded)
        self.turn(xn, self.xt, KT, [q], [0, 1], fcol(F_ENORM))
        self.p.barrier()
        self.top = mark
        raw = al("raw", [P, 8, T + 3])
        cws = al("cws", [P, 8, 4])
        v(V.memset(raw[:, :, :], 0.0))
        need(A, dve.now())
        with p.fori("even_qk", 2) as i:
            for l in (pe, act, dve):
                self.all_before("even_qk", l)
            v(V.tensor_copy(cws[:, :, :], ecw[:, bass.ds(i * 8, 8), :]))
            for s in range(4):
                need(M, self.arrived[s].now())
                for n in range(2):
                    for k in range(KT):
                        q = M.matmul(self.bank(s, T, T * n), self.slots[:, s, k, n * P:(n + 1) * P],
                                     self.xt[:, k, :], start=(k == 0), stop=(k == KT - 1), skip_group_check=True)
                q = pe.mark(q)
                self.refill(s, i * 4 + (U_EIN + 4 + s), q)
                need(A, q)
                q = act.mark(A.activation(raw[:, 2 * s:2 * s + 2, 3:3 + T],
                                          self.bank(s).rearrange("p (n t) -> p n t", n=2), ACT.Copy))
                need(V, q)
                last = [None] * 2
                for tap in range(4):
                    for n in range(2):
                        j = 2 * s + n
                        o = qk[:, bass.ds(i * 8 + j, 1), :]
                        src = raw[:, j:j + 1, tap:tap + T]
                        need(V, last[n])
                        if tap == 0:
                            last[n] = dve.mark(V.tensor_scalar(o, src, cws[:, j, 0:1], None, ALU.mult))
                        else:
                            last[n] = dve.mark(V.scalar_tensor_tensor(o, src, cws[:, j, tap:tap + 1], o,
                                                                      ALU.mult, ALU.add))
            need(A, last[1])
            o = qk[:, bass.ds(i * 8, 8), :]
            act.mark(A.activation(o, o, ACT.Silu))
            for l in (pe, act, dve):
                self.note("even_qk", l.name, l.now())

        pjv = pj[:, :, :, :].rearrange("p s t n -> p (s t) n")

        def keep(cg, b, q):
            need(A, q)
            return act.mark(A.activation(pjv[:, bass.ds((cg // 4) * 2, 2), bass.ds((cg % 4) * UC, UC)],
                                         self.bank(b).rearrange("p (t n) -> p t n", t=NT), ACT.Copy))

        self.project("even_in", U_EIN + 8, 20, 1, self.xt, keep)
        VS, OS, ZA, US, ZB = range(5)
        need(A, act.now())
        act.mark(A.activation(pj[:, OS], pj[:, OS], ACT.Sigmoid))
        act.mark(A.activation(pj[:, ZA], pj[:, ZA], ACT.Silu))
        zq = act.mark(A.activation(pj[:, ZB], pj[:, ZB], ACT.Silu))
        gt = al("gt", [P, NT, 2 * AH])
        lf = al("lf", [P, NT, AH])
        l2 = al("l2", [P, NT, AH])
        bc = al("bc", [P, NT, AH])
        ai = al("ai", [P, NT, AH])
        need(M, act.now())
        for t in range(NT):
            for k in range(KT):
                q = M.matmul(self.bank(4, 2 * AH, t * 2 * AH), self.xt[:, k, t * P:(t + 1) * P], wif[:, k, :],
                             start=(k == 0), stop=(k == KT - 1), skip_group_check=True)
        q = pe.mark(q)
        need(V, q)
        v(V.tensor_tensor(gt[:, :, :], self.bank(4, 4 * AH).rearrange("p (t n) -> p t n", t=NT),
                          bif[:, :].unsqueeze(1).to_broadcast([P, NT, 2 * AH]), ALU.add))
        fg = gt[:, :, AH:2 * AH]
        v(V.scalar_tensor_tensor(l2[:, :, :], fg, -1.0, fg, ALU.mult, ALU.max))
        need(A, dve.now())
        q = act.mark(A.activation(l2[:, :, :], l2[:, :, :], ACT.Exp, scale=-1.0))
        need(A, q)
        q = act.mark(A.activation(l2[:, :, :], l2[:, :, :], ACT.Ln, bias=1.0))
        need(V, q)
        v(V.scalar_tensor_tensor(lf[:, :, :], fg, 0.0, l2[:, :, :], ALU.min, ALU.subtract))
        need(M, dve.now())
        for t in range(NT):
            for s in range(t + 1):
                q = M.matmul(self.bank(5, AH, t * AH), c["upto_all"] if s == t else c["ones"], lf[:, s, :],
                             start=(s == 0), stop=(s == t), skip_group_check=True)
        q = pe.mark(q)
        need(V, q)
        v(V.tensor_copy(bc[:, :, :], self.bank(5, 2 * AH).rearrange("p (t n) -> p t n", t=NT)))
        v(V.tensor_tensor(ai[:, :, :], gt[:, :, 0:AH], bc[:, :, :], ALU.subtract))
        ab = raw[:, 0:4, 0:P]
        for t in range(NT):
            v(V.tensor_copy(ab, ai[:, t, :].unsqueeze(2).to_broadcast([P, AH, P])))
            need(M, dve.now())
            for h in range(AH):
                q = M.matmul(self.bank(6 + h // 2, P, (h % 2) * T + t * P), ab[:, h], c["ident"],
                             start=True, stop=True, skip_group_check=True)
            q = pe.mark(q)
            need(V, q)
        late = c["late"].rearrange("p (t s) -> p t s", t=NT)
        self.top = mark
        self.p.barrier()
        ww = al("ww", [P, AH, T])
        wt = al("wt", [P, AH, 2, P])
        mm = al("mm", [P, 8, NT, AH])
        hn = al("hn", [P, AH, AD])
        for t in range(NT):
            for b in range(2):
                v(V.tensor_tensor(ww[:, 2 * b:2 * b + 2], self.bank(6 + b).rearrange("p (h s) -> p h s", h=2),
                                  late[:, t].unsqueeze(1).to_broadcast([P, 2, T]), ALU.subtract))
            v(V.tensor_reduce(mm[:, 0, t], ww[:, :, :], AX, ALU.max))
            v(V.tensor_scalar(mm[:, 0, t], mm[:, 0, t], 0.0, None, ALU.max))
            v(V.tensor_scalar(mm[:, 1, t], mm[:, 0, t], -1.0, None, ALU.mult))
            v(V.tensor_tensor(mm[:, 3, t], mm[:, 1, t], bc[:, t], ALU.subtract))
            need(A, dve.now())
            act.mark(A.activation(mm[:, 3, t], mm[:, 3, t], ACT.Exp))
            for h in range(AH):
                eq = act.mark(A.activation(ww[:, h], ww[:, h], ACT.Exp, bias=mm[:, 1, t, h:h + 1]))
            need(M, act.now(), dve.now())
            for h in range(AH):
                for k in range(2):
                    q = M.matmul(self.bank(h // 2, T, (h % 2) * T), qk[:, 2 * h + k, t * P:(t + 1) * P],
                                 qk[:, 8 + 2 * h + k, :], start=(k == 0), stop=(k == 1), skip_group_check=True)
            q = pe.mark(q)
            need(V, eq, q)
            for h in range(AH):
                q = dve.mark(V.scalar_tensor_tensor(ww[:, h], self.bank(h // 2, T, (h % 2) * T), AD ** -0.5,
                                                    ww[:, h], ALU.mult, ALU.mult, accum_out=mm[:, 2, t, h:h + 1]))
            need(V, q)
            v(V.scalar_tensor_tensor(mm[:, 4, t], mm[:, 2, t], -1.0, mm[:, 2, t], ALU.mult, ALU.max))
            v(V.tensor_tensor(mm[:, 4, t], mm[:, 4, t], mm[:, 3, t], ALU.max))
            v(V.reciprocal(mm[:, 4, t], mm[:, 4, t]))
            need(M, dve.now())
            for h in range(AH):
                for s in range(2):
                    q = M.transpose(self.bank(2 + h // 2, P, ((h % 2) * 2 + s) * P), ww[:, h, s * P:(s + 1) * P],
                                    c["ident"])
            q = pe.mark(q)
            need(A, q)
            for b in range(2):
                q = act.mark(A.activation(wt[:, 2 * b:2 * b + 2], self.bank(2 + b).rearrange(
                    "p (h s j) -> p h s j", h=2, s=2), ACT.Copy))
            need(M, q)
            for h in range(AH):
                for s in range(t + 1):
                    q = M.matmul(self.bank(4 + h // 2, AD, (h % 2) * AD), wt[:, h, s, :],
                                 pj[:, VS, s, h * AD:(h + 1) * AD], start=(s == 0), stop=(s == t),
                                 skip_group_check=True)
            q = pe.mark(q)
            need(V, q)
            og = pj[:, OS, t].rearrange("p (h d) -> p h d", h=AH)
            for h in range(AH):
                q = dve.mark(V.scalar_tensor_tensor(hn[:, h], self.bank(4 + h // 2, AD, (h % 2) * AD),
                                                    mm[:, 4, t, h:h + 1], og[:, h], ALU.mult, ALU.mult))
            need(A, q)
            for h in range(AH):
                q = act.mark(A.activation(ww[:, h], hn[:, h], ACT.Square, accum_out=mm[:, 5, t, h:h + 1]))
            need(A, q)
            q = act.mark(A.activation(mm[:, 5, t], mm[:, 5, t], ACT.Ln, scale=1.0 / AD, bias=self.col(0)))
            need(A, q)
            q = act.mark(A.activation(mm[:, 5, t], mm[:, 5, t], ACT.Exp, scale=-0.5))
            need(V, q, zq)
            za = pj[:, ZA, t].rearrange("p (h d) -> p h d", h=AH)
            for h in range(AH):
                q = dve.mark(V.scalar_tensor_tensor(za[:, h], hn[:, h], mm[:, 5, t, h:h + 1], za[:, h],
                                                    ALU.mult, ALU.mult))
            need(V, q)
        self.p.barrier()
        need(M, self.arrived[5].now(), self.small.now())
        win = c["window"].rearrange("p (g s t) -> p g s t", g=4, s=NT)
        pw = self.slots[:, 5].rearrange("p a b -> p (a b)").rearrange("p (g f n) -> p g f n", g=4, f=2)
        pT = ww
        zb = []
        for g in range(4):
            b = g % 2
            for f in range(2):
                for s in range(NT):
                    q = M.matmul(self.bank(b, T, f * T), pj[:, US, s, (2 * g + f) * P:(2 * g + f + 1) * P],
                                 win[:, g, s], start=(s == 0), stop=(s == NT - 1), skip_group_check=True)
            q = pe.mark(q)
            need(A, q)
            q = act.mark(A.activation(pT[:, 2 * b:2 * b + 2], self.bank(b).rearrange("p (f t) -> p f t", f=2), ACT.Copy))
            need(M, q)
            if g >= 2:
                need(M, zb[g - 2])
            for t in range(NT):
                for f in range(2):
                    q = M.matmul(self.bank(2 + b, UC, t * UC), pT[:, 2 * b + f, t * P:(t + 1) * P], pw[:, g, f],
                                 start=(f == 0), stop=(f == 1), skip_group_check=True)
            q = pe.mark(q)
            need(V, q)
            cols = pj[:, ZB, :, g * UC:(g + 1) * UC]
            zb.append(dve.mark(V.tensor_tensor(
                cols, cols, self.bank(2 + b).rearrange("p (t n) -> p t n", t=NT), ALU.mult)))
        self.turn(pj[:, ZA], self.yt[:, 0:8], KT, [dve.now()], [4, 5], fcol(F_HEAD))
        q = self.turn(pj[:, ZB], self.yt[:, 8:16], KT, [dve.now()], [6, 7], fcol(F_POOL))
        need(M, q)
        self.project("even_out", U_EOUT, 8, 2, self.yt, self.add_to_x)

    def odd(self):
        nc, I, p, need, c = self.nc, self.ins, self.p, self.need, self.c
        pe, act, dve = self.pe, self.act, self.dve
        A, V, M = nc.scalar, nc.vector, nc.tensor
        self.fresh()
        al = self.alloc
        self.consts("late")
        wki = al("wki", [P, KT, 132])
        feat = al("feat", [P, FEATS])
        rb = al("rb", [BUCKETS, CH])
        st = al("st", [P, 4])
        self.load(wki[:, :, :], I["w_ki"])
        self.load(feat[:, :], I["feat"])
        loaded = self.load(rb[:, :], I["rel_bias_2"])
        fcol = lambda at: (lambda k: feat[:, at + k:at + k + 1])
        v = self.chain()
        pq = al("pq", [P, 2, NT, D])
        fb = al("fb", [CH, 2 * T])
        xn = al("xn", [P, NT, D])
        kk = al("kk", [P, NT, D])
        vv = al("vv", [P, NT, D])
        self.pq, self.vv = pq, vv
        need(M, loaded)
        q = pe.mark(M.matmul(self.ps[0:CH, 7, :], rb[:, :], c["onehot"][0:BUCKETS, :], start=True, stop=True))
        need(A, q)
        q = act.mark(A.activation(fb[:, :], self.ps[0:CH, 7, :], ACT.Copy))
        need(A, q)
        wrote = self.scratch_done.mark(A.dma_start(self.bias_rows, fb[:, :]))
        q = self.norm_rows(self.x, xn, D, 0, st)
        need(V, q)
        for t in range(NT):
            q = dve.mark(V.tensor_scalar(xn[:, t], self.x[:, t], st[:, t:t + 1], None, ALU.mult))
        need(A, loaded)
        q = self.turn(xn, self.xt, KT, [q], [0, 1], fcol(F_ONORM))
        need(M, q)
        pqv = pq[:, :, :, :].rearrange("p s t n -> p (s t) n")

        def keep(cg, b, q):
            need(A, q)
            return act.mark(A.activation(pqv[:, bass.ds((cg // 4) * 2, 2), bass.ds((cg % 4) * UC, UC)],
                                         self.bank(b).rearrange("p (t n) -> p t n", t=NT), ACT.Copy))

        self.project("odd_in", U_OIN, 8, 1, self.xt, keep)
        need(M, act.now())
        need(M, self.arrived[0].now(), self.arrived[1].now())
        for t in range(NT):
            for k in range(KT):
                q = M.matmul(self.bank(0, UC, t * UC), self.xt[:, k, t * P:(t + 1) * P], self.slots[:, 0, k, :],
                             start=(k == 0), stop=(k == KT - 1), skip_group_check=True)
        self.refill(0, U_OOUT, pe.mark(q))
        for n in range(2):
            for k in range(KT):
                q = M.matmul(self.bank(1, T, n * T), self.slots[:, 1, k, n * P:(n + 1) * P], self.xt[:, k, :],
                             start=(k == 0), stop=(k == KT - 1), skip_group_check=True)
        self.refill(1, U_OOUT + 1, pe.mark(q))
        for k in range(KT):
            M.matmul(self.bank(2, T), wki[:, k, 0:P], self.xt[:, k, :], start=(k == 0), stop=(k == KT - 1),
                     skip_group_check=True)
        for t in range(NT):
            for k in range(KT):
                q = M.matmul(self.bank(3, IH, t * IH), self.xt[:, k, t * P:(t + 1) * P], wki[:, k, P:P + IH],
                             start=(k == 0), stop=(k == KT - 1), skip_group_check=True)
        q = pe.mark(q)
        ck = xn[:, 0, 0:NT * UC].rearrange("p (t n) -> p t n", t=NT)
        ckt = xn[:, 0, 512:1024].rearrange("p (k t) -> p k t", k=2)
        qit = xn[:, 1, 0:512].rearrange("p (k t) -> p k t", k=2)
        kit = xn[:, 1, 512:512 + T]
        wi = al("wi", [P, NT, IH])
        s4 = al("s4", [P, 4])
        need(A, q)
        act.mark(A.activation(qit, self.bank(1).rearrange("p (k t) -> p k t", k=2), ACT.Copy))
        act.mark(A.activation(kit, self.bank(2, T), ACT.Copy))
        act.mark(A.activation(wi[:, :, :], self.bank(3, NT * IH).rearrange("p (t n) -> p t n", t=NT), ACT.Copy,
                              scale=IH ** -0.5))
        for t in range(NT):
            q = act.mark(A.activation(ck[:, t], self.bank(0, UC, t * UC), ACT.Square, accum_out=s4[:, t:t + 1]))
        need(A, q)
        q = act.mark(A.activation(s4[:, 0:NT], s4[:, 0:NT], ACT.Ln, scale=1.0 / UC, bias=self.col(0)))
        need(A, q)
        q = act.mark(A.activation(s4[:, 0:NT], s4[:, 0:NT], ACT.Exp, scale=-0.5))
        need(V, q)
        for t in range(NT):
            q = dve.mark(V.tensor_scalar(ck[:, t], self.bank(0, UC, t * UC), s4[:, t:t + 1], None, ALU.mult))
        need(M, act.now())
        q = self.turn(ck, ckt, 2, [q], [4], fcol(F_KV))
        need(M, q, self.arrived[2].now(), self.arrived[3].now())
        for s, dst in ((2, kk), (3, vv)):
            w = self.slots[:, s].rearrange("p a b -> p (a b)").rearrange("p (f n) -> p f n", f=2)
            for t in range(NT):
                for b in range(2):
                    for f in range(2):
                        m = M.matmul(self.bank(2 * (s - 2) + b + 4 * (t % 2)), ckt[:, f, t * P:(t + 1) * P],
                                     w[:, f, b * 512:(b + 1) * 512], start=(f == 0), stop=(f == 1),
                                     skip_group_check=True)
                m = pe.mark(m)
                need(A, m)
                b0 = 2 * (s - 2) + 4 * (t % 2)
                act.mark(A.activation(dst[:, t].rearrange("p (b n) -> p b n", b=2), self.ps[:, b0:b0 + 2], ACT.Copy))
            self.refill(s, U_OOUT + s, m)
        qT, kT = self.yt[:, 0:8], self.yt[:, 8:16]
        sh = al("sh", [P, NT, CH])
        need(V, act.now())
        for src, dst, at in ((pq[:, 0], qT, F_Q), (kk, kT, F_K)):
            tv = self.xt[:, :, :].rearrange("p k t -> p (k t)").rearrange("p (t h d) -> p t h d", t=NT, h=CH)
            sv = src.rearrange("p t (h d) -> p t h d", h=CH)
            v(V.tensor_tensor(tv, sv, sv, ALU.mult))
            v(V.tensor_reduce(sh[:, :, :], tv, AX, ALU.add))
            need(A, dve.now())
            q = act.mark(A.activation(sh[:, :, :], sh[:, :, :], ACT.Ln, scale=1.0 / CD, bias=self.col(0)))
            need(A, q)
            q = act.mark(A.activation(sh[:, :, :], sh[:, :, :], ACT.Exp, scale=-0.5))
            need(V, q)
            for t in range(NT):
                v(V.tensor_tensor(sv[:, t], sv[:, t], sh[:, t].unsqueeze(2).to_broadcast([P, CH, CD]), ALU.mult))
            need(M, act.now())
            self.turn(src, dst, KT, [dve.now()], [4, 5], lambda k: feat[:, at:at + 1])
        zq = act.mark(A.activation(pq[:, 1], pq[:, 1], ACT.Silu))
        self.p.barrier()
        late = c["late"].rearrange("p (t s) -> p t s", t=NT)
        rl = kk[:, 0].rearrange("p (h s) -> p h s", h=IH)
        work = kk[:, 1, 0:T]
        best = al("best", [P, 8])
        mask = al("mask", [P, NT, T])
        tb = al("tb", [P, CH, T])
        for t in range(NT):
            need(M, act.now(), dve.now())
            for h in range(IH):
                r = slice(CD * (h % 2), CD * (h % 2) + CD)
                q = M.matmul(self.bank(2 * (h % 2), T, (h // 2) * T), qit[r, h // 2, t * P:(t + 1) * P], kit[r, :],
                             start=True, stop=True, skip_group_check=True)
            q = pe.mark(q)
            need(A, q, dve.now())
            for h in range(IH):
                q = act.mark(A.activation(rl[:, h], self.bank(2 * (h % 2), T, (h // 2) * T), ACT.Relu,
                                          scale=IDIM ** -0.5))
            need(V, q)
            v(V.tensor_scalar(mask[:, t], rl[:, 0], wi[:, t, 0:1], None, ALU.mult))
            for h in range(1, IH):
                v(V.scalar_tensor_tensor(mask[:, t], rl[:, h], wi[:, t, h:h + 1], mask[:, t], ALU.mult, ALU.add))
            v(V.tensor_tensor(work, mask[:, t], late[:, t], ALU.subtract))
            for r in range(SEL // 8):
                v(V.max(best[:, :], work))
                v(V.match_replace(work, best[:, :], work, TAKEN))
            v(V.tensor_scalar(work, work, TAKEN / 2, -BIG, ALU.is_gt, ALU.mult))
            v(V.tensor_tensor(mask[:, t], work, late[:, t], ALU.subtract))
        lg = kk[:, 0].rearrange("p (h s) -> p h s", h=4)
        pt = kk[:, 1].rearrange("p (h s t) -> p h s t", h=4, s=2)
        mx = al("mx", [P, NT, CH])
        dn = al("dn", [P, NT, CH])
        out = xn
        for t in range(NT):
            self.p.barrier()
            if t == 0:
                need(A, wrote)
            src = self.bias_src(t)
            got = self.small.mark(A.dma_start(tb[:, :, :], src))
            need(V, got)
            need(M, got)
            for g in range(4):
                need(M, dve.now(), act.now())
                for j in range(4):
                    h = 4 * g + j
                    r = slice(CD * (h % 2), CD * (h % 2) + CD)
                    q = M.matmul(self.bank(h % 2, T, (j // 2) * T), qT[r, h // 2, t * P:(t + 1) * P],
                                 kT[r, h // 2, :], start=True, stop=True, skip_group_check=True)
                q = pe.mark(q)
                need(V, q)
                for b in range(2):
                    v(V.scalar_tensor_tensor(lg[:, b::2, :], self.bank(b).rearrange("p (h s) -> p h s", h=2),
                                             CD ** -0.5, tb[:, 4 * g + b:4 * g + 4:2, ::-1], ALU.mult, ALU.add))
                v(V.tensor_tensor(lg, lg, mask[:, t].unsqueeze(1).to_broadcast([P, 4, T]), ALU.add))
                v(V.tensor_reduce(mx[:, t, 4 * g:4 * g + 4], lg, AX, ALU.max))
                v(V.tensor_scalar(mx[:, t, 4 * g:4 * g + 4], mx[:, t, 4 * g:4 * g + 4], -1.0, None, ALU.mult))
                need(A, dve.now())
                for j in range(4):
                    h = 4 * g + j
                    q = act.mark(A.activation(lg[:, j], lg[:, j], ACT.Exp, bias=mx[:, t, h:h + 1],
                                              accum_out=dn[:, t, h:h + 1]))
                need(M, q)
                for j in range(4):
                    for s in range(t + 1):
                        q = M.transpose(self.bank(2 + j // 2, P, ((j % 2) * 2 + s) * P), lg[:, j, s * P:(s + 1) * P],
                                        c["ident"])
                q = pe.mark(q)
                need(A, q)
                for b in range(2):
                    q = act.mark(A.activation(pt[:, 2 * b:2 * b + 2, 0:t + 1], self.bank(2 + b).rearrange(
                        "p (h s j) -> p h s j", h=2, s=2)[:, :, 0:t + 1], ACT.Copy))
                need(M, q)
                for j in range(4):
                    h = 4 * g + j
                    for s in range(t + 1):
                        q = M.matmul(self.bank(4 + 2 * t + h // 8, CD, (h % 8) * CD), pt[:, j, s, :],
                                     vv[:, s, h * CD:(h + 1) * CD], start=(s == 0), stop=(s == t),
                                     skip_group_check=True)
                q = pe.mark(q)
                need(A, q)
            need(V, q, act.now(), zq)
            v(V.reciprocal(dn[:, t], dn[:, t]))
            v(V.tensor_tensor(out[:, t].rearrange("p (h d) -> p h d", h=CH),
                              self.ps[:, 4 + 2 * t:6 + 2 * t].rearrange("p b (h d) -> p (b h) d", h=8),
                              dn[:, t].unsqueeze(2).to_broadcast([P, CH, CD]), ALU.mult))
            v(V.tensor_tensor(out[:, t], out[:, t], pq[:, 1, t], ALU.mult))
        q = self.turn(out, self.xt, KT, [dve.now()], [0, 1])
        need(M, q)
        self.project("odd_out", U_OOUT, 4, 1, self.xt, self.add_to_x)
        self.need(nc.sync, dve.now())
        o = self.stored.mark(nc.sync.dma_start(self.out.rearrange("a (n p) d -> p (a n) d", p=P), self.x[:, :, :]))
        self.need(nc.sync, o)

    def bias_src(self, t):
        return bass.AP(self.bias_rows.tensor, t * P, [[1, P], [2 * T, CH], [1, T]])

    def add_to_x(self, cg, b, q):
        self.need(self.nc.vector, q)
        cols = self.x[:, :, bass.ds(cg * UC, UC)]
        return self.dve.mark(self.nc.vector.tensor_tensor(
            cols, cols, self.bank(b).rearrange("p (t n) -> p t n", t=NT), ALU.add))

    def all_before(self, loop, line):
        q = self.behind(loop, line.name)
        for e in (self.nc.tensor, self.nc.scalar, self.nc.vector):
            self.need(e, q)

    def note(self, loop, name, point):
        base = self.p.starts[point.line.name]
        self.p.found.setdefault("notes", {})[(loop, name)] = (point.line.name, point.value - base)

    def behind(self, loop, name):
        got = self.p.per.get("notes", {}).get((loop, name))
        if got is None:
            return None
        line = next(l for l in self.p.lines if l.name == got[0])
        return Point(line, self.p.starts[line.name] + got[1] - self.p.loop.per[line.name], self.p.loop)

    def finish_debug(self, t):
        self.need(self.nc.sync, self.dve.now(), self.act.now())
        q = self.small.mark(self.nc.sync.dma_start(self.dbg, t[:, :, :]))
        self.need(self.nc.sync, q)


def pack_units(w, rows_of_tiles=None):
    K, N = w.shape
    return w.reshape(K // D, KT, P, N // UC, UC).transpose(0, 3, 2, 1, 4)


def layout(I):
    A = {}
    w = I["gdn_w_in"][0]
    kw = QKH * HD
    sec = {"q": w[:, 0:kw], "k": w[:, kw:2 * kw], "v": w[:, 2 * kw:2 * kw + VH * HD],
           "z": w[:, 2 * kw + VH * HD:2 * kw + 2 * VH * HD]}
    heads = []
    for h in range(QKH):
        parts = [np.concatenate([sec["q"][:, h * HD:(h + 1) * HD], sec["k"][:, h * HD:(h + 1) * HD]], 1),
                 sec["v"][:, h * UC:(h + 1) * UC], sec["z"][:, h * UC:(h + 1) * UC]]
        heads.append(np.stack([pack_units(q)[0, 0] for q in parts]))
    cols = lambda w: pack_units(w)[0]
    halves = lambda w: pack_units(w).transpose(1, 0, 2, 3, 4).reshape(-1, P, KT, UC)
    wide = lambda w: w.reshape(2, P, D).transpose(1, 0, 2).reshape(P, KT, UC)
    wg, wup = (I[n][0].reshape(EXPERTS, KT, P, HID).transpose(0, 2, 1, 3) for n in ("moe_w_gate", "moe_w_up"))
    wdn = I["moe_w_down"][0].reshape(EXPERTS, 2, P, D).transpose(0, 2, 1, 3).reshape(EXPERTS, P, KT, UC)
    e = I["e_w_in_2"][0]
    g0, e1 = 5 * D, 5 * D + 2 * AH
    o = I["o_w_in_2"][0]
    ck, qi, ki = D, D + 256, D + 512
    units = np.concatenate([
        np.concatenate(heads), halves(I["gdn_w_out"][0]),
        np.stack([wg, wup, wdn], 1).reshape(3 * EXPERTS, P, KT, UC),
        cols(I["pe_w_gate"][0]), wide(I["pe_w_proj"][0])[None],
        I["e_w_pool_2"][0].reshape(4, 2, P, 256).transpose(2, 0, 1, 3).reshape(1, P, KT, UC),
        cols(e[:, :g0]), cols(e[:, e1:]), halves(I["e_w_out_2"][0]),
        cols(o[:, :D]), cols(o[:, ki + 68:]), cols(o[:, ck:ki]),
        wide(I["o_w_uk_2"][0])[None], wide(I["o_w_uv_2"][0])[None], cols(I["o_w_out_2"][0])])
    assert len(units) == UNITS
    A["wu"] = units
    ktile = lambda w: w.reshape(KT, P, -1).transpose(1, 0, 2)
    A["w_route"] = ktile(np.concatenate([I["moe_w_group"][0], I["moe_w_router"][0]], 1))
    A["b_route"] = np.concatenate([I["moe_b_group"], I["moe_b_router"]], 1)
    A["w_if"] = ktile(e[:, g0:e1])
    A["w_ki"] = ktile(np.concatenate([o[:, ki:ki + 64], o[:, ki:ki + 68]], 1))
    A["pt"] = I["p"][0, 0].T.reshape(2, P, T).transpose(1, 0, 2)
    A["ecw"] = I["e_conv_2"][0].reshape(4, 16, P).transpose(2, 1, 0)
    feat = lambda v: v.reshape(-1, P).T
    A["feat"] = np.concatenate([feat(I["e_norm_2"][0]), feat(I["o_norm_2"][0]), feat(I["e_g_head_2"][0]),
                                feat(I["e_s_pool_2"][0]), feat(I["o_g_kv_2"][0]),
                                feat(np.tile(I["o_g_q_2"][0], 2)), feat(np.tile(I["o_g_k_2"][0], 2))], 1)
    A["wab"] = w[:, 2 * kw + 2 * VH * HD:].reshape(KT, P, 64).transpose(1, 0, 2)
    c = I["gdn_conv_w"][0]
    q, k, v = c[:, :kw], c[:, kw:2 * kw], c[:, 2 * kw:]
    cw = np.stack([q.reshape(TAPS, QKH, HD), k.reshape(TAPS, QKH, HD),
                   v.reshape(TAPS, QKH, 2, HD)[:, :, 0], v.reshape(TAPS, QKH, 2, HD)[:, :, 1]], 2)
    A["cw"] = cw.transpose(3, 1, 2, 0).reshape(P, QKH, 4 * TAPS)
    A["xt"] = I["x"][0].T.reshape(KT, P, T).transpose(1, 0, 2)
    return A


KEEP = ["x", "gdn_a_log", "gdn_dt_bias", "gdn_norm_w", "ln_g", "ln_b", "e_b_if_2", "rel_bias_2"]


def arrays_of(inputs):
    I = {k: np.asarray(v) for k, v in inputs.items()}
    A = layout(I)
    for k in KEEP:
        A[k] = I[k]
    for g, v in constants().items():
        A["c_" + g] = np.concatenate(list(v.values()), 1)
    return {k: np.ascontiguousarray(v) for k, v in A.items()}


def program(nc, shapes, per, upto=99, dbg=None):
    ins = {k: nc.dram_tensor("in_" + k, s, F32, kind="ExternalInput").ap() for k, s in shapes.items()}
    out = nc.dram_tensor("out", (1, T, D), F32, kind="ExternalOutput").ap()
    d = nc.dram_tensor("dbg", dbg, F32, kind="ExternalOutput").ap() if dbg else None
    return Build(nc, ins, out, per, upto, d).p.found


def kernel(**inputs):
    import concourse.bacc as bacc
    from concourse.bass_utils import run_bass_kernel_spmd
    A = arrays_of(inputs)
    shapes = {k: v.shape for k, v in A.items()}
    counts = {}
    for _ in range(2):
        nc = bacc.Bacc("TRN2", target_bir_lowering=False, num_devices=1)
        counts = program(nc, shapes, counts)
    r = run_bass_kernel_spmd(nc, [{"in_" + k: v for k, v in A.items()}], core_ids=[0])
    return r.results[0]["out"]
```

```python
from contextlib import contextmanager

import numpy as np

import concourse.bass as bass
from concourse import mybir

F32 = mybir.dt.float32
ALU = mybir.AluOpType
ACT = mybir.ActivationFunctionType
AX, AXY = mybir.AxisListType.X, mybir.AxisListType.XY

P = 128
T = 256
NT = T // P
D = 1024
KT = D // P
UC = 256
QKH, VH, HD = 8, 16, 128
REP = VH // QKH
TAPS = 5
EXPERTS, TOPK, HID, GROUPS = 32, 2, 256, 4
EPG = EXPERTS // GROUPS
AH, AD = 4, 256
POOL_WINDOWS = (2, 4, 8, 16)
CH, CD = 16, 64
IH, IDIM = 4, 64
CAP = 64
SEL = 64
BUCKETS, MAXDIST = 32, 128
ALPHA = 2.0 ** 0.25
BIG = 1e30
LEVELS = (1, 2, 4, 8, 16, 32, 64)
NSLOT = 6
TAKEN = -2.0 ** 126
ARENA = 27500

U_GDN = 0
U_GOUT = U_GDN + 3 * QKH
U_MOE = U_GOUT + 8
U_PE = U_MOE + 3 * EXPERTS
U_POOL = U_PE + 5
U_EIN = U_POOL + 1
U_EOUT = U_EIN + 28
U_OIN = U_EOUT + 8
U_UK = U_OIN + 10
U_OOUT = U_UK + 2
UNITS = U_OOUT + 4
F_ENORM, F_ONORM, F_HEAD, F_POOL, F_KV, F_Q, F_K = 0, 8, 16, 24, 32, 34, 35
FEATS = 36


class Point:

    def __init__(self, line, value, loop):
        self.line, self.value, self.loop = line, value, loop

    def before(self):
        return Point(self.line, self.value - self.loop.per[self.line.name], self.loop)

    def at(self):
        if self.loop is None:
            return self.value
        per = self.loop.per.get(self.line.name, 0)
        if self.loop.open:
            return self.loop.i * per + self.value if per else self.value
        return self.value + (self.loop.n - 1) * per


class Loop:
    def __init__(self, n, i, per):
        self.n, self.i, self.per, self.open = n, i, per, True


class Line:

    def __init__(self, prog, name, step=1):
        self.prog, self.name, self.step, self.count = prog, name, step, 0
        self.sem = prog.nc.alloc_semaphore(name)
        prog.lines.append(self)

    def mark(self, ins):
        ins.then_inc(self.sem, self.step)
        self.count += self.step
        return Point(self, self.count, self.prog.loop)

    def now(self):
        return Point(self, self.count, self.prog.loop)


class Prog:

    def __init__(self, nc, per):
        self.nc, self.per, self.loop, self.lines, self.found, self.seen = nc, per, None, [], {}, {}
        self.pe, self.act, self.dve, self.pool = (Line(self, n) for n in ("pe", "act", "dve", "pool"))

    def need(self, engine, *points):
        for p in points:
            if p is None:
                continue
            key = (engine.engine, p.line.name, id(p.loop))
            if self.seen.get(key, -1) >= p.value:
                continue
            self.seen[key] = p.value
            engine.wait_ge(p.line.sem, p.at())

    def barrier(self):
        for e in (self.nc.tensor, self.nc.scalar, self.nc.vector, self.nc.gpsimd):
            self.need(e, *(l.now() for l in (self.pe, self.act, self.dve, self.pool)))

    @contextmanager
    def fori(self, name, n):
        starts = self.starts = {l.name: l.count for l in self.lines}
        per = self.per.get(name, {})
        with self.nc.Fori(0, n, 1) as i:
            self.loop = Loop(n, i, per)
            self.seen = {}
            yield i
            self.loop.open = False
        self.found[name] = {l.name: l.count - starts[l.name] for l in self.lines}
        for l in self.lines:
            l.count = starts[l.name] + n * (l.count - starts[l.name])
        self.loop = None
        self.seen = {}


    @contextmanager
    def only_if(self, flag):
        nc = self.nc
        self.need(nc.sync, self.dve.now())
        value = nc.values_load(flag, min_val=0, max_val=P)
        starts = {l.name: l.count for l in self.lines}
        with nc.If(value != 0):
            yield
            for e in (nc.tensor, nc.scalar, nc.vector, nc.gpsimd, nc.sync):
                self.need(e, *(l.now() for l in self.lines if l.count != starts[l.name]))
        owner = {"pe": nc.tensor, "act": nc.scalar, "dve": nc.vector, "pool": nc.gpsimd}
        with nc.Else():
            for l in self.lines:
                if l.count != starts[l.name]:
                    owner.get(l.name, nc.sync).sem_inc(l.sem, l.count - starts[l.name])
        self.seen = {}


def constants():
    r = np.arange(P)
    i, j = r[:, None], r[None, :]
    eye = (i == j).astype(np.float32)
    upto = [i <= j, i >= j]
    behind = [i > j, i < j]
    keep = [i >= j, i <= j]

    def level(b):
        return (i // (2 * b) == j // (2 * b)) & ((i // b) % 2 == 1) & ((j // b) % 2 == 0)

    def four(fwd, bwd):
        return np.stack([fwd, fwd, bwd, bwd], 1).astype(np.float32)

    t = np.arange(T)
    late = np.stack([t[None, :] > P * n + r[:, None] for n in range(NT)], 1)
    window = []
    for w in POOL_WINDOWS:
        back = t[None, :] - t[:, None]
        window.append(((back >= 0) & (back < w)) / np.minimum(t + 1, w)[None, :] - (back == 0))
    window = np.stack(window).reshape(len(POOL_WINDOWS), NT, P, T).transpose(2, 0, 1, 3)
    dist = np.maximum(np.arange(2 * T) - (T - 1), 0)
    half = BUCKETS // 2
    far = half + (np.log(np.maximum(dist, 1).astype(np.float32) / np.float32(half))
                  / np.float32(np.log(MAXDIST / half)) * np.float32(BUCKETS - half)).astype(np.int32)
    bucket = np.where(dist < half, dist, np.minimum(far, BUCKETS - 1))
    onehot = np.zeros((P, 2 * T))
    onehot[bucket, np.arange(2 * T)] = 1
    common = {
        "ident": eye, "ones": np.ones((P, P)), "upto_all": i <= j,
        "columns": np.tile(np.array([1e-6, 1e-5, 0.5 * -np.log(HD), 1.0, -1.0, 0, 0, 0]), (P, 1)),
        "places": np.tile(np.arange(1, CAP + 1), (P, 1)),
        "rank4": np.tile(np.arange(4, 0, -1), (P, NT)), "rank8": np.tile(np.arange(8, 0, -1), (P, NT)),
    }
    delta = {
        "upto": np.stack(upto, 1), "behind": np.stack(behind, 1),
        "bars": four(~keep[0], ~keep[1]) * BIG,
        "levels_t": np.stack([four(level(b).T, level(b)) for b in LEVELS], 1),
        "level1": four(level(1), level(1).T),
        "ident4": four(eye, eye),
    }
    late = {"late": late * BIG, "onehot": onehot}
    flat = lambda g: {k: np.ascontiguousarray(v.reshape(P, -1).astype(np.float32)) for k, v in g.items()}
    return {"common": flat(common), "delta": flat(delta), "late": flat(late), "pool": flat({"window": window})}


def const_map(group):
    at, out = 0, {}
    for k, v in constants()[group].items():
        out[k] = (at, v.shape[1])
        at += v.shape[1]
    return out, at


class Build:
    def __init__(self, nc, ins, out, per, upto=99, dbg=None):
        self.nc, self.ins, self.out, self.dbg = nc, ins, out, dbg
        self.p = p = Prog(nc, per)
        self.pe, self.act, self.dve, self.pool = p.pe, p.act, p.dve, p.pool
        self.need = p.need
        for engine, line in ((nc.tensor, p.pe), (nc.scalar, p.act), (nc.vector, p.dve), (nc.gpsimd, p.pool)):
            engine.sem_inc(line.sem, 1024)
            line.count = 1024
        self.ps = nc.alloc_psum_tensor("ps", [P, 8, 512], F32)
        self.slots = nc.alloc_sbuf_tensor("slots", [P, NSLOT, KT, UC], F32)
        self.arrived = [Line(p, f"slot{s}_arrived", 16) for s in range(NSLOT)]
        self.last = {}
        self.spill = nc.alloc_sbuf_tensor("spill", [P, 1], mybir.dt.int32)
        self.spilled = Line(p, "spilled_weights_arrived", 16)
        self.small = Line(p, "small_arrived", 16)
        self.scratch_done = Line(p, "bias_rows_stored", 16)
        self.stored = Line(p, "output_stored", 16)
        self.bias_rows = nc.dram_tensor("bias_rows", (CH, 2 * T), F32, kind="Internal").ap()
        self.x = nc.alloc_sbuf_tensor("x", [P, NT, D], F32)
        self.xt = nc.alloc_sbuf_tensor("xt", [P, KT, T], F32)
        self.yt = nc.alloc_sbuf_tensor("yt", [P, 16, T], F32)
        cm, n = const_map("common")
        self.cst = nc.alloc_sbuf_tensor("cst", [P, n], F32)
        self.c = {k: self.cst[:, a:a + m] for k, (a, m) in cm.items()}
        self.arena = nc.alloc_sbuf_tensor("arena", [P, ARENA], F32)
        self.top = 0
        self.stages(upto)

    def alloc(self, name, shape):
        n = int(np.prod(shape[1:]))
        v = self.arena[:shape[0], self.top:self.top + n]
        self.top += n
        assert self.top <= ARENA, (name, self.top)
        if len(shape) > 2:
            names = "abcd"[:len(shape) - 1]
            v = v.rearrange(f"p ({' '.join(names)}) -> p {' '.join(names)}",
                            **{k: m for k, m in zip(names, shape[1:])})
        return v

    def fresh(self):
        self.p.barrier()
        self.top = 0

    def consts(self, group, at=None):
        cm, n = const_map(group)
        v = self.alloc(group, [P, n]) if at is None else at[:, 0:n]
        self.load(v, self.ins["c_" + group])
        self.c.update({k: v[:, a:a + m] for k, (a, m) in cm.items()})

    def load(self, dst, src, queue=None):
        return self.small.mark((queue or self.nc.scalar).dma_start(dst, src))

    def bank(self, b, n=512, at=0):
        return self.ps[:, b, at:at + n]

    def refill(self, slot, unit, point):
        self.need(self.nc.sync, point)
        return self.arrived[slot].mark(self.nc.sync.dma_start(self.slots[:, slot], self.ins["wu"][unit]))

    def stages(self, upto):
        I = self.ins
        self.load(self.cst[:, :], I["c_common"])
        self.load(self.xt[:, :, :], I["xt"])
        for s in range(3):
            self.refill(s, U_GDN + s, None)
        self.refill(3, U_GOUT + 3, None)
        self.load(self.x[:, :, :], I["x"].rearrange("a (n p) d -> p (a n) d", p=P))
        self.gdn()
        if upto <= 1:
            return self.finish_debug(self.yt)
        self.moe()
        if upto <= 2:
            return self.finish_debug(self.x)
        self.embed()
        if upto <= 3:
            return self.finish_debug(self.x)
        self.even()
        if upto <= 4:
            return self.finish_debug(self.x)
        self.odd()
        if self.dbg is not None:
            self.finish_debug(self.x)

    def gdn(self):
        nc, I, p, need, c = self.nc, self.ins, self.p, self.need, self.c
        pe, act, dve, pool = self.pe, self.act, self.dve, self.pool
        A, V, G, M = nc.scalar, nc.vector, nc.gpsimd, nc.tensor
        al = self.alloc
        self.consts("delta")
        wab = al("wab", [P, KT, 64])
        alog = al("alog", [P, 32])
        dtb = al("dtb", [P, 32])
        cw = al("cw", [P, QKH, 4 * TAPS])
        nw = al("gdn_nw", [P, 1])
        self.load(wab[:, :, :], I["wab"])
        self.load(alog[:, :], I["gdn_a_log"].rearrange("a d h -> a (d h)").to_broadcast([P, 32]))
        self.load(dtb[:, :], I["gdn_dt_bias"].rearrange("a d h -> a (d h)").to_broadcast([P, 32]))
        self.load(cw[:, :, :], I["cw"])
        ready = self.load(nw[:, :], I["gdn_norm_w"].rearrange("a (p b) -> (a p) b", b=1))

        need(M, ready)
        for t in range(NT):
            for k in range(KT):
                q = M.matmul(self.bank(2, 64, 64 * t), self.xt[:, k, t * P:(t + 1) * P], wab[:, k, :],
                             start=(k == 0), stop=(k == KT - 1), skip_group_check=True)
        q = pe.mark(q)
        ab = self.bank(2, 128).rearrange("p (t z n) -> p t z n", t=NT, z=2)
        GC, BE, BG, GS = range(4)
        gate = al("gate", [P, 4, 2 * NT, VH])
        g = al("g", [P, NT, 2 * VH])
        s1 = al("gate_s1", [P, NT, 2 * VH])
        s2 = al("gate_s2", [P, NT, 2 * VH])
        byt = lambda z: gate[:, z].rearrange("p (d t) n -> p t d n", d=2)
        need(V, q, ready)
        a = dve.mark(V.tensor_tensor(s1[:, :, :], ab[:, :, 0, :],
                                     dtb[:, :].unsqueeze(1).to_broadcast([P, NT, 32]), ALU.add))
        need(V, a)
        b = dve.mark(V.scalar_tensor_tensor(s2[:, :, :], s1[:, :, :], -1.0, s1[:, :, :], ALU.mult, ALU.max))
        need(A, b)
        b = act.mark(A.activation(s2[:, :, :], s2[:, :, :], ACT.Exp, scale=-1.0))
        need(A, ready)
        e = act.mark(A.activation(alog[:, :], alog[:, :], ACT.Exp))
        need(A, q)
        eb = act.mark(A.activation(byt(BE), ab[:, :, 1, :].rearrange("p t (d n) -> p t d n", d=2),
                                   ACT.Exp, scale=-1.0))
        need(A, b)
        b = act.mark(A.activation(s2[:, :, :], s2[:, :, :], ACT.Ln, bias=1.0))
        need(V, b, e, eb)
        b = dve.mark(V.scalar_tensor_tensor(s1[:, :, :], s1[:, :, :], 0.0, s2[:, :, :], ALU.max, ALU.add))
        need(V, b)
        b = dve.mark(V.scalar_tensor_tensor(g[:, :, :], s1[:, :, :], -1.0,
                                            alog[:, :].unsqueeze(1).to_broadcast([P, NT, 32]),
                                            ALU.mult, ALU.mult))
        e = dve.mark(V.tensor_scalar(gate[:, BE], gate[:, BE], 1.0, None, ALU.add))
        need(V, e)
        be = dve.mark(V.reciprocal(gate[:, BE], gate[:, BE]))
        need(M, be)
        up = c["upto"].rearrange("p (d i) -> p d i", d=2)
        bh = c["behind"].rearrange("p (d i) -> p d i", d=2)
        for t in range(NT):
            for d in range(2):
                o = 32 * d + 16 * t
                M.matmul(self.bank(3, 16, o), up[:, d], g[:, t, 16 * d:16 * d + 16],
                         start=True, stop=True, skip_group_check=True)
                q = M.matmul(self.bank(4, 16, o), bh[:, d], g[:, t, 16 * d:16 * d + 16],
                             start=True, stop=True, skip_group_check=True)
        q = pe.mark(q)
        need(A, q)
        sums = self.bank(3, 64).rearrange("p (m n) -> p m n", m=4)
        eg = s2[:, :, :].rearrange("p t (d n) -> p (t d) n", d=2)
        act.mark(A.activation(gate[:, GC], sums, ACT.Copy))
        act.mark(A.activation(gate[:, GS], self.bank(4, 64).rearrange("p (m n) -> p m n", m=4), ACT.Exp))
        e = act.mark(A.activation(eg, sums, ACT.Exp))
        need(V, e)
        dve.mark(V.tensor_tensor(gate[:, BG], gate[:, BE], eg, ALU.mult))

        NI = 4
        sl = (slice(0, 4, 3), slice(1, 3))
        tile_of = lambda s, n: s if n < 2 else 1 - s
        mats = [P, 2, NI, P]
        raw = al("raw", [P, 4, T + TAPS - 1])
        cn = al("cn", [P, 4, T])
        cv = al("cv", [P, 4, T])
        zr = al("zr", [P, REP, T])
        sq, rn, rn2, f1 = (al(n, [P, 2, T]) for n in ("sq", "rn", "rn2", "f1"))
        cwh = al("cwh", [P, 4 * TAPS])
        sc = al("sc", [P, 4, 2 * NT, REP])
        gb, dm, am, an = (al(n, mats) for n in ("gb", "dm", "am", "an"))
        at, att, mt, X, XT = (al(n, mats) for n in ("at", "att", "mt", "X", "XT"))
        vn = al("vn", mats)
        er, qd, kdec, S = (al(n, [P, NI, P]) for n in ("er", "qd", "kdec", "S"))
        ktm = al("ktm", [P, NT, P])
        vtm = al("vtm", [P, NT, REP, P])
        Y, vb, kbe, nwt = gb, dm, am[:, 0], an[:, 0]
        need(A, dve.mark(V.memset(raw[:, :, :], 0.0)))
        bars = c["bars"].rearrange("p (n j) -> p n j", n=NI)
        lvt = c["levels_t"].rearrange("p (l n j) -> p l n j", l=len(LEVELS), n=NI)
        l1 = c["level1"].rearrange("p (n j) -> p n j", n=NI)
        id4 = c["ident4"].rearrange("p (n j) -> p n j", n=NI)
        ident = c["ident"]
        four = lambda b: self.bank(b).rearrange("p (n j) -> p n j", n=NI)
        two = lambda b: self.bank(b).rearrange("p (n t) -> p n t", n=2)
        col = self.col

        class Next:
            raw_done = {}

            def __init__(nx, h, note):
                nx.h, nx.note, nx.ops, nx.copied = h, note, [], []
                nx.behind = note

            def group(nx, j):
                s, n = j // 2, j % 2
                if j >= 2:
                    need(M, nx.copied[j - 2])
                elif nx.note:
                    need(M, self.behind("delta", f"bank{j}"))
                if n == 0:
                    need(M, self.arrived[s].now())
                for k in range(KT):
                    q = M.matmul(self.bank(n, T), self.slots[:, s, k, n * P:(n + 1) * P], self.xt[:, k, :],
                                 start=(k == 0), stop=(k == KT - 1), skip_group_check=True)
                q = pe.mark(q)
                if n == 1:
                    self.refill(s, nx.h * 3 + (U_GDN + 3 + s), q)
                need(A, q)
                dst = raw[:, j, 2:2 + T] if j < 4 else zr[:, n]
                nx.copied.append(act.mark(A.activation(dst, self.bank(n, T), ACT.Copy)))

            def taps(nx):
                nx.t1 = dve.mark(V.tensor_copy(
                    cwh[:, :], cw[:, bass.ds(nx.h, 1), :].rearrange("p a b -> p (a b)")
                    if not isinstance(nx.h, int) else cw[:, nx.h, :]))
                need(V, nx.t1)

            def conv(nx, tap, pair):
                if tap == 0:
                    need(V, nx.copied[2 * pair], nx.copied[2 * pair + 1])
                for s in (2 * pair, 2 * pair + 1):
                    src, w = raw[:, s, tap:tap + T], cwh[:, s * TAPS + tap:s * TAPS + tap + 1]
                    if tap == 0:
                        q = dve.mark(V.tensor_scalar(cn[:, s], src, w, None, ALU.mult))
                    else:
                        need(V, nx.last[s])
                        q = dve.mark(V.scalar_tensor_tensor(cn[:, s], src, w, cn[:, s], ALU.mult, ALU.add))
                    nx.last[s] = q

            last = {}

            def silu_z(nx):
                need(A, nx.copied[5])
                dst = self.yt[:, bass.ds(nx.h * 2, 2), :] if not isinstance(nx.h, int) else \
                    self.yt[:, 2 * nx.h:2 * nx.h + 2, :]
                act.mark(A.activation(dst, zr[:, :, :], ACT.Silu))

            def silu(nx):
                need(A, nx.last[1], nx.last[3])
                qk = act.mark(A.activation(cn[:, 0:2], cn[:, 0:2], ACT.Silu))
                v = act.mark(A.activation(cv[:, 2:4], cn[:, 2:4], ACT.Silu))
                need(V, qk)
                nx.squared = dve.mark(V.tensor_tensor(sq[:, :, :], cn[:, 0:2], cn[:, 0:2], ALU.mult))
                if nx.note:
                    self.note("delta", "cv_v", v)

            def unit(nx):
                need(M, nx.squared, nx.copied[4])
                q = pe.mark(M.matmul(self.bank(0), c["ones"], sq[:, :, :], start=True, stop=True))
                need(A, q)
                q = act.mark(A.activation(rn[:, :, :], two(0), ACT.Ln, bias=col(0)))
                if nx.note:
                    self.note("delta", "bank0", q)
                need(A, q)
                act.mark(A.activation(rn[:, 0], rn[:, 0], ACT.Exp, scale=-0.5, bias=col(2)))
                nx.norms = act.mark(A.activation(rn[:, 1], rn[:, 1], ACT.Exp, scale=-0.5))

            def apply_unit(nx):
                need(V, nx.norms)
                q = dve.mark(V.tensor_tensor(cv[:, 0:2], cn[:, 0:2], rn[:, :, :], ALU.mult))
                if nx.note:
                    self.note("delta", "cv_qk", q)

            def scalars(nx):
                ds = (lambda n: bass.ds(nx.h * n, n)) if not isinstance(nx.h, int) else \
                    (lambda n: slice(nx.h * n, nx.h * n + n))
                for s in range(2):
                    nx.spread = dve.mark(V.tensor_copy(
                        gb[:, s].rearrange("p (d v) j -> p d v j", d=2),
                        gate[:, GC, sl[s], ds(2)].unsqueeze(3).to_broadcast([P, 2, REP, P])))
                for z in range(4):
                    nx.scalar = dve.mark(V.tensor_copy(sc[:, z], gate[:, z, :, ds(2)]))

            def decay_rows(nx):
                need(M, nx.spread)
                for s in range(2):
                    for n in range(NI):
                        q = M.transpose(self.bank(2 + s, P, n * P), gb[:, s, n], ident)
                nx.rows = pe.mark(q)

            def decay(nx):
                need(V, nx.rows)
                need(A, nx.rows, nx.scalar)
                ex = act.mark(A.activation(er[:, :, :], four(3), ACT.Exp))
                need(V, ex)
                t1 = [dve.mark(V.tensor_tensor(dm[:, s], four(2 + s), bars, ALU.add)) for s in range(2)]
                for s in range(2):
                    need(A, t1[s])
                    for n in range(NI):
                        t2 = act.mark(A.activation(dm[:, s, n], dm[:, s, n], ACT.Exp, scale=-1.0,
                                                   bias=sc[:, GC, 2 * (n // 2) + tile_of(s, n), n % 2:n % 2 + 1]))
                    if nx.note:
                        self.note("delta", f"decay{s}", t2)

        def head(i, nx):
            later = lambda name: self.behind("delta", name)
            need(A, later("act"))
            need(V, later("dve"), later("scanned"))
            need(G, later("pool"), later("scanned"))
            G_ = (lambda j: nx.group(j)) if nx else (lambda j: None)
            need(M, later("cv_v"), later("cv_qk"))
            for t in range(NT):
                ts = slice(t * P, (t + 1) * P)
                M.transpose(self.bank(4, P, t * P), cv[:, 1, ts], ident)
                for v in range(REP):
                    M.transpose(self.bank(5, P, (t * 2 + v) * P), cv[:, 2 + v, ts], ident)
                M.matmul(self.bank(7, P, t * P), cv[:, 1, ts], cv[:, 1, ts], start=True, stop=True,
                         skip_group_check=True)
                q = M.matmul(self.bank(7, P, (2 + t) * P), cv[:, 0, ts], cv[:, 1, ts], start=True,
                             stop=True, skip_group_check=True)
            kq = pe.mark(q)
            need(A, kq)
            act.mark(A.activation(ktm[:, :, :], self.bank(4, 2 * P).rearrange("p (t j) -> p t j", t=2), ACT.Copy))
            tm = act.mark(A.activation(vtm[:, :, :, :].rearrange("p t v j -> p (t v) j"), four(5), ACT.Copy))
            G_(0)
            a1, a2, xq = [], [], []
            for s in range(2):
                need(V, kq, later(f"decay{s}"))
                for n in range(NI):
                    t = tile_of(s, n)
                    q = dve.mark(V.scalar_tensor_tensor(
                        am[:, s, n], self.bank(7, P, t * P), sc[:, BE, 2 * (n // 2) + t, n % 2:n % 2 + 1],
                        dm[:, s, n], ALU.mult, ALU.mult))
                a1.append(q)
            for s in range(2):
                need(V, a1[s])
                xq.append(dve.mark(V.tensor_tensor(X[:, s], am[:, s], l1, ALU.mult)))
            for s in range(2):
                need(V, xq[s])
                xq[s] = dve.mark(V.tensor_tensor(X[:, s], id4, X[:, s], ALU.subtract))
            for s in range(2):
                qkp = self.bank(7, 2 * P, 2 * P).rearrange("p (t j) -> p t j", t=2)
                qkp = qkp if s == 0 else qkp[:, ::-1]
                a2.append(dve.mark(V.tensor_tensor(
                    an[:, s].rearrange("p (d v) j -> p d v j", d=2), qkp.unsqueeze(2).to_broadcast([P, 2, REP, P]),
                    dm[:, s].rearrange("p (d v) j -> p d v j", d=2), ALU.mult)))
            def turned(src, b, ready, dst):
                need(M, ready)
                for n in range(NI):
                    q = M.transpose(self.bank(b, P, n * P), src[:, n], ident)
                q = pe.mark(q)
                need(A, q)
                return act.mark(A.activation(dst, four(b), ACT.Copy))

            atq = [turned(am[:, s], 2 + s, a1[s], at[:, s]) for s in range(2)]
            G_(1)
            need(M, tm)
            xtq = [turned(X[:, s], 4 + s, xq[s], XT[:, s]) for s in range(2)]
            need(M, *atq)
            attq = [turned(an[:, s], 2 + s, a2[s], att[:, s]) for s in range(2)]
            if nx:
                nx.taps()
            mq = [None, None]
            for s in range(2):
                need(G, atq[s])
                mq[s] = pool.mark(G.tensor_tensor(mt[:, s], at[:, s], lvt[:, 1], ALU.mult))
            scaled = {}

            def scale_rows():
                need(G, tm, a2[1])
                bc = lambda z, s: sc[:, z, sl[s], :].unsqueeze(3).to_broadcast([P, 2, REP, P])
                kt = lambda s: (ktm[:, :, :] if s == 0 else ktm[:, ::-1, :]).unsqueeze(2).to_broadcast([P, 2, REP, P])
                dv = lambda x: x.rearrange("p (d v) j -> p d v j", d=2)
                for s in range(2):
                    for d in range(2):
                        t = tile_of(s, 2 * d)
                        pool.mark(G.tensor_tensor(vb[:, s, 2 * d:2 * d + 2], vtm[:, t],
                                                  sc[:, BE, 2 * d + t, :].unsqueeze(2).to_broadcast([P, REP, P]),
                                                  ALU.mult))
                for d in range(2):
                    for dst, z, s in ((kdec, GS, 0), (kbe, BG, 1)):
                        t = tile_of(s, 2 * d)
                        q = pool.mark(G.tensor_tensor(dst[:, 2 * d:2 * d + 2],
                                                      ktm[:, t].unsqueeze(1).to_broadcast([P, REP, P]),
                                                      sc[:, z, 2 * d + t, :].unsqueeze(2).to_broadcast([P, REP, P]),
                                                      ALU.mult))
                scaled["q"] = q

            ops = []
            if nx:
                ops = [(0, 0), (1, 0), (2, 0), (3, 0), (4, 0), (0, 1), (1, 1), (2, 1), (3, 1), (4, 1)]
            for l in range(1, len(LEVELS)):
                lastl = l == len(LEVELS) - 1
                yq, zq = [], []
                for s in range(2):
                    if l > 1:
                        need(M, attq[s])
                        xtq[s] = turned(X[:, s], 2 + s, xq[s], XT[:, s])
                    need(M, mq[s], xq[s])
                    if l == 1:
                        need(M, xtq[s])
                    for n in range(NI):
                        q = M.matmul(self.bank(4 + s, P, n * P), mt[:, s, n], X[:, s, n], start=True,
                                     stop=True, skip_group_check=True)
                    q = pe.mark(q)
                    if not lastl:
                        need(G, q)
                        mq[s] = pool.mark(G.tensor_tensor(mt[:, s], at[:, s], lvt[:, l + 1], ALU.mult))
                    need(A, q)
                    yq.append(act.mark(A.activation(Y[:, s], four(4 + s), ACT.Copy)))
                if l in (1, 2, 3, 5):
                    G_(min(1 + l, 5))
                if l == 1:
                    scale_rows()
                if l == 5 and nx:
                    nx.silu_z()
                for s in range(2):
                    need(M, yq[s], xtq[s])
                    if l == 1:
                        need(M, later("rms"))
                    for n in range(NI):
                        if lastl:
                            q = M.matmul(self.bank(6 + s, P, n * P), Y[:, s, n], XT[:, s, n], start=True,
                                         stop=True, skip_group_check=True)
                        else:
                            q = M.matmul(self.bank(6 + s, P, n * P), XT[:, s, n], Y[:, s, n], start=True,
                                         stop=True, skip_group_check=True)
                    zq.append(pe.mark(q))
                for s in range(2):
                    need(V, zq[s])
                    dst = XT if lastl else X
                    xq[s] = dve.mark(V.tensor_tensor(dst[:, s], dst[:, s], four(6 + s), ALU.subtract))
                if lastl:
                    break
                if l == 1:
                    qsrc = cv[:, 0].rearrange("p (t j) -> p t j", t=2)[:, ::-1]
                    qdq = dve.mark(V.tensor_tensor(
                        qd[:, :, :].rearrange("p (d v) j -> p d v j", d=2),
                        er[:, :, :].rearrange("p (d v) j -> p d v j", d=2),
                        qsrc.unsqueeze(2).to_broadcast([P, 2, REP, P]), ALU.mult))
                if l >= 2:
                    for _ in range(4):
                        if ops:
                            nx.conv(*ops.pop(0))
                if l == 4 and nx:
                    nx.silu()
            need(M, xq[0], scaled["q"])
            for n in range(NI):
                q = M.matmul(self.bank(4, P, n * P), XT[:, 0, n], vb[:, 0, n], start=True, stop=True,
                             skip_group_check=True)
            vq0 = pe.mark(q)
            need(M, xq[1])
            for n in range(NI):
                q = M.matmul(self.bank(2, P, n * P), kbe[:, n], XT[:, 1, n], start=True, stop=True,
                             skip_group_check=True)
            wq = pe.mark(q)
            need(A, vq0)
            v0 = act.mark(A.activation(vn[:, 0], four(4), ACT.Copy))
            need(A, wq)
            w1 = act.mark(A.activation(nwt, four(2), ACT.Copy, scale=-1.0))
            if nx:
                nx.unit()
            need(M, v0)
            for n in range(NI):
                q = M.matmul(self.bank(3, P, n * P), kdec[:, n], vn[:, 0, n], start=True, stop=True,
                             skip_group_check=True)
            sp = pe.mark(q)
            need(V, sp)
            sq_ = dve.mark(V.tensor_copy(S[:, :, :], four(3)))
            if nx:
                need(V, *zq)
                nx.scalars()
                nx.apply_unit()
            out = lambda s, n: self.bank(6, P, (n % 2) * T + tile_of(s, n) * P)
            for n in range(NI):
                M.matmul(out(0, n), vn[:, 0, n], att[:, 0, n], start=(n == 0), stop=False, skip_group_check=True)
            need(M, w1, sq_, qdq)
            for n in range(NI):
                M.matmul(self.bank(5, P, n * P), XT[:, 1, n], vb[:, 1, n], start=True, stop=False,
                         skip_group_check=True)
                q = M.matmul(self.bank(5, P, n * P), nwt[:, n], S[:, n], start=False, stop=True,
                             skip_group_check=True)
            vq1 = pe.mark(q)
            need(A, vq1)
            v1 = act.mark(A.activation(vn[:, 1], four(5), ACT.Copy))
            if nx:
                nx.decay_rows()
            for n in range(NI):
                M.matmul(out(1, n), S[:, n], qd[:, n], start=False, stop=False, skip_group_check=True)
            need(M, v1)
            for n in range(NI):
                q = M.matmul(out(1, n), vn[:, 1, n], att[:, 1, n], start=False, stop=True, skip_group_check=True)
            op = pe.mark(q)
            need(A, op)
            q = act.mark(A.activation(f1[:, :, :], two(6), ACT.Square))
            rms = act.mark(A.activation(sq[:, :, :], two(6), ACT.Copy, scale=nw[:, 0:1]))
            need(M, q)
            q = pe.mark(M.matmul(self.bank(1), c["ones"], f1[:, :, :], start=True, stop=True))
            if nx:
                need(A, qdq)
                nx.decay()
            need(A, q)
            ln = act.mark(A.activation(rn2[:, :, :], two(1), ACT.Ln, scale=1.0 / HD, bias=col(0)))
            need(A, ln)
            aq = act.mark(A.activation(rn2[:, :, :], rn2[:, :, :], ACT.Exp, scale=-0.5))
            need(G, aq)
            q = pool.mark(G.tensor_tensor(rn2[:, :, :], rn2[:, :, :], sq[:, :, :], ALU.mult))
            need(G, q)
            y = self.yt[:, bass.ds(i * 2, 2), :] if not isinstance(i, int) else self.yt[:, 2 * i:2 * i + 2, :]
            q = pool.mark(G.tensor_tensor(y, rn2[:, :, :], y, ALU.mult))
            if nx:
                for name, point in (("bank1", ln), ("rms", rms), ("act", aq), ("dve", dve.now()), ("pool", q),
                                    ("scanned", op)):
                    self.note("delta", name, point)

        first = Next(0, False)
        for j in range(6):
            first.group(j)
        need(V, dve.now())
        first.taps()
        for pair in range(2):
            for tap in range(TAPS):
                first.conv(tap, pair)
        first.silu()
        first.silu_z()
        first.unit()
        first.apply_unit()
        first.scalars()
        first.decay_rows()
        first.decay()
        p.barrier()
        with p.fori("delta", QKH - 1) as i:
            head(i, Next(i + 1, True))
        head(QKH - 1, None)

    def col(self, k):
        return self.c["columns"][:, k:k + 1]

    def project(self, name, first, units, halves, lhs, evac, skip=0):
        M, pe = self.nc.tensor, self.pe
        groups = 4 // halves
        free = {}

        def body(i):
            for cg in range(groups):
                if free.get(cg) is not None:
                    self.need(M, free[cg])
                for h in range(halves):
                    s = cg * halves + h
                    self.need(M, self.arrived[s].now())
                    for t in range(NT):
                        for k in range(KT):
                            q = M.matmul(self.bank(cg, UC, t * UC), lhs[:, h * KT + k, t * P:(t + 1) * P],
                                         self.slots[:, s, k, :], start=(t == 0 and k == 0 and h == 0),
                                         stop=(k == KT - 1 and h == halves - 1), skip_group_check=True)
                    q = pe.mark(q)
                    if first + 4 + skip < UNITS:
                        self.refill(s, i * 4 + (first + 4 + skip + s), q)
                free[cg] = evac(i * groups + cg, cg, q)

        n = units // 4
        if n == 1:
            body(0)
            return
        with self.p.fori(name, n) as i:
            for cg in range(groups):
                free[cg] = self.behind(name, f"bank{cg}")
            body(i)
            for cg in range(groups):
                self.note(name, f"bank{cg}", free[cg])

    def norm_rows(self, src, sq, width, eps, st, center=False):
        A, V, act, dve = self.nc.scalar, self.nc.vector, self.act, self.dve
        for t in range(NT):
            if center:
                q = dve.mark(V.reduce_sum(st[:, 2 + t:3 + t], src[:, t], AX))
                self.need(V, q)
                q = dve.mark(V.tensor_scalar(st[:, 2 + t:3 + t], st[:, 2 + t:3 + t], 1.0 / width, None, ALU.mult))
                self.need(V, q)
                q = dve.mark(V.tensor_scalar(src[:, t], src[:, t], st[:, 2 + t:3 + t], None, ALU.subtract))
                self.need(A, q)
            q = act.mark(A.activation(sq[:, t], src[:, t], ACT.Square, accum_out=st[:, t:t + 1]))
        self.need(A, q)
        q = act.mark(A.activation(st[:, 0:NT], st[:, 0:NT], ACT.Ln, scale=1.0 / width, bias=self.col(eps)))
        self.need(A, q)
        return act.mark(A.activation(st[:, 0:NT], st[:, 0:NT], ACT.Exp, scale=-0.5))

    def turn(self, src, dst, ktiles, ready, banks, scale=None):
        M, A = self.nc.tensor, self.nc.scalar
        free = [None] * len(banks)
        self.need(M, *ready)
        for g in range(ktiles // 2):
            b = g % len(banks)
            self.need(M, free[b])
            for k in range(2):
                for t in range(NT):
                    q = M.transpose(self.bank(banks[b], P, (2 * k + t) * P),
                                    src[:, t, (2 * g + k) * P:(2 * g + k + 1) * P], self.c["ident"])
            q = self.pe.mark(q)
            self.need(A, q)
            if scale is None:
                free[b] = self.act.mark(A.activation(
                    dst[:, 2 * g:2 * g + 2, :], self.bank(banks[b]).rearrange("p (k t) -> p k t", k=2), ACT.Copy))
            else:
                for k in range(2):
                    free[b] = self.act.mark(A.activation(
                        dst[:, 2 * g + k, :], self.bank(banks[b], T, k * T), ACT.Copy, scale=scale(2 * g + k)))
        return free[b]

    def layer_norm(self, row, st, sq, gb):
        V, dve = self.nc.vector, self.dve
        q = self.norm_rows(self.x, sq, D, 1, st, center=True)
        self.need(V, q, gb[1])
        for t in range(NT):
            q = dve.mark(V.scalar_tensor_tensor(self.x[:, t], self.x[:, t], st[:, t:t + 1], gb[0][:, row],
                                                ALU.mult, ALU.mult))
            self.need(V, q)
            q = dve.mark(V.tensor_tensor(self.x[:, t], self.x[:, t], gb[0][:, 2 + row], ALU.add))
        return q

    def moe(self):
        nc, I, p, need, c = self.nc, self.ins, self.p, self.need, self.c
        pe, act, dve, pool = self.pe, self.act, self.dve, self.pool
        A, V, M = nc.scalar, nc.vector, nc.tensor
        self.fresh()
        al = self.alloc
        rows = al("rows", [P, 4, D])
        wr = al("w_route", [P, KT, GROUPS + EXPERTS])
        br = al("b_route", [P, GROUPS + EXPERTS])
        st = al("st", [P, 4])
        sq = al("sq", [P, NT, D])
        self.load(wr[:, :, :], I["w_route"])
        self.load(br[:, :], I["b_route"].to_broadcast([P, GROUPS + EXPERTS]))
        self.load(rows[:, 0:2], I["ln_g"][0].unsqueeze(0).to_broadcast([P, 2, D]))
        loaded = self.load(rows[:, 2:4], I["ln_b"][0].unsqueeze(0).to_broadcast([P, 2, D]))
        for s in (4, 5):
            self.refill(s, U_MOE + s, None)

        def add(cg, b, q):
            need(V, q)
            cols = bass.ds(cg * UC, UC)
            return dve.mark(V.scalar_tensor_tensor(
                self.x[:, :, cols], self.x[:, :, cols], ALPHA, self.bank(b).rearrange("p (t n) -> p t n", t=NT),
                ALU.mult, ALU.add))

        self.project("delta_out", U_GOUT, 8, 2, self.yt, add)
        need(V, dve.now())
        q = self.layer_norm(0, st, sq, (rows, loaded))
        q = self.turn(self.x, self.xt, KT, [q], [0, 1])

        NG = GROUPS + EXPERTS
        lg = al("lg", [P, NT, NG])
        comb = al("comb", [P, NT, GROUPS, EPG])
        sel = al("sel", [P, NT, GROUPS, EPG])
        m = al("m", [P, NT, 8])
        g1 = al("g1", [P, NT, GROUPS])
        e1, e2, o1, o2 = (al(n, [P, NT, EPG]) for n in ("e1", "e2", "o1", "o2"))
        need(M, q, loaded)
        for t in range(NT):
            for k in range(KT):
                q = M.matmul(self.bank(2, NG, t * NG), self.xt[:, k, t * P:(t + 1) * P], wr[:, k, :],
                             start=(k == 0), stop=(k == KT - 1), skip_group_check=True)
        q = pe.mark(q)
        need(V, q)

        def v(ins):
            need(V, dve.mark(ins))

        def first_of(o, x, mx, rank, n):
            v(V.tensor_tensor(o, x, mx.to_broadcast([P, NT, n]), ALU.is_equal))
            v(V.tensor_tensor(o, o, rank, ALU.mult))
            v(V.tensor_reduce(m[:, :, 7], o, AX, ALU.max))
            v(V.tensor_tensor(o, o, m[:, :, 7].unsqueeze(2).to_broadcast([P, NT, n]), ALU.is_equal))

        r4 = c["rank4"].rearrange("p (t n) -> p t n", t=NT)
        r8 = c["rank8"].rearrange("p (t n) -> p t n", t=NT)
        gl = lg[:, :, 0:GROUPS]
        v(V.tensor_tensor(lg[:, :, :], self.bank(2, NT * NG).rearrange("p (t n) -> p t n", t=NT),
                          br[:, :].unsqueeze(1).to_broadcast([P, NT, NG]), ALU.add))
        v(V.tensor_reduce(m[:, :, 0], gl, AX, ALU.max))
        v(V.tensor_tensor(e1[:, :, 0:GROUPS], gl, m[:, :, 0].unsqueeze(2).to_broadcast([P, NT, GROUPS]), ALU.subtract))
        q = dve.now()
        need(A, q)
        ex = act.mark(A.activation(e1[:, :, 0:GROUPS], e1[:, :, 0:GROUPS], ACT.Exp))
        first_of(g1[:, :, :], gl, m[:, :, 0].unsqueeze(2), r4, GROUPS)
        need(V, ex)
        v(V.tensor_reduce(m[:, :, 1], e1[:, :, 0:GROUPS], AX, ALU.add))
        v(V.reciprocal(m[:, :, 1], m[:, :, 1]))
        v(V.memset(e1[:, :, :], 0.0))
        el = lg[:, :, GROUPS:].rearrange("p t (g e) -> p t g e", g=GROUPS)
        for g in range(GROUPS):
            v(V.tensor_tensor(e2[:, :, :], el[:, :, g], g1[:, :, g:g + 1].to_broadcast([P, NT, EPG]), ALU.mult))
            v(V.tensor_tensor(e1[:, :, :], e1[:, :, :], e2[:, :, :], ALU.add))
        v(V.tensor_reduce(m[:, :, 2], e1[:, :, :], AX, ALU.max))
        first_of(o1[:, :, :], e1[:, :, :], m[:, :, 2].unsqueeze(2), r8, EPG)
        v(V.scalar_tensor_tensor(e2[:, :, :], o1[:, :, :], -BIG, e1[:, :, :], ALU.mult, ALU.add))
        v(V.tensor_reduce(m[:, :, 3], e2[:, :, :], AX, ALU.max))
        first_of(o2[:, :, :], e2[:, :, :], m[:, :, 3].unsqueeze(2), r8, EPG)
        v(V.tensor_tensor(m[:, :, 4], m[:, :, 3], m[:, :, 2], ALU.subtract))
        need(A, dve.now())
        ex = act.mark(A.activation(m[:, :, 4], m[:, :, 4], ACT.Exp))
        need(V, ex)
        v(V.tensor_scalar(m[:, :, 5], m[:, :, 4], 1.0, None, ALU.add))
        v(V.reciprocal(m[:, :, 5], m[:, :, 5]))
        v(V.tensor_tensor(m[:, :, 5], m[:, :, 5], m[:, :, 1], ALU.mult))
        v(V.tensor_tensor(m[:, :, 6], m[:, :, 5], m[:, :, 4], ALU.mult))
        for g in range(GROUPS):
            v(V.tensor_tensor(sel[:, :, g], o1[:, :, :], g1[:, :, g:g + 1].to_broadcast([P, NT, EPG]), ALU.mult))
            v(V.tensor_tensor(e2[:, :, :], o2[:, :, :], g1[:, :, g:g + 1].to_broadcast([P, NT, EPG]), ALU.mult))
            v(V.tensor_tensor(sel[:, :, g], sel[:, :, g], e2[:, :, :], ALU.add))
        need(M, dve.now())
        selv = sel[:, :, :, :].rearrange("p t g e -> p t (g e)")
        M.matmul(self.bank(3, EXPERTS), c["upto_all"], selv[:, 0], start=True, stop=True, skip_group_check=True)
        M.matmul(self.bank(3, EXPERTS, EXPERTS), c["ones"], selv[:, 0], start=True, stop=False, skip_group_check=True)
        counted = pe.mark(M.matmul(self.bank(3, EXPERTS, EXPERTS), c["upto_all"], selv[:, 1], start=False, stop=True,
                                   skip_group_check=True))
        v(V.tensor_tensor(o1[:, :, :], o1[:, :, :], m[:, :, 5].unsqueeze(2).to_broadcast([P, NT, EPG]), ALU.mult))
        v(V.tensor_tensor(o2[:, :, :], o2[:, :, :], m[:, :, 6].unsqueeze(2).to_broadcast([P, NT, EPG]), ALU.mult))
        v(V.tensor_tensor(o1[:, :, :], o1[:, :, :], o2[:, :, :], ALU.add))
        for g in range(GROUPS):
            v(V.tensor_tensor(comb[:, :, g], o1[:, :, :], g1[:, :, g:g + 1].to_broadcast([P, NT, EPG]), ALU.mult))

        FT = HID // P
        combv = comb[:, :, :, :].rearrange("p t g e -> p t (g e)")
        place = al("place", [P, NT, EXPERTS + 2])
        rest = al("rest", [P, NT, EXPERTS])
        cw, cp = (al(n, [P, NT, 2]) for n in ("cw", "cp"))
        sb, sw = (al(n, [P, NT, 2, CAP]) for n in ("sb", "sw"))
        xg = al("xg", [P, KT, 2 * CAP])
        sg, ht = (al(n, [P, 2, FT, CAP]) for n in ("sg", "ht"))
        dt = al("dt", [P, KT, 2 * CAP])
        og = al("og", [P, D])
        swt = al("swt", [P, NT, P])
        zero = al("zero", [P, P])
        need(V, counted)
        v(V.memset(place[:, :, EXPERTS:], 0.0))
        v(V.tensor_tensor(place[:, :, 0:EXPERTS], self.bank(3, NT * EXPERTS).rearrange("p (t n) -> p t n", t=NT),
                          selv, ALU.mult))
        v(V.tensor_scalar(rest[:, :, :], place[:, :, 0:EXPERTS], CAP + 0.5, None, ALU.is_ge))
        v(V.tensor_reduce(m[:, 0, 0:1], rest[:, :, :], AXY, ALU.max))
        v(V.tensor_tensor(rest[:, :, :], rest[:, :, :], combv, ALU.mult))
        need(M, dve.now())
        q = pe.mark(M.matmul(self.bank(1, 1), c["ones"], m[:, 0, 0:1], start=True, stop=True))
        need(V, q)
        v(V.tensor_copy(self.spill[:, 0:1], self.bank(1, 1)))
        v(V.memset(zero[:, :], 0.0))
        v(V.memset(dt[:, :, :], 0.0))
        v(V.memset(swt[:, :, :], 0.0))
        down = lambda w: w.rearrange("p a b -> p (a b)").rearrange("p (f n) -> p f n", f=FT)
        wide = lambda w: w.unsqueeze(3).to_broadcast([P, NT, 2, CAP])
        places = c["places"].unsqueeze(1).unsqueeze(1).to_broadcast([P, NT, 2, CAP])
        half = lambda b: self.bank(b).rearrange("p (k s) -> p k s", k=KT // 2)

        def gather(ready):
            need(M, ready)
            q = []
            for k in range(KT):
                for t in range(NT):
                    w = M.matmul(self.bank(2 + k // 4, P, k % 4 * P), self.x[:, t, k * P:(k + 1) * P],
                                 sb[:, t].rearrange("p e s -> p (e s)"), start=(t == 0), stop=(t == NT - 1),
                                 skip_group_check=True)
                if k % 4 == 3:
                    q.append(pe.mark(w))
            need(A, q[0])
            a = act.mark(A.activation(xg[:, 0:4], half(2), ACT.Copy))
            need(V, q[1])
            return q[1], a, dve.mark(V.tensor_copy(xg[:, 4:8], half(3)))

        def turn_results(ready):
            need(M, *ready)
            q = []
            for k in range(KT):
                w = M.transpose(self.bank(k // 4, P, k % 4 * P), dt[:, k], c["ident"])
                if k % 4 == 3:
                    q.append(pe.mark(w))
            need(A, q[0])
            need(V, q[1])
            return (act.mark(A.activation(og[:, 0:512], self.bank(0), ACT.Copy)),
                    dve.mark(V.tensor_copy(og[:, 512:], self.bank(1))))

        def scatter(ready):
            need(M, *ready)
            for b in range(4):
                q = M.matmul(self.bank(4 + b), swt[:, b // 2], og[:, b % 2 * 512:(b % 2 + 1) * 512], start=False,
                             stop=True, skip_group_check=True)
            return pe.mark(q)

        v(V.tensor_tensor(sb[:, :, :, :], places, wide(place[:, :, 0:2]), ALU.is_equal))
        need(M, dve.now(), act.now())
        for b in range(4):
            M.matmul(self.bank(4 + b), zero[:, :], self.x[:, b // 2, (b % 2) * 512:(b % 2 + 1) * 512],
                     start=True, stop=False, skip_group_check=True)
        gathered = gather(dve.now())
        p.barrier()
        with p.fori("experts", EXPERTS // 2) as i:
            later = lambda name: self.behind("experts", name)
            need(V, later("gathered"), later("sw_turned"), later("xg_v"))
            need(V, dve.mark(V.tensor_copy(cw[:, :, :], combv[:, :, bass.ds(i * 2, 2)])))
            swq = dve.mark(V.tensor_tensor(sw[:, :, :, :], sb[:, :, :, :], wide(cw[:, :, :]), ALU.mult))
            cpq = dve.mark(V.tensor_copy(cp[:, :, :], place[:, :, bass.ds(i * 2 + 2, 2)]))
            need(V, swq, cpq)
            sbq = dve.mark(V.tensor_tensor(sb[:, :, :, :], places, wide(cp[:, :, :]), ALU.is_equal))
            hq = []
            for e in range(2):
                gate, up = 3 * e, 3 * e + 1
                need(M, self.arrived[gate].now(), self.arrived[up].now(), later("xg_a"), later("xg_v"))
                for n in range(2 * FT):
                    for k in range(KT):
                        q = M.matmul(self.bank(2 + e, CAP, n * CAP),
                                     self.slots[:, 3 * e + n // FT, k, n % FT * P:(n % FT + 1) * P],
                                     xg[:, k, e * CAP:(e + 1) * CAP], start=(k == 0), stop=(k == KT - 1),
                                     skip_group_check=True)
                q = pe.mark(q)
                self.refill(gate, i * 6 + (U_MOE + 6 + gate), q)
                self.refill(up, i * 6 + (U_MOE + 6 + up), q)
                halves = self.bank(2 + e, 2 * FT * CAP).rearrange("p (z f s) -> p z f s", z=2, f=FT)
                need(A, q, later(f"ht{e}"))
                a = act.mark(A.activation(sg[:, e], halves[:, 0], ACT.Silu))
                need(V, a, later(f"down{e}"))
                hq.append(dve.mark(V.tensor_tensor(ht[:, e], halves[:, 1], sg[:, e], ALU.mult)))
                self.note("experts", f"ht{e}", hq[e])
                if e == 0:
                    ogq = turn_results([later("dt_a"), later("dt_v")])
            scatter(ogq)
            need(M, swq)
            for t in range(NT):
                q = M.transpose(self.bank(1, P, t * P), sw[:, t].rearrange("p e s -> p (e s)"), c["ident"])
            tq = pe.mark(q)
            self.note("experts", "sw_turned", tq)
            need(A, tq)
            swtq = act.mark(A.activation(swt[:, :, :], self.bank(1, T).rearrange("p (t s) -> p t s", t=NT), ACT.Copy))
            for e in range(2):
                s = 3 * e + 2
                need(M, hq[e], self.arrived[s].now())
                if e == 1:
                    need(M, swtq)
                for k in range(KT):
                    for f in range(FT):
                        q = M.matmul(self.bank(e, CAP, k * CAP), down(self.slots[:, s])[:, f, k * P:(k + 1) * P],
                                     ht[:, e, f], start=(f == 0), stop=(f == FT - 1), skip_group_check=True)
                q = pe.mark(q)
                self.note("experts", f"down{e}", q)
                self.refill(s, i * 6 + (U_MOE + 6 + s), q)
                src = self.bank(e).rearrange("p (k s) -> p k s", k=KT)
                if e == 0:
                    need(A, q)
                    dta = act.mark(A.activation(dt[:, :, 0:CAP], src, ACT.Copy))
                    need(M, hq[1])
                    gathered = gather(sbq)
                else:
                    need(V, q)
                    dtv = dve.mark(V.tensor_copy(dt[:, :, CAP:], src))
            for name, point in (("gathered", gathered[0]), ("xg_a", gathered[1]), ("xg_v", gathered[2]),
                                ("dt_a", dta), ("dt_v", dtv)):
                self.note("experts", name, point)
        scatter(turn_results([dta, dtv]))

        p.barrier()
        wb = al("wb", [P, 3, KT, UC])
        sd, hd = (al(n, [P, NT, HID]) for n in ("sd", "hd"))
        hdt = al("hdt", [P, FT, T])
        cr = al("cr", [P, NT, 1])
        with p.only_if(self.spill[0:1, 0:1]):
            with p.fori("spilled", EXPERTS) as i:
                later = lambda name: self.behind("spilled", name)
                need(nc.sync, later("downed"))
                for z in range(3):
                    wq = self.spilled.mark(nc.sync.dma_start(wb[:, z], I["wu"][i * 3 + (U_MOE + z)]))
                need(V, later("hidden"))
                crq = dve.mark(V.tensor_copy(cr[:, :, :], rest[:, :, bass.ds(i, 1)]))
                need(M, wq, later("hidden"))
                for t in range(NT):
                    for n in range(2):
                        for k in range(KT):
                            q = M.matmul(self.bank(t, HID, n * HID), self.xt[:, k, t * P:(t + 1) * P], wb[:, n, k, :],
                                         start=(k == 0), stop=(k == KT - 1), skip_group_check=True)
                q = pe.mark(q)
                need(A, q, later("hidden"))
                for t in range(NT):
                    a = act.mark(A.activation(sd[:, t], self.bank(t, HID), ACT.Silu))
                need(V, a, crq)
                for t in range(NT):
                    h = dve.mark(V.scalar_tensor_tensor(hd[:, t], self.bank(t, HID, HID), cr[:, t], sd[:, t],
                                                        ALU.mult, ALU.mult))
                self.note("spilled", "hidden", h)
                need(M, h)
                for f in range(FT):
                    for t in range(NT):
                        q = M.transpose(self.bank(2, P, (f * NT + t) * P), hd[:, t, f * P:(f + 1) * P], c["ident"])
                q = pe.mark(q)
                need(A, q)
                a = act.mark(A.activation(hdt[:, :, :], self.bank(2).rearrange("p (f t) -> p f t", f=FT), ACT.Copy))
                need(M, a)
                for b in range(4):
                    for f in range(FT):
                        q = M.matmul(self.bank(4 + b), hdt[:, f, (b // 2) * P:(b // 2 + 1) * P],
                                     down(wb[:, 2])[:, f, (b % 2) * 512:(b % 2 + 1) * 512], start=False, stop=True,
                                     skip_group_check=True)
                q = pe.mark(q)
                self.note("spilled", "downed", q)
        need(V, pe.now())
        for t in range(NT):
            q = dve.mark(V.scalar_tensor_tensor(
                self.x[:, t].rearrange("p (a n) -> p a n", a=2), self.x[:, t].rearrange("p (a n) -> p a n", a=2),
                ALPHA, self.ps[:, 4 + 2 * t:6 + 2 * t], ALU.mult, ALU.add))
        need(V, q)
        self.layer_norm(1, st, sq, (rows, loaded))

    def chain(self):
        def v(ins):
            q = self.dve.mark(ins)
            self.need(self.nc.vector, q)
            return q
        return v

    def embed(self):
        nc, I, need = self.nc, self.ins, self.need
        pe, act, dve = self.pe, self.act, self.dve
        A, V, M = nc.scalar, nc.vector, nc.tensor
        self.fresh()
        pt = self.alloc("pt", [P, 2, T])
        sg = self.alloc("sg", [P, 4, NT, UC])
        loaded = self.load(pt[:, :, :], I["pt"])
        t = self.turn(self.x, self.xt, KT, [dve.now()], [0, 1])
        need(M, t, loaded, self.arrived[4].now())
        wp = self.slots[:, 4].rearrange("p a b -> p (a b)").rearrange("p (f n) -> p f n", f=2)
        for cg in range(4):
            for t in range(NT):
                for f in range(2):
                    q = M.matmul(self.bank(4 + cg, UC, t * UC), pt[:, f, t * P:(t + 1) * P],
                                 wp[:, f, cg * UC:(cg + 1) * UC], start=(f == 0), stop=(f == 1),
                                 skip_group_check=True)
        pq = pe.mark(q)

        def gate(cg, b, q):
            need(A, q)
            q = act.mark(A.activation(sg[:, cg], self.bank(b).rearrange("p (t n) -> p t n", t=NT), ACT.Sigmoid))
            need(V, q, pq)
            r = dve.mark(V.tensor_tensor(sg[:, cg], sg[:, cg],
                                         self.bank(4 + cg).rearrange("p (t n) -> p t n", t=NT), ALU.mult))
            need(V, r)
            xc = self.x[:, :, cg * UC:(cg + 1) * UC]
            dve.mark(V.tensor_tensor(xc, xc, sg[:, cg], ALU.add))
            return q

        self.project("embed", U_PE, 4, 1, self.xt, gate, skip=2)

    def even(self):
        nc, I, p, need, c = self.nc, self.ins, self.p, self.need, self.c
        pe, act, dve = self.pe, self.act, self.dve
        A, V, M = nc.scalar, nc.vector, nc.tensor
        self.fresh()
        al = self.alloc
        self.consts("pool", self.slots[:, 4].rearrange("p a b -> p (a b)"))
        self.consts("late")
        ecw = al("ecw", [P, 16, 4])
        wif = al("wif", [P, KT, 2 * AH])
        bif = al("bif", [P, 2 * AH])
        feat = al("feat", [P, FEATS])
        self.load(ecw[:, :, :], I["ecw"])
        self.load(wif[:, :, :], I["w_if"])
        self.load(bif[:, :], I["e_b_if_2"].to_broadcast([P, 2 * AH]))
        loaded = self.load(feat[:, :], I["feat"])
        fcol = lambda at: (lambda k: feat[:, at + k:at + k + 1])
        st = al("st", [P, 4])
        qk = al("qk", [P, 16, T])
        pj = al("pj", [P, 5, NT, D])
        mark = self.top
        xn = al("xn", [P, NT, D])
        v = self.chain()
        q = self.norm_rows(self.x, xn, D, 0, st)
        need(V, q)
        for t in range(NT):
            q = dve.mark(V.tensor_scalar(xn[:, t], self.x[:, t], st[:, t:t + 1], None, ALU.mult))
        need(A, loaded)
        self.turn(xn, self.xt, KT, [q], [0, 1], fcol(F_ENORM))
        self.p.barrier()
        self.top = mark
        raw = al("raw", [P, 8, T + 3])
        cws = al("cws", [P, 8, 4])
        v(V.memset(raw[:, :, :], 0.0))
        need(A, dve.now())
        with p.fori("even_qk", 2) as i:
            for l in (pe, act, dve):
                self.all_before("even_qk", l)
            v(V.tensor_copy(cws[:, :, :], ecw[:, bass.ds(i * 8, 8), :]))
            for s in range(4):
                need(M, self.arrived[s].now())
                for n in range(2):
                    for k in range(KT):
                        q = M.matmul(self.bank(s, T, T * n), self.slots[:, s, k, n * P:(n + 1) * P],
                                     self.xt[:, k, :], start=(k == 0), stop=(k == KT - 1), skip_group_check=True)
                q = pe.mark(q)
                self.refill(s, i * 4 + (U_EIN + 4 + s), q)
                need(A, q)
                q = act.mark(A.activation(raw[:, 2 * s:2 * s + 2, 3:3 + T],
                                          self.bank(s).rearrange("p (n t) -> p n t", n=2), ACT.Copy))
                need(V, q)
                last = [None] * 2
                for tap in range(4):
                    for n in range(2):
                        j = 2 * s + n
                        o = qk[:, bass.ds(i * 8 + j, 1), :]
                        src = raw[:, j:j + 1, tap:tap + T]
                        need(V, last[n])
                        if tap == 0:
                            last[n] = dve.mark(V.tensor_scalar(o, src, cws[:, j, 0:1], None, ALU.mult))
                        else:
                            last[n] = dve.mark(V.scalar_tensor_tensor(o, src, cws[:, j, tap:tap + 1], o,
                                                                      ALU.mult, ALU.add))
            need(A, last[1])
            o = qk[:, bass.ds(i * 8, 8), :]
            act.mark(A.activation(o, o, ACT.Silu))
            for l in (pe, act, dve):
                self.note("even_qk", l.name, l.now())

        pjv = pj[:, :, :, :].rearrange("p s t n -> p (s t) n")

        def keep(cg, b, q):
            need(A, q)
            return act.mark(A.activation(pjv[:, bass.ds((cg // 4) * 2, 2), bass.ds((cg % 4) * UC, UC)],
                                         self.bank(b).rearrange("p (t n) -> p t n", t=NT), ACT.Copy))

        self.project("even_in", U_EIN + 8, 20, 1, self.xt, keep)
        VS, OS, ZA, US, ZB = range(5)
        need(A, act.now())
        act.mark(A.activation(pj[:, OS], pj[:, OS], ACT.Sigmoid))
        act.mark(A.activation(pj[:, ZA], pj[:, ZA], ACT.Silu))
        zq = act.mark(A.activation(pj[:, ZB], pj[:, ZB], ACT.Silu))
        gt = al("gt", [P, NT, 2 * AH])
        lf = al("lf", [P, NT, AH])
        l2 = al("l2", [P, NT, AH])
        bc = al("bc", [P, NT, AH])
        ai = al("ai", [P, NT, AH])
        need(M, act.now())
        for t in range(NT):
            for k in range(KT):
                q = M.matmul(self.bank(4, 2 * AH, t * 2 * AH), self.xt[:, k, t * P:(t + 1) * P], wif[:, k, :],
                             start=(k == 0), stop=(k == KT - 1), skip_group_check=True)
        q = pe.mark(q)
        need(V, q)
        v(V.tensor_tensor(gt[:, :, :], self.bank(4, 4 * AH).rearrange("p (t n) -> p t n", t=NT),
                          bif[:, :].unsqueeze(1).to_broadcast([P, NT, 2 * AH]), ALU.add))
        fg = gt[:, :, AH:2 * AH]
        v(V.scalar_tensor_tensor(l2[:, :, :], fg, -1.0, fg, ALU.mult, ALU.max))
        need(A, dve.now())
        q = act.mark(A.activation(l2[:, :, :], l2[:, :, :], ACT.Exp, scale=-1.0))
        need(A, q)
        q = act.mark(A.activation(l2[:, :, :], l2[:, :, :], ACT.Ln, bias=1.0))
        need(V, q)
        v(V.scalar_tensor_tensor(lf[:, :, :], fg, 0.0, l2[:, :, :], ALU.min, ALU.subtract))
        need(M, dve.now())
        for t in range(NT):
            for s in range(t + 1):
                q = M.matmul(self.bank(5, AH, t * AH), c["upto_all"] if s == t else c["ones"], lf[:, s, :],
                             start=(s == 0), stop=(s == t), skip_group_check=True)
        q = pe.mark(q)
        need(V, q)
        v(V.tensor_copy(bc[:, :, :], self.bank(5, 2 * AH).rearrange("p (t n) -> p t n", t=NT)))
        v(V.tensor_tensor(ai[:, :, :], gt[:, :, 0:AH], bc[:, :, :], ALU.subtract))
        ab = raw[:, 0:4, 0:P]
        for t in range(NT):
            v(V.tensor_copy(ab, ai[:, t, :].unsqueeze(2).to_broadcast([P, AH, P])))
            need(M, dve.now())
            for h in range(AH):
                q = M.matmul(self.bank(6 + h // 2, P, (h % 2) * T + t * P), ab[:, h], c["ident"],
                             start=True, stop=True, skip_group_check=True)
            q = pe.mark(q)
            need(V, q)
        late = c["late"].rearrange("p (t s) -> p t s", t=NT)
        self.top = mark
        self.p.barrier()
        ww = al("ww", [P, AH, T])
        wt = al("wt", [P, AH, 2, P])
        mm = al("mm", [P, 8, NT, AH])
        hn = al("hn", [P, AH, AD])
        for t in range(NT):
            for b in range(2):
                v(V.tensor_tensor(ww[:, 2 * b:2 * b + 2], self.bank(6 + b).rearrange("p (h s) -> p h s", h=2),
                                  late[:, t].unsqueeze(1).to_broadcast([P, 2, T]), ALU.subtract))
            v(V.tensor_reduce(mm[:, 0, t], ww[:, :, :], AX, ALU.max))
            v(V.tensor_scalar(mm[:, 0, t], mm[:, 0, t], 0.0, None, ALU.max))
            v(V.tensor_scalar(mm[:, 1, t], mm[:, 0, t], -1.0, None, ALU.mult))
            v(V.tensor_tensor(mm[:, 3, t], mm[:, 1, t], bc[:, t], ALU.subtract))
            need(A, dve.now())
            act.mark(A.activation(mm[:, 3, t], mm[:, 3, t], ACT.Exp))
            for h in range(AH):
                eq = act.mark(A.activation(ww[:, h], ww[:, h], ACT.Exp, bias=mm[:, 1, t, h:h + 1]))
            need(M, act.now(), dve.now())
            for h in range(AH):
                for k in range(2):
                    q = M.matmul(self.bank(h // 2, T, (h % 2) * T), qk[:, 2 * h + k, t * P:(t + 1) * P],
                                 qk[:, 8 + 2 * h + k, :], start=(k == 0), stop=(k == 1), skip_group_check=True)
            q = pe.mark(q)
            need(V, eq, q)
            for h in range(AH):
                q = dve.mark(V.scalar_tensor_tensor(ww[:, h], self.bank(h // 2, T, (h % 2) * T), AD ** -0.5,
                                                    ww[:, h], ALU.mult, ALU.mult, accum_out=mm[:, 2, t, h:h + 1]))
            need(V, q)
            v(V.scalar_tensor_tensor(mm[:, 4, t], mm[:, 2, t], -1.0, mm[:, 2, t], ALU.mult, ALU.max))
            v(V.tensor_tensor(mm[:, 4, t], mm[:, 4, t], mm[:, 3, t], ALU.max))
            v(V.reciprocal(mm[:, 4, t], mm[:, 4, t]))
            need(M, dve.now())
            for h in range(AH):
                for s in range(2):
                    q = M.transpose(self.bank(2 + h // 2, P, ((h % 2) * 2 + s) * P), ww[:, h, s * P:(s + 1) * P],
                                    c["ident"])
            q = pe.mark(q)
            need(A, q)
            for b in range(2):
                q = act.mark(A.activation(wt[:, 2 * b:2 * b + 2], self.bank(2 + b).rearrange(
                    "p (h s j) -> p h s j", h=2, s=2), ACT.Copy))
            need(M, q)
            for h in range(AH):
                for s in range(t + 1):
                    q = M.matmul(self.bank(4 + h // 2, AD, (h % 2) * AD), wt[:, h, s, :],
                                 pj[:, VS, s, h * AD:(h + 1) * AD], start=(s == 0), stop=(s == t),
                                 skip_group_check=True)
            q = pe.mark(q)
            need(V, q)
            og = pj[:, OS, t].rearrange("p (h d) -> p h d", h=AH)
            for h in range(AH):
                q = dve.mark(V.scalar_tensor_tensor(hn[:, h], self.bank(4 + h // 2, AD, (h % 2) * AD),
                                                    mm[:, 4, t, h:h + 1], og[:, h], ALU.mult, ALU.mult))
            need(A, q)
            for h in range(AH):
                q = act.mark(A.activation(ww[:, h], hn[:, h], ACT.Square, accum_out=mm[:, 5, t, h:h + 1]))
            need(A, q)
            q = act.mark(A.activation(mm[:, 5, t], mm[:, 5, t], ACT.Ln, scale=1.0 / AD, bias=self.col(0)))
            need(A, q)
            q = act.mark(A.activation(mm[:, 5, t], mm[:, 5, t], ACT.Exp, scale=-0.5))
            need(V, q, zq)
            za = pj[:, ZA, t].rearrange("p (h d) -> p h d", h=AH)
            for h in range(AH):
                q = dve.mark(V.scalar_tensor_tensor(za[:, h], hn[:, h], mm[:, 5, t, h:h + 1], za[:, h],
                                                    ALU.mult, ALU.mult))
            need(V, q)
        self.p.barrier()
        need(M, self.arrived[5].now(), self.small.now())
        win = c["window"].rearrange("p (g s t) -> p g s t", g=4, s=NT)
        pw = self.slots[:, 5].rearrange("p a b -> p (a b)").rearrange("p (g f n) -> p g f n", g=4, f=2)
        pT = ww
        zb = []
        for g in range(4):
            b = g % 2
            for f in range(2):
                for s in range(NT):
                    q = M.matmul(self.bank(b, T, f * T), pj[:, US, s, (2 * g + f) * P:(2 * g + f + 1) * P],
                                 win[:, g, s], start=(s == 0), stop=(s == NT - 1), skip_group_check=True)
            q = pe.mark(q)
            need(A, q)
            q = act.mark(A.activation(pT[:, 2 * b:2 * b + 2], self.bank(b).rearrange("p (f t) -> p f t", f=2), ACT.Copy))
            need(M, q)
            if g >= 2:
                need(M, zb[g - 2])
            for t in range(NT):
                for f in range(2):
                    q = M.matmul(self.bank(2 + b, UC, t * UC), pT[:, 2 * b + f, t * P:(t + 1) * P], pw[:, g, f],
                                 start=(f == 0), stop=(f == 1), skip_group_check=True)
            q = pe.mark(q)
            need(V, q)
            cols = pj[:, ZB, :, g * UC:(g + 1) * UC]
            zb.append(dve.mark(V.tensor_tensor(
                cols, cols, self.bank(2 + b).rearrange("p (t n) -> p t n", t=NT), ALU.mult)))
        self.turn(pj[:, ZA], self.yt[:, 0:8], KT, [dve.now()], [4, 5], fcol(F_HEAD))
        q = self.turn(pj[:, ZB], self.yt[:, 8:16], KT, [dve.now()], [6, 7], fcol(F_POOL))
        need(M, q)
        self.project("even_out", U_EOUT, 8, 2, self.yt, self.add_to_x)

    def odd(self):
        nc, I, p, need, c = self.nc, self.ins, self.p, self.need, self.c
        pe, act, dve = self.pe, self.act, self.dve
        A, V, M = nc.scalar, nc.vector, nc.tensor
        self.fresh()
        al = self.alloc
        self.consts("late")
        wki = al("wki", [P, KT, 132])
        feat = al("feat", [P, FEATS])
        rb = al("rb", [BUCKETS, CH])
        st = al("st", [P, 4])
        self.load(wki[:, :, :], I["w_ki"])
        self.load(feat[:, :], I["feat"])
        loaded = self.load(rb[:, :], I["rel_bias_2"])
        fcol = lambda at: (lambda k: feat[:, at + k:at + k + 1])
        v = self.chain()
        pq = al("pq", [P, 2, NT, D])
        fb = al("fb", [CH, 2 * T])
        xn = al("xn", [P, NT, D])
        kk = al("kk", [P, NT, D])
        vv = al("vv", [P, NT, D])
        self.pq, self.vv = pq, vv
        need(M, loaded)
        q = pe.mark(M.matmul(self.ps[0:CH, 7, :], rb[:, :], c["onehot"][0:BUCKETS, :], start=True, stop=True))
        need(A, q)
        q = act.mark(A.activation(fb[:, :], self.ps[0:CH, 7, :], ACT.Copy))
        need(A, q)
        wrote = self.scratch_done.mark(A.dma_start(self.bias_rows, fb[:, :]))
        q = self.norm_rows(self.x, xn, D, 0, st)
        need(V, q)
        for t in range(NT):
            q = dve.mark(V.tensor_scalar(xn[:, t], self.x[:, t], st[:, t:t + 1], None, ALU.mult))
        need(A, loaded)
        q = self.turn(xn, self.xt, KT, [q], [0, 1], fcol(F_ONORM))
        need(M, q)
        pqv = pq[:, :, :, :].rearrange("p s t n -> p (s t) n")

        def keep(cg, b, q):
            need(A, q)
            return act.mark(A.activation(pqv[:, bass.ds((cg // 4) * 2, 2), bass.ds((cg % 4) * UC, UC)],
                                         self.bank(b).rearrange("p (t n) -> p t n", t=NT), ACT.Copy))

        self.project("odd_in", U_OIN, 8, 1, self.xt, keep)
        need(M, act.now())
        need(M, self.arrived[0].now(), self.arrived[1].now())
        for t in range(NT):
            for k in range(KT):
                q = M.matmul(self.bank(0, UC, t * UC), self.xt[:, k, t * P:(t + 1) * P], self.slots[:, 0, k, :],
                             start=(k == 0), stop=(k == KT - 1), skip_group_check=True)
        self.refill(0, U_OOUT, pe.mark(q))
        for n in range(2):
            for k in range(KT):
                q = M.matmul(self.bank(1, T, n * T), self.slots[:, 1, k, n * P:(n + 1) * P], self.xt[:, k, :],
                             start=(k == 0), stop=(k == KT - 1), skip_group_check=True)
        self.refill(1, U_OOUT + 1, pe.mark(q))
        for k in range(KT):
            M.matmul(self.bank(2, T), wki[:, k, 0:P], self.xt[:, k, :], start=(k == 0), stop=(k == KT - 1),
                     skip_group_check=True)
        for t in range(NT):
            for k in range(KT):
                q = M.matmul(self.bank(3, IH, t * IH), self.xt[:, k, t * P:(t + 1) * P], wki[:, k, P:P + IH],
                             start=(k == 0), stop=(k == KT - 1), skip_group_check=True)
        q = pe.mark(q)
        ck = xn[:, 0, 0:NT * UC].rearrange("p (t n) -> p t n", t=NT)
        ckt = xn[:, 0, 512:1024].rearrange("p (k t) -> p k t", k=2)
        qit = xn[:, 1, 0:512].rearrange("p (k t) -> p k t", k=2)
        kit = xn[:, 1, 512:512 + T]
        wi = al("wi", [P, NT, IH])
        s4 = al("s4", [P, 4])
        need(A, q)
        act.mark(A.activation(qit, self.bank(1).rearrange("p (k t) -> p k t", k=2), ACT.Copy))
        act.mark(A.activation(kit, self.bank(2, T), ACT.Copy))
        act.mark(A.activation(wi[:, :, :], self.bank(3, NT * IH).rearrange("p (t n) -> p t n", t=NT), ACT.Copy,
                              scale=IH ** -0.5))
        for t in range(NT):
            q = act.mark(A.activation(ck[:, t], self.bank(0, UC, t * UC), ACT.Square, accum_out=s4[:, t:t + 1]))
        need(A, q)
        q = act.mark(A.activation(s4[:, 0:NT], s4[:, 0:NT], ACT.Ln, scale=1.0 / UC, bias=self.col(0)))
        need(A, q)
        q = act.mark(A.activation(s4[:, 0:NT], s4[:, 0:NT], ACT.Exp, scale=-0.5))
        need(V, q)
        for t in range(NT):
            q = dve.mark(V.tensor_scalar(ck[:, t], self.bank(0, UC, t * UC), s4[:, t:t + 1], None, ALU.mult))
        need(M, act.now())
        q = self.turn(ck, ckt, 2, [q], [4], fcol(F_KV))
        need(M, q, self.arrived[2].now(), self.arrived[3].now())
        for s, dst in ((2, kk), (3, vv)):
            w = self.slots[:, s].rearrange("p a b -> p (a b)").rearrange("p (f n) -> p f n", f=2)
            for t in range(NT):
                for b in range(2):
                    for f in range(2):
                        m = M.matmul(self.bank(2 * (s - 2) + b + 4 * (t % 2)), ckt[:, f, t * P:(t + 1) * P],
                                     w[:, f, b * 512:(b + 1) * 512], start=(f == 0), stop=(f == 1),
                                     skip_group_check=True)
                m = pe.mark(m)
                need(A, m)
                b0 = 2 * (s - 2) + 4 * (t % 2)
                act.mark(A.activation(dst[:, t].rearrange("p (b n) -> p b n", b=2), self.ps[:, b0:b0 + 2], ACT.Copy))
            self.refill(s, U_OOUT + s, m)
        qT, kT = self.yt[:, 0:8], self.yt[:, 8:16]
        sh = al("sh", [P, NT, CH])
        need(V, act.now())
        for src, dst, at in ((pq[:, 0], qT, F_Q), (kk, kT, F_K)):
            tv = self.xt[:, :, :].rearrange("p k t -> p (k t)").rearrange("p (t h d) -> p t h d", t=NT, h=CH)
            sv = src.rearrange("p t (h d) -> p t h d", h=CH)
            v(V.tensor_tensor(tv, sv, sv, ALU.mult))
            v(V.tensor_reduce(sh[:, :, :], tv, AX, ALU.add))
            need(A, dve.now())
            q = act.mark(A.activation(sh[:, :, :], sh[:, :, :], ACT.Ln, scale=1.0 / CD, bias=self.col(0)))
            need(A, q)
            q = act.mark(A.activation(sh[:, :, :], sh[:, :, :], ACT.Exp, scale=-0.5))
            need(V, q)
            for t in range(NT):
                v(V.tensor_tensor(sv[:, t], sv[:, t], sh[:, t].unsqueeze(2).to_broadcast([P, CH, CD]), ALU.mult))
            need(M, act.now())
            self.turn(src, dst, KT, [dve.now()], [4, 5], lambda k: feat[:, at:at + 1])
        zq = act.mark(A.activation(pq[:, 1], pq[:, 1], ACT.Silu))
        self.p.barrier()
        late = c["late"].rearrange("p (t s) -> p t s", t=NT)
        rl = kk[:, 0].rearrange("p (h s) -> p h s", h=IH)
        work = kk[:, 1, 0:T]
        best = al("best", [P, 8])
        mask = al("mask", [P, NT, T])
        tb = al("tb", [P, CH, T])
        for t in range(NT):
            need(M, act.now(), dve.now())
            for h in range(IH):
                r = slice(CD * (h % 2), CD * (h % 2) + CD)
                q = M.matmul(self.bank(2 * (h % 2), T, (h // 2) * T), qit[r, h // 2, t * P:(t + 1) * P], kit[r, :],
                             start=True, stop=True, skip_group_check=True)
            q = pe.mark(q)
            need(A, q, dve.now())
            for h in range(IH):
                q = act.mark(A.activation(rl[:, h], self.bank(2 * (h % 2), T, (h // 2) * T), ACT.Relu,
                                          scale=IDIM ** -0.5))
            need(V, q)
            v(V.tensor_scalar(mask[:, t], rl[:, 0], wi[:, t, 0:1], None, ALU.mult))
            for h in range(1, IH):
                v(V.scalar_tensor_tensor(mask[:, t], rl[:, h], wi[:, t, h:h + 1], mask[:, t], ALU.mult, ALU.add))
            v(V.tensor_tensor(work, mask[:, t], late[:, t], ALU.subtract))
            for r in range(SEL // 8):
                v(V.max(best[:, :], work))
                v(V.match_replace(work, best[:, :], work, TAKEN))
            v(V.tensor_scalar(work, work, TAKEN / 2, -BIG, ALU.is_gt, ALU.mult))
            v(V.tensor_tensor(mask[:, t], work, late[:, t], ALU.subtract))
        lg = kk[:, 0].rearrange("p (h s) -> p h s", h=4)
        pt = kk[:, 1].rearrange("p (h s t) -> p h s t", h=4, s=2)
        mx = al("mx", [P, NT, CH])
        dn = al("dn", [P, NT, CH])
        out = xn
        for t in range(NT):
            self.p.barrier()
            if t == 0:
                need(A, wrote)
            src = self.bias_src(t)
            got = self.small.mark(A.dma_start(tb[:, :, :], src))
            need(V, got)
            need(M, got)
            for g in range(4):
                need(M, dve.now(), act.now())
                for j in range(4):
                    h = 4 * g + j
                    r = slice(CD * (h % 2), CD * (h % 2) + CD)
                    q = M.matmul(self.bank(h % 2, T, (j // 2) * T), qT[r, h // 2, t * P:(t + 1) * P],
                                 kT[r, h // 2, :], start=True, stop=True, skip_group_check=True)
                q = pe.mark(q)
                need(V, q)
                for b in range(2):
                    v(V.scalar_tensor_tensor(lg[:, b::2, :], self.bank(b).rearrange("p (h s) -> p h s", h=2),
                                             CD ** -0.5, tb[:, 4 * g + b:4 * g + 4:2, ::-1], ALU.mult, ALU.add))
                v(V.tensor_tensor(lg, lg, mask[:, t].unsqueeze(1).to_broadcast([P, 4, T]), ALU.add))
                v(V.tensor_reduce(mx[:, t, 4 * g:4 * g + 4], lg, AX, ALU.max))
                v(V.tensor_scalar(mx[:, t, 4 * g:4 * g + 4], mx[:, t, 4 * g:4 * g + 4], -1.0, None, ALU.mult))
                need(A, dve.now())
                for j in range(4):
                    h = 4 * g + j
                    q = act.mark(A.activation(lg[:, j], lg[:, j], ACT.Exp, bias=mx[:, t, h:h + 1],
                                              accum_out=dn[:, t, h:h + 1]))
                need(M, q)
                for j in range(4):
                    for s in range(t + 1):
                        q = M.transpose(self.bank(2 + j // 2, P, ((j % 2) * 2 + s) * P), lg[:, j, s * P:(s + 1) * P],
                                        c["ident"])
                q = pe.mark(q)
                need(A, q)
                for b in range(2):
                    q = act.mark(A.activation(pt[:, 2 * b:2 * b + 2, 0:t + 1], self.bank(2 + b).rearrange(
                        "p (h s j) -> p h s j", h=2, s=2)[:, :, 0:t + 1], ACT.Copy))
                need(M, q)
                for j in range(4):
                    h = 4 * g + j
                    for s in range(t + 1):
                        q = M.matmul(self.bank(4 + 2 * t + h // 8, CD, (h % 8) * CD), pt[:, j, s, :],
                                     vv[:, s, h * CD:(h + 1) * CD], start=(s == 0), stop=(s == t),
                                     skip_group_check=True)
                q = pe.mark(q)
                need(A, q)
            need(V, q, act.now(), zq)
            v(V.reciprocal(dn[:, t], dn[:, t]))
            v(V.tensor_tensor(out[:, t].rearrange("p (h d) -> p h d", h=CH),
                              self.ps[:, 4 + 2 * t:6 + 2 * t].rearrange("p b (h d) -> p (b h) d", h=8),
                              dn[:, t].unsqueeze(2).to_broadcast([P, CH, CD]), ALU.mult))
            v(V.tensor_tensor(out[:, t], out[:, t], pq[:, 1, t], ALU.mult))
        q = self.turn(out, self.xt, KT, [dve.now()], [0, 1])
        need(M, q)
        self.project("odd_out", U_OOUT, 4, 1, self.xt, self.add_to_x)
        self.need(nc.sync, dve.now())
        o = self.stored.mark(nc.sync.dma_start(self.out.rearrange("a (n p) d -> p (a n) d", p=P), self.x[:, :, :]))
        self.need(nc.sync, o)

    def bias_src(self, t):
        return bass.AP(self.bias_rows.tensor, t * P, [[1, P], [2 * T, CH], [1, T]])

    def add_to_x(self, cg, b, q):
        self.need(self.nc.vector, q)
        cols = self.x[:, :, bass.ds(cg * UC, UC)]
        return self.dve.mark(self.nc.vector.tensor_tensor(
            cols, cols, self.bank(b).rearrange("p (t n) -> p t n", t=NT), ALU.add))

    def all_before(self, loop, line):
        q = self.behind(loop, line.name)
        for e in (self.nc.tensor, self.nc.scalar, self.nc.vector):
            self.need(e, q)

    def note(self, loop, name, point):
        base = self.p.starts[point.line.name]
        self.p.found.setdefault("notes", {})[(loop, name)] = (point.line.name, point.value - base)
        self.last[(loop, name)] = point

    def behind(self, loop, name):
        if self.p.loop is None:
            return self.last.get((loop, name))
        got = self.p.per.get("notes", {}).get((loop, name))
        if got is None:
            return None
        line = next(l for l in self.p.lines if l.name == got[0])
        return Point(line, self.p.starts[line.name] + got[1] - self.p.loop.per[line.name], self.p.loop)

    def finish_debug(self, t):
        self.need(self.nc.sync, self.dve.now(), self.act.now(), self.pool.now())
        q = self.small.mark(self.nc.sync.dma_start(self.dbg, t[:, :, :]))
        self.need(self.nc.sync, q)


def pack_units(w, rows_of_tiles=None):
    K, N = w.shape
    return w.reshape(K // D, KT, P, N // UC, UC).transpose(0, 3, 2, 1, 4)


def layout(I):
    A = {}
    w = I["gdn_w_in"][0]
    kw = QKH * HD
    sec = {"q": w[:, 0:kw], "k": w[:, kw:2 * kw], "v": w[:, 2 * kw:2 * kw + VH * HD],
           "z": w[:, 2 * kw + VH * HD:2 * kw + 2 * VH * HD]}
    heads = []
    for h in range(QKH):
        parts = [np.concatenate([sec["q"][:, h * HD:(h + 1) * HD], sec["k"][:, h * HD:(h + 1) * HD]], 1),
                 sec["v"][:, h * UC:(h + 1) * UC], sec["z"][:, h * UC:(h + 1) * UC]]
        heads.append(np.stack([pack_units(q)[0, 0] for q in parts]))
    cols = lambda w: pack_units(w)[0]
    halves = lambda w: pack_units(w).transpose(1, 0, 2, 3, 4).reshape(-1, P, KT, UC)
    wide = lambda w: w.reshape(2, P, D).transpose(1, 0, 2).reshape(P, KT, UC)
    wg, wup = (I[n][0].reshape(EXPERTS, KT, P, HID).transpose(0, 2, 1, 3) for n in ("moe_w_gate", "moe_w_up"))
    wdn = I["moe_w_down"][0].reshape(EXPERTS, 2, P, D).transpose(0, 2, 1, 3).reshape(EXPERTS, P, KT, UC)
    e = I["e_w_in_2"][0]
    g0, e1 = 5 * D, 5 * D + 2 * AH
    o = I["o_w_in_2"][0]
    ck, qi, ki = D, D + 256, D + 512
    units = np.concatenate([
        np.concatenate(heads), halves(I["gdn_w_out"][0]),
        np.stack([wg, wup, wdn], 1).reshape(3 * EXPERTS, P, KT, UC),
        cols(I["pe_w_gate"][0]), wide(I["pe_w_proj"][0])[None],
        I["e_w_pool_2"][0].reshape(4, 2, P, 256).transpose(2, 0, 1, 3).reshape(1, P, KT, UC),
        cols(e[:, :g0]), cols(e[:, e1:]), halves(I["e_w_out_2"][0]),
        cols(o[:, :D]), cols(o[:, ki + 68:]), cols(o[:, ck:ki]),
        wide(I["o_w_uk_2"][0])[None], wide(I["o_w_uv_2"][0])[None], cols(I["o_w_out_2"][0])])
    assert len(units) == UNITS
    A["wu"] = units
    ktile = lambda w: w.reshape(KT, P, -1).transpose(1, 0, 2)
    A["w_route"] = ktile(np.concatenate([I["moe_w_group"][0], I["moe_w_router"][0]], 1))
    A["b_route"] = np.concatenate([I["moe_b_group"], I["moe_b_router"]], 1)
    A["w_if"] = ktile(e[:, g0:e1])
    A["w_ki"] = ktile(np.concatenate([o[:, ki:ki + 64], o[:, ki:ki + 68]], 1))
    A["pt"] = I["p"][0, 0].T.reshape(2, P, T).transpose(1, 0, 2)
    A["ecw"] = I["e_conv_2"][0].reshape(4, 16, P).transpose(2, 1, 0)
    feat = lambda v: v.reshape(-1, P).T
    A["feat"] = np.concatenate([feat(I["e_norm_2"][0]), feat(I["o_norm_2"][0]), feat(I["e_g_head_2"][0]),
                                feat(I["e_s_pool_2"][0]), feat(I["o_g_kv_2"][0]),
                                feat(np.tile(I["o_g_q_2"][0], 2)), feat(np.tile(I["o_g_k_2"][0], 2))], 1)
    A["wab"] = w[:, 2 * kw + 2 * VH * HD:].reshape(KT, P, 64).transpose(1, 0, 2)
    c = I["gdn_conv_w"][0]
    q, k, v = c[:, :kw], c[:, kw:2 * kw], c[:, 2 * kw:]
    cw = np.stack([q.reshape(TAPS, QKH, HD), k.reshape(TAPS, QKH, HD),
                   v.reshape(TAPS, QKH, 2, HD)[:, :, 0], v.reshape(TAPS, QKH, 2, HD)[:, :, 1]], 2)
    A["cw"] = cw.transpose(3, 1, 2, 0).reshape(P, QKH, 4 * TAPS)
    A["xt"] = I["x"][0].T.reshape(KT, P, T).transpose(1, 0, 2)
    return A


KEEP = ["x", "gdn_a_log", "gdn_dt_bias", "gdn_norm_w", "ln_g", "ln_b", "e_b_if_2", "rel_bias_2"]


def arrays_of(inputs):
    I = {k: np.asarray(v) for k, v in inputs.items()}
    A = layout(I)
    for k in KEEP:
        A[k] = I[k]
    for g, v in constants().items():
        A["c_" + g] = np.concatenate(list(v.values()), 1)
    return {k: np.ascontiguousarray(v) for k, v in A.items()}


def program(nc, shapes, per, upto=99, dbg=None):
    ins = {k: nc.dram_tensor("in_" + k, s, F32, kind="ExternalInput").ap() for k, s in shapes.items()}
    out = nc.dram_tensor("out", (1, T, D), F32, kind="ExternalOutput").ap()
    d = nc.dram_tensor("dbg", dbg, F32, kind="ExternalOutput").ap() if dbg else None
    return Build(nc, ins, out, per, upto, d).p.found


def kernel(**inputs):
    import concourse.bacc as bacc
    from concourse.bass_utils import run_bass_kernel_spmd
    A = arrays_of(inputs)
    shapes = {k: v.shape for k, v in A.items()}
    counts = {}
    for _ in range(2):
        nc = bacc.Bacc("TRN2", target_bir_lowering=False, num_devices=1)
        counts = program(nc, shapes, counts)
    r = run_bass_kernel_spmd(nc, [{"in_" + k: v for k, v in A.items()}], core_ids=[0])
    return r.results[0]["out"]
```

```python
from contextlib import contextmanager

import numpy as np

import concourse.bass as bass
from concourse import mybir

F32 = mybir.dt.float32
ALU = mybir.AluOpType
ACT = mybir.ActivationFunctionType
AX, AXY = mybir.AxisListType.X, mybir.AxisListType.XY

P = 128
T = 256
NT = T // P
D = 1024
KT = D // P
UC = 256
QKH, VH, HD = 8, 16, 128
REP = VH // QKH
TAPS = 5
EXPERTS, TOPK, HID, GROUPS = 32, 2, 256, 4
EPG = EXPERTS // GROUPS
AH, AD = 4, 256
POOL_WINDOWS = (2, 4, 8, 16)
CH, CD = 16, 64
IH, IDIM = 4, 64
CAP = 64
SEL = 64
BUCKETS, MAXDIST = 32, 128
ALPHA = 2.0 ** 0.25
BIG = 1e30
LEVELS = (1, 2, 4, 8, 16, 32, 64)
NSLOT = 6
TAKEN = -2.0 ** 126
ARENA = 27500

U_GDN = 0
U_GOUT = U_GDN + 3 * QKH
U_MOE = U_GOUT + 8
U_PE = U_MOE + 3 * EXPERTS
U_POOL = U_PE + 5
U_EIN = U_POOL + 1
U_EOUT = U_EIN + 28
U_OIN = U_EOUT + 8
U_OOUT = U_OIN + 8
U_UK = U_OOUT + 4
U_CKV = U_UK + 2
UNITS = U_CKV + 2
F_ENORM, F_ONORM, F_HEAD, F_POOL, F_KV, F_Q, F_K = 0, 8, 16, 24, 32, 34, 35
FEATS = 36


class Point:

    def __init__(self, line, value, loop):
        self.line, self.value, self.loop = line, value, loop

    def before(self):
        return Point(self.line, self.value - self.loop.per[self.line.name], self.loop)

    def at(self):
        if self.loop is None:
            return self.value
        per = self.loop.per.get(self.line.name, 0)
        if self.loop.open:
            return self.loop.i * per + self.value if per else self.value
        return self.value + (self.loop.n - 1) * per


class Loop:
    def __init__(self, n, i, per):
        self.n, self.i, self.per, self.open = n, i, per, True


class Line:

    def __init__(self, prog, name, step=1):
        self.prog, self.name, self.step, self.count = prog, name, step, 0
        self.sem = prog.nc.alloc_semaphore(name)
        prog.lines.append(self)

    def mark(self, ins):
        ins.then_inc(self.sem, self.step)
        self.count += self.step
        return Point(self, self.count, self.prog.loop)

    def now(self):
        return Point(self, self.count, self.prog.loop)


class Prog:

    def __init__(self, nc, per):
        self.nc, self.per, self.loop, self.lines, self.found, self.seen = nc, per, None, [], {}, {}
        self.pe, self.act, self.dve, self.pool = (Line(self, n) for n in ("pe", "act", "dve", "pool"))

    def need(self, engine, *points):
        for p in points:
            if p is None:
                continue
            key = (engine.engine, p.line.name, id(p.loop))
            if self.seen.get(key, -1) >= p.value:
                continue
            self.seen[key] = p.value
            engine.wait_ge(p.line.sem, p.at())

    def barrier(self):
        for e in (self.nc.tensor, self.nc.scalar, self.nc.vector, self.nc.gpsimd):
            self.need(e, *(l.now() for l in (self.pe, self.act, self.dve, self.pool)))

    @contextmanager
    def fori(self, name, n):
        starts = self.starts = {l.name: l.count for l in self.lines}
        per = self.per.get(name, {})
        with self.nc.Fori(0, n, 1) as i:
            self.loop = Loop(n, i, per)
            self.seen = {}
            yield i
            self.loop.open = False
        self.found[name] = {l.name: l.count - starts[l.name] for l in self.lines}
        for l in self.lines:
            l.count = starts[l.name] + n * (l.count - starts[l.name])
        self.loop = None
        self.seen = {}


    @contextmanager
    def only_if(self, flag):
        nc = self.nc
        self.need(nc.sync, self.dve.now())
        value = nc.values_load(flag, min_val=0, max_val=P)
        starts = {l.name: l.count for l in self.lines}
        with nc.If(value != 0):
            yield
            for e in (nc.tensor, nc.scalar, nc.vector, nc.gpsimd, nc.sync):
                self.need(e, *(l.now() for l in self.lines if l.count != starts[l.name]))
        owner = {"pe": nc.tensor, "act": nc.scalar, "dve": nc.vector, "pool": nc.gpsimd}
        with nc.Else():
            for l in self.lines:
                if l.count != starts[l.name]:
                    owner.get(l.name, nc.sync).sem_inc(l.sem, l.count - starts[l.name])
        self.seen = {}


def constants():
    r = np.arange(P)
    i, j = r[:, None], r[None, :]
    eye = (i == j).astype(np.float32)
    upto = [i <= j, i >= j]
    behind = [i > j, i < j]
    keep = [i >= j, i <= j]

    def level(b):
        return (i // (2 * b) == j // (2 * b)) & ((i // b) % 2 == 1) & ((j // b) % 2 == 0)

    def four(fwd, bwd):
        return np.stack([fwd, fwd, bwd, bwd], 1).astype(np.float32)

    t = np.arange(T)
    late = np.stack([t[None, :] > P * n + r[:, None] for n in range(NT)], 1)
    window = []
    for w in POOL_WINDOWS:
        back = t[None, :] - t[:, None]
        window.append(((back >= 0) & (back < w)) / np.minimum(t + 1, w)[None, :] - (back == 0))
    window = np.stack(window).reshape(len(POOL_WINDOWS), NT, P, T).transpose(2, 0, 1, 3)
    dist = np.maximum(np.arange(2 * T) - (T - 1), 0)
    half = BUCKETS // 2
    far = half + (np.log(np.maximum(dist, 1).astype(np.float32) / np.float32(half))
                  / np.float32(np.log(MAXDIST / half)) * np.float32(BUCKETS - half)).astype(np.int32)
    bucket = np.where(dist < half, dist, np.minimum(far, BUCKETS - 1))
    onehot = np.zeros((P, 2 * T))
    onehot[bucket, np.arange(2 * T)] = 1
    common = {
        "ident": eye, "ones": np.ones((P, P)), "upto_all": i <= j,
        "columns": np.tile(np.array([1e-6, 1e-5, 0.5 * -np.log(HD), 1.0, -1.0, 0, 0, 0]), (P, 1)),
        "places": np.tile(np.arange(1, CAP + 1), (P, 1)),
        "rank4": np.tile(np.arange(4, 0, -1), (P, NT)), "rank8": np.tile(np.arange(8, 0, -1), (P, NT)),
    }
    delta = {
        "upto": np.stack(upto, 1), "behind": np.stack(behind, 1),
        "bars": four(~keep[0], ~keep[1]) * BIG,
        "levels_t": np.stack([four(level(b).T, level(b)) for b in LEVELS], 1),
        "level1": four(level(1), level(1).T),
        "ident4": four(eye, eye),
    }
    late = {"late": late * BIG, "onehot": onehot}
    flat = lambda g: {k: np.ascontiguousarray(v.reshape(P, -1).astype(np.float32)) for k, v in g.items()}
    return {"common": flat(common), "delta": flat(delta), "late": flat(late), "pool": flat({"window": window})}


def const_map(group):
    at, out = 0, {}
    for k, v in constants()[group].items():
        out[k] = (at, v.shape[1])
        at += v.shape[1]
    return out, at


class Build:
    def __init__(self, nc, ins, out, per):
        self.nc, self.ins, self.out = nc, ins, out
        self.p = p = Prog(nc, per)
        self.pe, self.act, self.dve, self.pool = p.pe, p.act, p.dve, p.pool
        self.need = p.need
        self.kept = Line(p, "product_kept")
        for engine, line in ((nc.tensor, p.pe), (nc.scalar, p.act), (nc.vector, p.dve), (nc.gpsimd, p.pool),
                             (nc.scalar, self.kept)):
            engine.sem_inc(line.sem, 1024)
            line.count = 1024
        self.ps = nc.alloc_psum_tensor("ps", [P, 8, 512], F32)
        self.slots = nc.alloc_sbuf_tensor("slots", [P, NSLOT, KT, UC], F32)
        self.arrived = [Line(p, f"slot{s}_arrived", 16) for s in range(NSLOT)]
        self.last = {}
        self.warm, self.warmed = nc.alloc_sbuf_tensor("warm", [P, 1], F32), None
        self.spill = nc.alloc_sbuf_tensor("spill", [P, 1], mybir.dt.int32)
        self.spilled = Line(p, "spilled_weights_arrived", 16)
        self.small = Line(p, "small_arrived", 16)
        self.scratch_done = Line(p, "bias_rows_stored", 16)
        self.stored = Line(p, "output_stored", 16)
        self.bias_rows = nc.dram_tensor("bias_rows", (CH, 2 * T), F32, kind="Internal").ap()
        self.x = nc.alloc_sbuf_tensor("x", [P, NT, D], F32)
        self.xt = nc.alloc_sbuf_tensor("xt", [P, KT, T], F32)
        self.yt = nc.alloc_sbuf_tensor("yt", [P, 16, T], F32)
        cm, n = const_map("common")
        self.cst = nc.alloc_sbuf_tensor("cst", [P, n], F32)
        self.c = {k: self.cst[:, a:a + m] for k, (a, m) in cm.items()}
        self.arena = nc.alloc_sbuf_tensor("arena", [P, ARENA], F32)
        self.top = 0
        self.stages()

    def alloc(self, name, shape):
        n = int(np.prod(shape[1:]))
        v = self.arena[:shape[0], self.top:self.top + n]
        self.top += n
        assert self.top <= ARENA, (name, self.top)
        if len(shape) > 2:
            names = "abcd"[:len(shape) - 1]
            v = v.rearrange(f"p ({' '.join(names)}) -> p {' '.join(names)}",
                            **{k: m for k, m in zip(names, shape[1:])})
        return v

    def fresh(self):
        self.preload_ln()
        self.p.barrier()
        self.need(self.nc.sync, *(l.now() for l in (self.pe, self.act, self.dve, self.pool)))
        self.top = 0

    def consts(self, group, at=None, line=None):
        cm, n = const_map(group)
        v = self.alloc(group, [P, n]) if at is None else at[:, 0:n]
        self.load(v, self.ins["c_" + group], line)
        self.c.update({k: v[:, a:a + m] for k, (a, m) in cm.items()})

    def load(self, dst, src, line=None):
        return (line or self.small).mark(self.nc.sync.dma_start(dst, src))

    def bank(self, b, n=512, at=0):
        return self.ps[:, b, at:at + n]

    def refill(self, slot, unit, point):
        self.need(self.nc.sync, point)
        return self.arrived[slot].mark(self.nc.sync.dma_start(self.slots[:, slot], self.ins["wu"][unit]))

    def stages(self):
        self.gdn()
        self.moe()
        self.embed()
        self.even()
        self.odd()

    def gdn(self):
        nc, I, p, need, c = self.nc, self.ins, self.p, self.need, self.c
        pe, act, dve, pool = self.pe, self.act, self.dve, self.pool
        A, V, G, M = nc.scalar, nc.vector, nc.gpsimd, nc.tensor
        al = self.alloc
        wab = al("wab", [P, KT, 64])
        alog = al("alog", [P, 32])
        dtb = al("dtb", [P, 32])
        cw = al("cw", [P, QKH, 4 * TAPS])
        nw = al("gdn_nw", [P, 1])
        first = Line(p, "gate_inputs_arrived", 16)
        delta_arrived = Line(p, "delta_constants_arrived", 16)
        for k in (0, KT // 2):
            self.load(self.xt[:, k:k + KT // 2, :], I["xt"][:, k:k + KT // 2, :], first)
        self.load(wab[:, :, :], I["wab"], first)
        self.load(alog[:, :], I["gdn_a_log"].rearrange("a d h -> a (d h)").to_broadcast([P, 32]), first)
        ready = self.load(dtb[:, :], I["gdn_dt_bias"].rearrange("a d h -> a (d h)").to_broadcast([P, 32]), first)
        self.refill(0, U_GDN, None)
        self.load(self.cst[:, :], I["c_common"])
        self.load(cw[:, :, :], I["cw"])
        common = self.load(nw[:, :], I["gdn_norm_w"].rearrange("a (p b) -> (a p) b", b=1))
        self.refill(1, U_GDN + 1, None)
        self.refill(2, U_GDN + 2, None)
        self.consts("delta", line=delta_arrived)
        const = delta_arrived.now()
        self.refill(3, U_GOUT + 3, None)
        self.load(self.x[:, :, :], I["x"].rearrange("a (n p) d -> p (a n) d", p=P))

        GC, BE, BG, GS = range(4)
        gate = al("gate", [P, 4, 2 * NT, VH])
        NI = 4
        sl = (slice(0, 4, 3), slice(1, 3))
        tile_of = lambda s, n: s if n < 2 else 1 - s
        mats = [P, 2, NI, P]
        raw = al("raw", [P, 4, T + TAPS - 1])
        cn = al("cn", [P, 4, T])
        cv = al("cv", [P, 4, T])
        zr = al("zr", [P, REP, T])
        sq, rn, rn2, f1 = (al(n, [P, 2, T]) for n in ("sq", "rn", "rn2", "f1"))
        cwh = al("cwh", [P, 4 * TAPS])
        sc = al("sc", [P, 4, 2 * NT, REP])
        gb, dm, am, an = (al(n, mats) for n in ("gb", "dm", "am", "an"))
        at, att, mt, X, XT = (al(n, mats) for n in ("at", "att", "mt", "X", "XT"))
        vn = al("vn", mats)
        er, qd, kdec, S = (al(n, [P, NI, P]) for n in ("er", "qd", "kdec", "S"))
        ktm = al("ktm", [P, NT, P])
        vtm = al("vtm", [P, NT, REP, P])
        Y, vb, kbe, nwt = gb, dm, am[:, 0], an[:, 0]
        need(A, dve.mark(V.memset(raw[:, :, :], 0.0)))
        bars = c["bars"].rearrange("p (n j) -> p n j", n=NI)
        lvt = c["levels_t"].rearrange("p (l n j) -> p l n j", l=len(LEVELS), n=NI)
        l1 = c["level1"].rearrange("p (n j) -> p n j", n=NI)
        id4 = c["ident4"].rearrange("p (n j) -> p n j", n=NI)
        ident = c["ident"]
        four = lambda b: self.bank(b).rearrange("p (n j) -> p n j", n=NI)
        two = lambda b: self.bank(b).rearrange("p (n t) -> p n t", n=2)
        col = self.col

        class Next:

            def __init__(nx, h, note):
                nx.h, nx.note, nx.copied, nx.last = h, note, [], {}

            def group(nx, j):
                s, n = j // 2, j % 2
                if j >= 2:
                    need(M, nx.copied[j - 2])
                elif nx.note:
                    need(M, self.behind("delta", f"bank{j}"))
                if n == 0:
                    need(M, self.arrived[s].now())
                for k in range(KT):
                    q = M.matmul(self.bank(n, T), self.slots[:, s, k, n * P:(n + 1) * P], self.xt[:, k, :],
                                 start=(k == 0), stop=(k == KT - 1), skip_group_check=True)
                q = pe.mark(q)
                if n == 1:
                    self.refill(s, nx.h * 3 + (U_GDN + 3 + s), q)
                need(A, q)
                dst = raw[:, j, 2:2 + T] if j < 4 else zr[:, n]
                nx.copied.append(act.mark(A.activation(dst, self.bank(n, T), ACT.Copy)))

            def taps(nx):
                nx.t1 = dve.mark(V.tensor_copy(
                    cwh[:, :], cw[:, bass.ds(nx.h, 1), :].rearrange("p a b -> p (a b)")
                    if not isinstance(nx.h, int) else cw[:, nx.h, :]))
                need(V, nx.t1)

            def conv(nx, tap, pair):
                if tap == 0:
                    need(V, nx.copied[2 * pair], nx.copied[2 * pair + 1])
                for s in (2 * pair, 2 * pair + 1):
                    src, w = raw[:, s, tap:tap + T], cwh[:, s * TAPS + tap:s * TAPS + tap + 1]
                    if tap == 0:
                        q = dve.mark(V.tensor_scalar(cn[:, s], src, w, None, ALU.mult))
                    else:
                        need(V, nx.last[s])
                        q = dve.mark(V.scalar_tensor_tensor(cn[:, s], src, w, cn[:, s], ALU.mult, ALU.add))
                    nx.last[s] = q

            def silu_z(nx):
                need(A, nx.copied[5])
                dst = self.yt[:, bass.ds(nx.h * 2, 2), :] if not isinstance(nx.h, int) else \
                    self.yt[:, 2 * nx.h:2 * nx.h + 2, :]
                act.mark(A.activation(dst, zr[:, :, :], ACT.Silu))

            def silu(nx):
                need(A, nx.last[1], nx.last[3])
                qk = act.mark(A.activation(cn[:, 0:2], cn[:, 0:2], ACT.Silu))
                v = act.mark(A.activation(cv[:, 2:4], cn[:, 2:4], ACT.Silu))
                need(V, qk)
                nx.squared = dve.mark(V.tensor_tensor(sq[:, :, :], cn[:, 0:2], cn[:, 0:2], ALU.mult))
                if nx.note:
                    self.note("delta", "cv_v", v)

            def unit(nx):
                need(M, nx.squared, nx.copied[4])
                q = pe.mark(M.matmul(self.bank(0), c["ones"], sq[:, :, :], start=True, stop=True))
                need(A, q)
                q = act.mark(A.activation(rn[:, :, :], two(0), ACT.Ln, bias=col(0)))
                if nx.note:
                    self.note("delta", "bank0", q)
                need(A, q)
                act.mark(A.activation(rn[:, 0], rn[:, 0], ACT.Exp, scale=-0.5, bias=col(2)))
                nx.norms = act.mark(A.activation(rn[:, 1], rn[:, 1], ACT.Exp, scale=-0.5))

            def apply_unit(nx):
                need(V, nx.norms)
                q = dve.mark(V.tensor_tensor(cv[:, 0:2], cn[:, 0:2], rn[:, :, :], ALU.mult))
                if nx.note:
                    self.note("delta", "cv_qk", q)

            def scalars(nx):
                ds = (lambda n: bass.ds(nx.h * n, n)) if not isinstance(nx.h, int) else \
                    (lambda n: slice(nx.h * n, nx.h * n + n))
                for s in range(2):
                    nx.spread = dve.mark(V.tensor_copy(
                        gb[:, s].rearrange("p (d v) j -> p d v j", d=2),
                        gate[:, GC, sl[s], ds(2)].unsqueeze(3).to_broadcast([P, 2, REP, P])))
                for z in range(4):
                    nx.scalar = dve.mark(V.tensor_copy(sc[:, z], gate[:, z, :, ds(2)]))

            def decay_rows(nx):
                need(M, nx.spread)
                for s in range(2):
                    for n in range(NI):
                        q = M.transpose(self.bank(2 + s, P, n * P), gb[:, s, n], ident)
                nx.rows = pe.mark(q)

            def decay(nx):
                need(V, nx.rows)
                need(A, nx.rows, nx.scalar)
                ex = act.mark(A.activation(er[:, :, :], four(3), ACT.Exp))
                need(V, ex)
                t1 = [dve.mark(V.tensor_tensor(dm[:, s], four(2 + s), bars, ALU.add)) for s in range(2)]
                for s in range(2):
                    need(A, t1[s])
                    for n in range(NI):
                        t2 = act.mark(A.activation(dm[:, s, n], dm[:, s, n], ACT.Exp, scale=-1.0,
                                                   bias=sc[:, GC, 2 * (n // 2) + tile_of(s, n), n % 2:n % 2 + 1]))
                    if nx.note:
                        self.note("delta", f"decay{s}", t2)

        first = Next(0, False)
        need(M, ready)
        for t in range(NT):
            for k in range(KT):
                q = M.matmul(self.bank(2, 64, 64 * t), self.xt[:, k, t * P:(t + 1) * P], wab[:, k, :],
                             start=(k == 0), stop=(k == KT - 1), skip_group_check=True)
        q = pe.mark(q)
        ab = self.bank(2, 128).rearrange("p (t z n) -> p t z n", t=NT, z=2)
        g = al("g", [P, NT, 2 * VH])
        s1 = al("gate_s1", [P, NT, 2 * VH])
        s2 = al("gate_s2", [P, NT, 2 * VH])
        byt = lambda z: gate[:, z].rearrange("p (d t) n -> p t d n", d=2)
        need(V, q, ready)
        a = dve.mark(V.tensor_tensor(s1[:, :, :], ab[:, :, 0, :],
                                     dtb[:, :].unsqueeze(1).to_broadcast([P, NT, 32]), ALU.add))
        need(V, a)
        b = dve.mark(V.scalar_tensor_tensor(s2[:, :, :], s1[:, :, :], -1.0, s1[:, :, :], ALU.mult, ALU.max))
        need(A, b)
        b = act.mark(A.activation(s2[:, :, :], s2[:, :, :], ACT.Exp, scale=-1.0))
        need(A, ready)
        e = act.mark(A.activation(alog[:, :], alog[:, :], ACT.Exp))
        need(A, q)
        eb = act.mark(A.activation(byt(BE), ab[:, :, 1, :].rearrange("p t (d n) -> p t d n", d=2),
                                   ACT.Exp, scale=-1.0))
        need(A, b)
        b = act.mark(A.activation(s2[:, :, :], s2[:, :, :], ACT.Ln, bias=1.0))
        need(V, b, e, eb)
        b = dve.mark(V.scalar_tensor_tensor(s1[:, :, :], s1[:, :, :], 0.0, s2[:, :, :], ALU.max, ALU.add))
        need(V, b)
        b = dve.mark(V.scalar_tensor_tensor(g[:, :, :], s1[:, :, :], -1.0,
                                            alog[:, :].unsqueeze(1).to_broadcast([P, NT, 32]),
                                            ALU.mult, ALU.mult))
        e = dve.mark(V.tensor_scalar(gate[:, BE], gate[:, BE], 1.0, None, ALU.add))
        need(V, e)
        be = dve.mark(V.reciprocal(gate[:, BE], gate[:, BE]))
        first.group(0)
        first.group(1)
        need(M, be, const)
        up = c["upto"].rearrange("p (d i) -> p d i", d=2)
        bh = c["behind"].rearrange("p (d i) -> p d i", d=2)
        for t in range(NT):
            for d in range(2):
                o = 32 * d + 16 * t
                M.matmul(self.bank(3, 16, o), up[:, d], g[:, t, 16 * d:16 * d + 16],
                         start=True, stop=True, skip_group_check=True)
                q = M.matmul(self.bank(4, 16, o), bh[:, d], g[:, t, 16 * d:16 * d + 16],
                             start=True, stop=True, skip_group_check=True)
        q = pe.mark(q)
        need(A, q)
        sums = self.bank(3, 64).rearrange("p (m n) -> p m n", m=4)
        eg = s2[:, :, :].rearrange("p t (d n) -> p (t d) n", d=2)
        act.mark(A.activation(gate[:, GC], sums, ACT.Copy))
        act.mark(A.activation(gate[:, GS], self.bank(4, 64).rearrange("p (m n) -> p m n", m=4), ACT.Exp))
        e = act.mark(A.activation(eg, sums, ACT.Exp))
        need(V, e)
        dve.mark(V.tensor_tensor(gate[:, BG], gate[:, BE], eg, ALU.mult))

        def head(i, nx):
            later = lambda name: self.behind("delta", name)
            need(A, later("act"))
            need(V, later("dve"), later("scanned"))
            need(G, later("pool"), later("scanned"))
            G_ = (lambda j: nx.group(j)) if nx else (lambda j: None)
            need(M, later("cv_v"), later("cv_qk"))
            for t in range(NT):
                ts = slice(t * P, (t + 1) * P)
                M.transpose(self.bank(4, P, t * P), cv[:, 1, ts], ident)
                for v in range(REP):
                    M.transpose(self.bank(5, P, (t * 2 + v) * P), cv[:, 2 + v, ts], ident)
                M.matmul(self.bank(7, P, t * P), cv[:, 1, ts], cv[:, 1, ts], start=True, stop=True,
                         skip_group_check=True)
                q = M.matmul(self.bank(7, P, (2 + t) * P), cv[:, 0, ts], cv[:, 1, ts], start=True,
                             stop=True, skip_group_check=True)
            kq = pe.mark(q)
            need(A, kq)
            act.mark(A.activation(ktm[:, :, :], self.bank(4, 2 * P).rearrange("p (t j) -> p t j", t=2), ACT.Copy))
            tm = act.mark(A.activation(vtm[:, :, :, :].rearrange("p t v j -> p (t v) j"), four(5), ACT.Copy))
            G_(0)
            a1, a2, xq = [], [], []
            for s in range(2):
                need(V, kq, later(f"decay{s}"))
                for n in range(NI):
                    t = tile_of(s, n)
                    q = dve.mark(V.scalar_tensor_tensor(
                        am[:, s, n], self.bank(7, P, t * P), sc[:, BE, 2 * (n // 2) + t, n % 2:n % 2 + 1],
                        dm[:, s, n], ALU.mult, ALU.mult))
                a1.append(q)
            for s in range(2):
                need(V, a1[s])
                xq.append(dve.mark(V.tensor_tensor(X[:, s], am[:, s], l1, ALU.mult)))
            for s in range(2):
                need(V, xq[s])
                xq[s] = dve.mark(V.tensor_tensor(X[:, s], id4, X[:, s], ALU.subtract))
            for s in range(2):
                qkp = self.bank(7, 2 * P, 2 * P).rearrange("p (t j) -> p t j", t=2)
                qkp = qkp if s == 0 else qkp[:, ::-1]
                a2.append(dve.mark(V.tensor_tensor(
                    an[:, s].rearrange("p (d v) j -> p d v j", d=2), qkp.unsqueeze(2).to_broadcast([P, 2, REP, P]),
                    dm[:, s].rearrange("p (d v) j -> p d v j", d=2), ALU.mult)))
            def turned(src, b, ready, dst):
                need(M, ready)
                for n in range(NI):
                    q = M.transpose(self.bank(b, P, n * P), src[:, n], ident)
                q = pe.mark(q)
                need(A, q)
                return act.mark(A.activation(dst, four(b), ACT.Copy))

            atq = [turned(am[:, s], 2 + s, a1[s], at[:, s]) for s in range(2)]
            G_(1)
            need(M, tm)
            xtq = [turned(X[:, s], 4 + s, xq[s], XT[:, s]) for s in range(2)]
            need(M, *atq)
            attq = [turned(an[:, s], 2 + s, a2[s], att[:, s]) for s in range(2)]
            if nx:
                nx.taps()
            mq = [None, None]
            for s in range(2):
                need(G, atq[s])
                mq[s] = pool.mark(G.tensor_tensor(mt[:, s], at[:, s], lvt[:, 1], ALU.mult))
            scaled = {}

            def scale_rows():
                need(G, tm, a2[1])
                """beta v, and k by the decay behind it (first step) or by beta exp(gc) (second)."""
                for s in range(2):
                    for d in range(2):
                        t = tile_of(s, 2 * d)
                        pool.mark(G.tensor_tensor(vb[:, s, 2 * d:2 * d + 2], vtm[:, t],
                                                  sc[:, BE, 2 * d + t, :].unsqueeze(2).to_broadcast([P, REP, P]),
                                                  ALU.mult))
                for d in range(2):
                    for dst, z, s in ((kdec, GS, 0), (kbe, BG, 1)):
                        t = tile_of(s, 2 * d)
                        q = pool.mark(G.tensor_tensor(dst[:, 2 * d:2 * d + 2],
                                                      ktm[:, t].unsqueeze(1).to_broadcast([P, REP, P]),
                                                      sc[:, z, 2 * d + t, :].unsqueeze(2).to_broadcast([P, REP, P]),
                                                      ALU.mult))
                scaled["q"] = q

            ops = []
            if nx:
                ops = [(0, 0), (1, 0), (2, 0), (3, 0), (4, 0), (0, 1), (1, 1), (2, 1), (3, 1), (4, 1)]
            for l in range(1, len(LEVELS)):
                lastl = l == len(LEVELS) - 1
                yq, zq = [], []
                for s in range(2):
                    if l > 1:
                        need(M, attq[s])
                        xtq[s] = turned(X[:, s], 2 + s, xq[s], XT[:, s])
                    need(M, mq[s], xq[s])
                    if l == 1:
                        need(M, xtq[s])
                    for n in range(NI):
                        q = M.matmul(self.bank(4 + s, P, n * P), mt[:, s, n], X[:, s, n], start=True,
                                     stop=True, skip_group_check=True)
                    q = pe.mark(q)
                    if not lastl:
                        need(G, q)
                        mq[s] = pool.mark(G.tensor_tensor(mt[:, s], at[:, s], lvt[:, l + 1], ALU.mult))
                    need(A, q)
                    yq.append(act.mark(A.activation(Y[:, s], four(4 + s), ACT.Copy)))
                if l in (1, 2, 3, 5):
                    G_(min(1 + l, 5))
                if l == 1:
                    scale_rows()
                if l == 5 and nx:
                    nx.silu_z()
                for s in range(2):
                    need(M, yq[s], xtq[s])
                    if l == 1:
                        need(M, later("rms"))
                    for n in range(NI):
                        if lastl:
                            q = M.matmul(self.bank(6 + s, P, n * P), Y[:, s, n], XT[:, s, n], start=True,
                                         stop=True, skip_group_check=True)
                        else:
                            q = M.matmul(self.bank(6 + s, P, n * P), XT[:, s, n], Y[:, s, n], start=True,
                                         stop=True, skip_group_check=True)
                    zq.append(pe.mark(q))
                for s in range(2):
                    need(V, zq[s])
                    dst = XT if lastl else X
                    xq[s] = dve.mark(V.tensor_tensor(dst[:, s], dst[:, s], four(6 + s), ALU.subtract))
                if lastl:
                    break
                if l == 1:
                    qsrc = cv[:, 0].rearrange("p (t j) -> p t j", t=2)[:, ::-1]
                    qdq = dve.mark(V.tensor_tensor(
                        qd[:, :, :].rearrange("p (d v) j -> p d v j", d=2),
                        er[:, :, :].rearrange("p (d v) j -> p d v j", d=2),
                        qsrc.unsqueeze(2).to_broadcast([P, 2, REP, P]), ALU.mult))
                if l >= 2:
                    for _ in range(4):
                        if ops:
                            nx.conv(*ops.pop(0))
                if l == 4 and nx:
                    nx.silu()
            need(M, xq[0], scaled["q"])
            for n in range(NI):
                q = M.matmul(self.bank(4, P, n * P), XT[:, 0, n], vb[:, 0, n], start=True, stop=True,
                             skip_group_check=True)
            vq0 = pe.mark(q)
            need(M, xq[1])
            for n in range(NI):
                q = M.matmul(self.bank(2, P, n * P), kbe[:, n], XT[:, 1, n], start=True, stop=True,
                             skip_group_check=True)
            wq = pe.mark(q)
            need(A, vq0)
            v0 = act.mark(A.activation(vn[:, 0], four(4), ACT.Copy))
            need(A, wq)
            w1 = act.mark(A.activation(nwt, four(2), ACT.Copy, scale=-1.0))
            if nx:
                nx.unit()
            need(M, v0)
            for n in range(NI):
                q = M.matmul(self.bank(3, P, n * P), kdec[:, n], vn[:, 0, n], start=True, stop=True,
                             skip_group_check=True)
            sp = pe.mark(q)
            need(V, sp)
            sq_ = dve.mark(V.tensor_copy(S[:, :, :], four(3)))
            if nx:
                need(V, *zq)
                nx.scalars()
                nx.apply_unit()
            out = lambda s, n: self.bank(6, P, (n % 2) * T + tile_of(s, n) * P)
            for n in range(NI):
                M.matmul(out(0, n), vn[:, 0, n], att[:, 0, n], start=(n == 0), stop=False, skip_group_check=True)
            need(M, w1, sq_, qdq)
            for n in range(NI):
                M.matmul(self.bank(5, P, n * P), XT[:, 1, n], vb[:, 1, n], start=True, stop=False,
                         skip_group_check=True)
                q = M.matmul(self.bank(5, P, n * P), nwt[:, n], S[:, n], start=False, stop=True,
                             skip_group_check=True)
            vq1 = pe.mark(q)
            need(A, vq1)
            v1 = act.mark(A.activation(vn[:, 1], four(5), ACT.Copy))
            if nx:
                nx.decay_rows()
            for n in range(NI):
                M.matmul(out(1, n), S[:, n], qd[:, n], start=False, stop=False, skip_group_check=True)
            need(M, v1)
            for n in range(NI):
                q = M.matmul(out(1, n), vn[:, 1, n], att[:, 1, n], start=False, stop=True, skip_group_check=True)
            op = pe.mark(q)
            need(A, op)
            q = act.mark(A.activation(f1[:, :, :], two(6), ACT.Square))
            rms = act.mark(A.activation(sq[:, :, :], two(6), ACT.Copy, scale=nw[:, 0:1]))
            need(M, q)
            q = pe.mark(M.matmul(self.bank(1), c["ones"], f1[:, :, :], start=True, stop=True))
            if nx:
                need(A, qdq)
                nx.decay()
            need(A, q)
            ln = act.mark(A.activation(rn2[:, :, :], two(1), ACT.Ln, scale=1.0 / HD, bias=col(0)))
            need(A, ln)
            aq = act.mark(A.activation(rn2[:, :, :], rn2[:, :, :], ACT.Exp, scale=-0.5))
            need(G, aq)
            q = pool.mark(G.tensor_tensor(rn2[:, :, :], rn2[:, :, :], sq[:, :, :], ALU.mult))
            need(G, q)
            y = self.yt[:, bass.ds(i * 2, 2), :] if not isinstance(i, int) else self.yt[:, 2 * i:2 * i + 2, :]
            q = pool.mark(G.tensor_tensor(y, rn2[:, :, :], y, ALU.mult))
            if nx:
                for name, point in (("bank1", ln), ("rms", rms), ("act", aq), ("dve", dve.now()), ("pool", q),
                                    ("scanned", op)):
                    self.note("delta", name, point)

        for e in (A, V, G, M):
            need(e, const, common)
        need(V, dve.now(), act.now())
        first.scalars()
        for j in range(2, 6):
            first.group(j)
            if j == 2:
                need(M, act.now())
                first.decay_rows()
                first.decay()
        first.taps()
        for pair in range(2):
            for tap in range(TAPS):
                first.conv(tap, pair)
        first.silu()
        first.silu_z()
        first.unit()
        first.apply_unit()
        p.barrier()
        with p.fori("delta", QKH - 1) as i:
            head(i, Next(i + 1, True))
        head(QKH - 1, None)

    def col(self, k):
        return self.c["columns"][:, k:k + 1]

    def project(self, name, first, units, halves, lhs, evac, skip=0):
        M, pe = self.nc.tensor, self.pe
        groups = 4 // halves
        free = {}

        def body(i):
            for cg in range(groups):
                if free.get(cg) is not None:
                    self.need(M, free[cg])
                for h in range(halves):
                    s = cg * halves + h
                    self.need(M, self.arrived[s].now())
                    for t in range(NT):
                        for k in range(KT):
                            q = M.matmul(self.bank(cg, UC, t * UC), lhs[:, h * KT + k, t * P:(t + 1) * P],
                                         self.slots[:, s, k, :], start=(t == 0 and k == 0 and h == 0),
                                         stop=(k == KT - 1 and h == halves - 1), skip_group_check=True)
                    q = pe.mark(q)
                    if first + 4 + skip < UNITS:
                        self.refill(s, i * 4 + (first + 4 + skip + s), q)
                free[cg] = evac(i * groups + cg, cg, q)

        n = units // 4
        if n == 1:
            body(0)
            return
        with self.p.fori(name, n) as i:
            for cg in range(groups):
                free[cg] = self.behind(name, f"bank{cg}")
            body(i)
            for cg in range(groups):
                self.note(name, f"bank{cg}", free[cg])

    def preload_ln(self):
        self.need(self.nc.scalar, self.warmed)
        self.warmed = self.act.mark(self.nc.scalar.activation(self.warm[:, :], self.col(3), ACT.Ln))

    def norm_rows(self, src, sq, width, eps, st):
        A, act = self.nc.scalar, self.act
        for t in range(NT):
            q = act.mark(A.activation(sq[:, t], src[:, t], ACT.Square, accum_out=st[:, t:t + 1]))
        self.need(A, q)
        q = act.mark(A.activation(st[:, 0:NT], st[:, 0:NT], ACT.Ln, scale=1.0 / width, bias=self.col(eps)))
        self.need(A, q)
        return act.mark(A.activation(st[:, 0:NT], st[:, 0:NT], ACT.Exp, scale=-0.5))

    def turn(self, src, dst, ktiles, ready, banks, scale=None):
        M, A = self.nc.tensor, self.nc.scalar
        free = [None] * len(banks)
        self.need(M, *ready)
        for g in range(ktiles // 2):
            b = g % len(banks)
            self.need(M, free[b])
            for k in range(2):
                for t in range(NT):
                    q = M.transpose(self.bank(banks[b], P, (2 * k + t) * P),
                                    src[:, t, (2 * g + k) * P:(2 * g + k + 1) * P], self.c["ident"])
            q = self.pe.mark(q)
            self.need(A, q)
            if scale is None:
                free[b] = self.act.mark(A.activation(
                    dst[:, 2 * g:2 * g + 2, :], self.bank(banks[b]).rearrange("p (k t) -> p k t", k=2), ACT.Copy))
            else:
                for k in range(2):
                    free[b] = self.act.mark(A.activation(
                        dst[:, 2 * g + k, :], self.bank(banks[b], T, k * T), ACT.Copy, scale=scale(2 * g + k)))
        return free[b]

    def layer_norm(self, row, stats, gb):
        A, V, act, dve = self.nc.scalar, self.nc.vector, self.act, self.dve
        for t in range(NT):
            for n in range(2):
                q = dve.mark(V.bn_stats(stats[:, t, 6 * n:6 * n + 6], self.x[:, t, n * 512:(n + 1) * 512]))
        self.need(V, q)
        for t in range(NT):
            q = m = dve.mark(V.bn_aggr(stats[:, t, 12:14], stats[:, t, 0:12]))
        self.need(A, q)
        var = stats[:, :, 13:14]
        q = act.mark(A.activation(var, var, ACT.Ln, bias=self.col(1)))
        self.need(A, q)
        q = act.mark(A.activation(var, var, ACT.Exp, scale=-0.5))
        self.need(V, m, gb[1])
        for t in range(NT):
            x = self.x[:, t]
            m = dve.mark(V.scalar_tensor_tensor(x, x, stats[:, t, 12:13], gb[0][:, row], ALU.subtract, ALU.mult))
        self.need(V, q, m)
        for t in range(NT):
            x = self.x[:, t]
            q = dve.mark(V.scalar_tensor_tensor(x, x, stats[:, t, 13:14], gb[0][:, 2 + row], ALU.mult, ALU.add))
        return q

    def moe(self):
        nc, I, p, need, c = self.nc, self.ins, self.p, self.need, self.c
        pe, act, dve, pool = self.pe, self.act, self.dve, self.pool
        A, V, M = nc.scalar, nc.vector, nc.tensor
        self.fresh()
        al = self.alloc
        rows = al("rows", [P, 4, D])
        wr = al("w_route", [P, KT, GROUPS + EXPERTS])
        br = al("b_route", [P, GROUPS + EXPERTS])
        stats = al("stats", [P, NT, 14])
        self.load(wr[:, :, :], I["w_route"])
        self.load(br[:, :], I["b_route"].to_broadcast([P, GROUPS + EXPERTS]))
        self.load(rows[:, 0:2], I["ln_g"][0].unsqueeze(0).to_broadcast([P, 2, D]))
        loaded = self.load(rows[:, 2:4], I["ln_b"][0].unsqueeze(0).to_broadcast([P, 2, D]))
        for s in (4, 5):
            self.refill(s, U_MOE + s, None)

        def add(cg, b, q):
            need(V, q)
            cols = bass.ds(cg * UC, UC)
            return dve.mark(V.scalar_tensor_tensor(
                self.x[:, :, cols], self.x[:, :, cols], ALPHA, self.bank(b).rearrange("p (t n) -> p t n", t=NT),
                ALU.mult, ALU.add))

        self.project("delta_out", U_GOUT, 8, 2, self.yt, add)
        need(V, dve.now())
        q = self.layer_norm(0, stats, (rows, loaded))
        q = self.turn(self.x, self.xt, KT, [q], [0, 1])

        NG = GROUPS + EXPERTS
        lg = al("lg", [P, NT, NG])
        comb = al("comb", [P, NT, GROUPS, EPG])
        sel = al("sel", [P, NT, GROUPS, EPG])
        m = al("m", [P, NT, 8])
        g1 = al("g1", [P, NT, GROUPS])
        e1, e2, o1, o2 = (al(n, [P, NT, EPG]) for n in ("e1", "e2", "o1", "o2"))
        need(M, q, loaded)
        for t in range(NT):
            for k in range(KT):
                q = M.matmul(self.bank(2, NG, t * NG), self.xt[:, k, t * P:(t + 1) * P], wr[:, k, :],
                             start=(k == 0), stop=(k == KT - 1), skip_group_check=True)
        q = pe.mark(q)
        need(V, q)

        def v(ins):
            need(V, dve.mark(ins))

        def first_of(o, x, mx, rank, n):
            v(V.tensor_tensor(o, x, mx.to_broadcast([P, NT, n]), ALU.is_equal))
            v(V.tensor_tensor(o, o, rank, ALU.mult))
            v(V.tensor_reduce(m[:, :, 7], o, AX, ALU.max))
            v(V.tensor_tensor(o, o, m[:, :, 7].unsqueeze(2).to_broadcast([P, NT, n]), ALU.is_equal))

        r4 = c["rank4"].rearrange("p (t n) -> p t n", t=NT)
        r8 = c["rank8"].rearrange("p (t n) -> p t n", t=NT)
        gl = lg[:, :, 0:GROUPS]
        v(V.tensor_tensor(lg[:, :, :], self.bank(2, NT * NG).rearrange("p (t n) -> p t n", t=NT),
                          br[:, :].unsqueeze(1).to_broadcast([P, NT, NG]), ALU.add))
        v(V.tensor_reduce(m[:, :, 0], gl, AX, ALU.max))
        v(V.tensor_tensor(e1[:, :, 0:GROUPS], gl, m[:, :, 0].unsqueeze(2).to_broadcast([P, NT, GROUPS]), ALU.subtract))
        q = dve.now()
        need(A, q)
        ex = act.mark(A.activation(e1[:, :, 0:GROUPS], e1[:, :, 0:GROUPS], ACT.Exp))
        first_of(g1[:, :, :], gl, m[:, :, 0].unsqueeze(2), r4, GROUPS)
        need(V, ex)
        v(V.tensor_reduce(m[:, :, 1], e1[:, :, 0:GROUPS], AX, ALU.add))
        v(V.reciprocal(m[:, :, 1], m[:, :, 1]))
        el = lg[:, :, GROUPS:].rearrange("p t (g e) -> p t g e", g=GROUPS)
        for t in range(NT):
            v(V.tensor_tensor(comb[:, t], el[:, t], g1[:, t, :].unsqueeze(2).to_broadcast([P, GROUPS, EPG]), ALU.mult))
        for a, b in ((0, 1), (2, 3), (0, 2)):
            v(V.tensor_tensor(comb[:, :, a], comb[:, :, a], comb[:, :, b], ALU.add))
        v(V.tensor_copy(e1[:, :, :], comb[:, :, 0]))
        v(V.tensor_reduce(m[:, :, 2], e1[:, :, :], AX, ALU.max))
        first_of(o1[:, :, :], e1[:, :, :], m[:, :, 2].unsqueeze(2), r8, EPG)
        v(V.scalar_tensor_tensor(e2[:, :, :], o1[:, :, :], -BIG, e1[:, :, :], ALU.mult, ALU.add))
        v(V.tensor_reduce(m[:, :, 3], e2[:, :, :], AX, ALU.max))
        first_of(o2[:, :, :], e2[:, :, :], m[:, :, 3].unsqueeze(2), r8, EPG)
        v(V.tensor_tensor(m[:, :, 4], m[:, :, 3], m[:, :, 2], ALU.subtract))
        need(A, dve.now())
        ex = act.mark(A.activation(m[:, :, 4], m[:, :, 4], ACT.Exp))
        need(V, ex)
        v(V.tensor_scalar(m[:, :, 5], m[:, :, 4], 1.0, None, ALU.add))
        v(V.reciprocal(m[:, :, 5], m[:, :, 5]))
        v(V.tensor_tensor(m[:, :, 5], m[:, :, 5], m[:, :, 1], ALU.mult))
        v(V.tensor_tensor(m[:, :, 6], m[:, :, 5], m[:, :, 4], ALU.mult))
        v(V.tensor_tensor(e2[:, :, :], o1[:, :, :], o2[:, :, :], ALU.add))
        byg = lambda x, t: (x[:, t].unsqueeze(1).to_broadcast([P, GROUPS, EPG]),
                            g1[:, t, :].unsqueeze(2).to_broadcast([P, GROUPS, EPG]))
        for t in range(NT):
            v(V.tensor_tensor(sel[:, t], *byg(e2, t), ALU.mult))
        need(M, dve.now())
        selv = sel[:, :, :, :].rearrange("p t g e -> p t (g e)")
        M.matmul(self.bank(3, EXPERTS), c["upto_all"], selv[:, 0], start=True, stop=True, skip_group_check=True)
        M.matmul(self.bank(3, EXPERTS, EXPERTS), c["ones"], selv[:, 0], start=True, stop=False, skip_group_check=True)
        counted = pe.mark(M.matmul(self.bank(3, EXPERTS, EXPERTS), c["upto_all"], selv[:, 1], start=False, stop=True,
                                   skip_group_check=True))
        v(V.tensor_tensor(o1[:, :, :], o1[:, :, :], m[:, :, 5].unsqueeze(2).to_broadcast([P, NT, EPG]), ALU.mult))
        v(V.tensor_tensor(o2[:, :, :], o2[:, :, :], m[:, :, 6].unsqueeze(2).to_broadcast([P, NT, EPG]), ALU.mult))
        v(V.tensor_tensor(o1[:, :, :], o1[:, :, :], o2[:, :, :], ALU.add))
        for t in range(NT):
            v(V.tensor_tensor(comb[:, t], *byg(o1, t), ALU.mult))

        FT = HID // P
        combv = comb[:, :, :, :].rearrange("p t g e -> p t (g e)")
        place = al("place", [P, NT, EXPERTS + 2])
        rest = al("rest", [P, NT, EXPERTS])
        cw, cp = (al(n, [P, NT, 2]) for n in ("cw", "cp"))
        sb, sw = (al(n, [P, NT, 2, CAP]) for n in ("sb", "sw"))
        xg = al("xg", [P, KT, 2 * CAP])
        sg, ht = (al(n, [P, 2, FT, CAP]) for n in ("sg", "ht"))
        og = al("og", [P, D])
        swt = al("swt", [P, NT, P])
        zero = al("zero", [P, P])
        need(V, counted)
        v(V.memset(place[:, :, EXPERTS:], 0.0))
        v(V.tensor_tensor(place[:, :, 0:EXPERTS], self.bank(3, NT * EXPERTS).rearrange("p (t n) -> p t n", t=NT),
                          selv, ALU.mult))
        v(V.tensor_scalar(rest[:, :, :], place[:, :, 0:EXPERTS], CAP + 0.5, None, ALU.is_ge))
        v(V.tensor_reduce(m[:, 0, 0:1], rest[:, :, :], AXY, ALU.max))
        v(V.tensor_tensor(rest[:, :, :], rest[:, :, :], combv, ALU.mult))
        need(M, dve.now())
        q = pe.mark(M.matmul(self.bank(1, 1), c["ones"], m[:, 0, 0:1], start=True, stop=True))
        need(V, q)
        v(V.tensor_copy(self.spill[:, 0:1], self.bank(1, 1)))
        v(V.memset(zero[:, :], 0.0))
        v(V.memset(og[:, :], 0.0))
        v(V.memset(swt[:, :, :], 0.0))
        down = lambda w: w.rearrange("p a b -> p (a b)").rearrange("p (f n) -> p f n", f=FT)
        wide = lambda w: w.unsqueeze(3).to_broadcast([P, NT, 2, CAP])
        places = c["places"].unsqueeze(1).unsqueeze(1).to_broadcast([P, NT, 2, CAP])
        half = lambda b: self.bank(b).rearrange("p (k s) -> p k s", k=KT // 2)

        def gather(ready):
            need(M, ready)
            q = []
            for k in range(KT):
                for t in range(NT):
                    w = M.matmul(self.bank(2 + k // 4, P, k % 4 * P), self.x[:, t, k * P:(k + 1) * P],
                                 sb[:, t].rearrange("p e s -> p (e s)"), start=(t == 0), stop=(t == NT - 1),
                                 skip_group_check=True)
                if k % 4 == 3:
                    q.append(pe.mark(w))
            need(A, q[0])
            a = act.mark(A.activation(xg[:, 0:4], half(2), ACT.Copy))
            need(V, q[1])
            return q[1], a, dve.mark(V.tensor_copy(xg[:, 4:8], half(3)))

        def scatter(ready):
            need(M, *ready)
            for b in range(4):
                q = M.matmul(self.bank(4 + b), swt[:, b // 2], og[:, b % 2 * 512:(b % 2 + 1) * 512], start=False,
                             stop=True, skip_group_check=True)
            return pe.mark(q)

        v(V.tensor_tensor(sb[:, :, :, :], places, wide(place[:, :, 0:2]), ALU.is_equal))
        need(M, dve.now(), act.now())
        for b in range(4):
            M.matmul(self.bank(4 + b), zero[:, :], self.x[:, b // 2, (b % 2) * 512:(b % 2 + 1) * 512],
                     start=True, stop=False, skip_group_check=True)
        gathered = gather(dve.now())
        p.barrier()
        with p.fori("experts", EXPERTS // 2) as i:
            later = lambda name: self.behind("experts", name)
            need(V, later("gathered"), later("sw_turned"), later("xg_v"))
            need(V, dve.mark(V.tensor_copy(cw[:, :, :], combv[:, :, bass.ds(i * 2, 2)])))
            swq = dve.mark(V.tensor_tensor(sw[:, :, :, :], sb[:, :, :, :], wide(cw[:, :, :]), ALU.mult))
            cpq = dve.mark(V.tensor_copy(cp[:, :, :], place[:, :, bass.ds(i * 2 + 2, 2)]))
            need(V, swq, cpq)
            sbq = dve.mark(V.tensor_tensor(sb[:, :, :, :], places, wide(cp[:, :, :]), ALU.is_equal))
            hq = []
            for e in range(2):
                gate, up = 3 * e, 3 * e + 1
                need(M, self.arrived[gate].now(), self.arrived[up].now(), later("xg_a"), later("xg_v"))
                for n in range(2 * FT):
                    for k in range(KT):
                        q = M.matmul(self.bank(2 + e, CAP, n * CAP),
                                     self.slots[:, 3 * e + n // FT, k, n % FT * P:(n % FT + 1) * P],
                                     xg[:, k, e * CAP:(e + 1) * CAP], start=(k == 0), stop=(k == KT - 1),
                                     skip_group_check=True)
                q = pe.mark(q)
                self.refill(gate, i * 6 + (U_MOE + 6 + gate), q)
                self.refill(up, i * 6 + (U_MOE + 6 + up), q)
                halves = self.bank(2 + e, 2 * FT * CAP).rearrange("p (z f s) -> p z f s", z=2, f=FT)
                need(A, q, later(f"ht{e}"))
                a = act.mark(A.activation(sg[:, e], halves[:, 0], ACT.Silu))
                need(V, a, later(f"down{e}"))
                hq.append(dve.mark(V.tensor_tensor(ht[:, e], halves[:, 1], sg[:, e], ALU.mult)))
                self.note("experts", f"ht{e}", hq[e])
                if e == 0:
                    scatter([later("og_a"), later("og_v"), swq])
                    for t in range(NT):
                        q = M.transpose(self.bank(0, P, t * P), sw[:, t].rearrange("p e s -> p (e s)"), c["ident"])
                    tq = pe.mark(q)
                    self.note("experts", "sw_turned", tq)
                    need(A, tq)
                    swtq = act.mark(A.activation(swt[:, :, :], self.bank(0, T).rearrange("p (t s) -> p t s", t=NT),
                                                 ACT.Copy))
            for e in range(2):
                s, r = 3 * e + 2, slice(e * CAP, (e + 1) * CAP)
                need(M, hq[e], self.arrived[s].now(), swtq)
                for b in range(2):
                    if e == 0 and b == 1:
                        need(M, hq[1])
                        gathered = gather(sbq)
                    for f in range(FT):
                        q = M.matmul(self.ps[r, b, :], ht[:, e, f], down(self.slots[:, s])[:, f, b * 512:(b + 1) * 512],
                                     start=(f == 0), stop=(f == FT - 1), skip_group_check=True)
                    q = pe.mark(q)
                    if b == 0:
                        need(A, q)
                        oga = act.mark(A.activation(og[r, 0:512], self.ps[r, 0, :], ACT.Copy))
                    else:
                        need(V, q)
                        ogv = dve.mark(V.tensor_copy(og[r, 512:], self.ps[r, 1, :]))
                self.note("experts", f"down{e}", q)
                self.refill(s, i * 6 + (U_MOE + 6 + s), q)
            for name, point in (("gathered", gathered[0]), ("xg_a", gathered[1]), ("xg_v", gathered[2]),
                                ("og_a", oga), ("og_v", ogv)):
                self.note("experts", name, point)
        scatter([oga, ogv, swtq])

        self.preload_ln()
        p.barrier()
        wb = al("wb", [P, 3, KT, UC])
        sd, hd = (al(n, [P, NT, HID]) for n in ("sd", "hd"))
        hdt = al("hdt", [P, FT, T])
        cr = al("cr", [P, NT, 1])
        with p.only_if(self.spill[0:1, 0:1]):
            with p.fori("spilled", EXPERTS) as i:
                later = lambda name: self.behind("spilled", name)
                need(nc.sync, later("downed"))
                for z in range(3):
                    wq = self.spilled.mark(nc.sync.dma_start(wb[:, z], I["wu"][i * 3 + (U_MOE + z)]))
                need(V, later("hidden"))
                crq = dve.mark(V.tensor_copy(cr[:, :, :], rest[:, :, bass.ds(i, 1)]))
                need(M, wq, later("hidden"))
                for t in range(NT):
                    for n in range(2):
                        for k in range(KT):
                            q = M.matmul(self.bank(t, HID, n * HID), self.xt[:, k, t * P:(t + 1) * P], wb[:, n, k, :],
                                         start=(k == 0), stop=(k == KT - 1), skip_group_check=True)
                q = pe.mark(q)
                need(A, q, later("hidden"))
                for t in range(NT):
                    a = act.mark(A.activation(sd[:, t], self.bank(t, HID), ACT.Silu))
                need(V, a, crq)
                for t in range(NT):
                    h = dve.mark(V.scalar_tensor_tensor(hd[:, t], self.bank(t, HID, HID), cr[:, t], sd[:, t],
                                                        ALU.mult, ALU.mult))
                self.note("spilled", "hidden", h)
                need(M, h)
                for f in range(FT):
                    for t in range(NT):
                        q = M.transpose(self.bank(2, P, (f * NT + t) * P), hd[:, t, f * P:(f + 1) * P], c["ident"])
                q = pe.mark(q)
                need(A, q)
                a = act.mark(A.activation(hdt[:, :, :], self.bank(2).rearrange("p (f t) -> p f t", f=FT), ACT.Copy))
                need(M, a)
                for b in range(4):
                    for f in range(FT):
                        q = M.matmul(self.bank(4 + b), hdt[:, f, (b // 2) * P:(b // 2 + 1) * P],
                                     down(wb[:, 2])[:, f, (b % 2) * 512:(b % 2 + 1) * 512], start=False, stop=True,
                                     skip_group_check=True)
                q = pe.mark(q)
                self.note("spilled", "downed", q)
        need(V, pe.now())
        for t in range(NT):
            q = dve.mark(V.scalar_tensor_tensor(
                self.x[:, t].rearrange("p (a n) -> p a n", a=2), self.x[:, t].rearrange("p (a n) -> p a n", a=2),
                ALPHA, self.ps[:, 4 + 2 * t:6 + 2 * t], ALU.mult, ALU.add))
        need(V, q)
        self.layer_norm(1, stats, (rows, loaded))

    def chain(self):
        def v(ins):
            q = self.dve.mark(ins)
            self.need(self.nc.vector, q)
            return q
        return v

    def embed(self):
        nc, I, need = self.nc, self.ins, self.need
        pe, act, dve = self.pe, self.act, self.dve
        A, V, M = nc.scalar, nc.vector, nc.tensor
        self.fresh()
        pt = self.alloc("pt", [P, 2, T])
        sg = self.alloc("sg", [P, 4, NT, UC])
        loaded = self.load(pt[:, :, :], I["pt"])
        t = self.turn(self.x, self.xt, KT, [dve.now()], [0, 1])
        need(M, t, loaded, self.arrived[4].now())
        wp = self.slots[:, 4].rearrange("p a b -> p (a b)").rearrange("p (f n) -> p f n", f=2)
        for cg in range(4):
            for t in range(NT):
                for f in range(2):
                    q = M.matmul(self.bank(4 + cg, UC, t * UC), pt[:, f, t * P:(t + 1) * P],
                                 wp[:, f, cg * UC:(cg + 1) * UC], start=(f == 0), stop=(f == 1),
                                 skip_group_check=True)
        pq = pe.mark(q)

        def gate(cg, b, q):
            need(A, q)
            q = act.mark(A.activation(sg[:, cg], self.bank(b).rearrange("p (t n) -> p t n", t=NT), ACT.Sigmoid))
            need(V, q, pq)
            r = dve.mark(V.tensor_tensor(sg[:, cg], sg[:, cg],
                                         self.bank(4 + cg).rearrange("p (t n) -> p t n", t=NT), ALU.mult))
            need(V, r)
            xc = self.x[:, :, cg * UC:(cg + 1) * UC]
            dve.mark(V.tensor_tensor(xc, xc, sg[:, cg], ALU.add))
            return q

        self.project("embed", U_PE, 4, 1, self.xt, gate, skip=2)

    def even(self):
        nc, I, p, need, c = self.nc, self.ins, self.p, self.need, self.c
        pe, act, dve = self.pe, self.act, self.dve
        A, V, M = nc.scalar, nc.vector, nc.tensor
        self.fresh()
        al = self.alloc
        self.consts("pool", self.slots[:, 4].rearrange("p a b -> p (a b)"))
        self.consts("late")
        ecw = al("ecw", [P, 16, 4])
        wif = al("wif", [P, KT, 2 * AH])
        bif = al("bif", [P, 2 * AH])
        feat = al("feat", [P, FEATS])
        self.load(ecw[:, :, :], I["ecw"])
        self.load(wif[:, :, :], I["w_if"])
        self.load(bif[:, :], I["e_b_if_2"].to_broadcast([P, 2 * AH]))
        loaded = self.load(feat[:, :], I["feat"])
        fcol = lambda at: (lambda k: feat[:, at + k:at + k + 1])
        st = al("st", [P, 4])
        qk = al("qk", [P, 16, T])
        pj = al("pj", [P, 5, NT, D])
        mark = self.top
        xn = al("xn", [P, NT, D])
        v = self.chain()
        q = self.norm_rows(self.x, xn, D, 0, st)
        need(V, q)
        for t in range(NT):
            q = dve.mark(V.tensor_scalar(xn[:, t], self.x[:, t], st[:, t:t + 1], None, ALU.mult))
        need(A, loaded)
        self.turn(xn, self.xt, KT, [q], [0, 1], fcol(F_ENORM))
        self.p.barrier()
        self.top = mark
        raw = al("raw", [P, 8, T + 3])
        cws = al("cws", [P, 8, 4])
        gt = al("gt", [P, NT, 2 * AH])
        lf, l2, bc, ai = (al(n, [P, NT, AH]) for n in ("lf", "l2", "bc", "ai"))
        ab = al("ab", [P, NT, AH, P])
        arow = al("arow", [P, AH, T])
        w0 = al("w0", [P, AH, P])
        w1 = al("w1", [P, AH, T])
        wt = al("wt", [P, AH, 3, P])
        mm = al("mm", [P, 8, NT, AH])
        hn = al("hn", [P, NT, AH, AD])
        ww = (w0, w1)
        v(V.memset(raw[:, :, :], 0.0))
        need(A, dve.now())
        for t in range(NT):
            for k in range(KT):
                q = M.matmul(self.bank(4, 2 * AH, t * 2 * AH), self.xt[:, k, t * P:(t + 1) * P], wif[:, k, :],
                             start=(k == 0), stop=(k == KT - 1), skip_group_check=True)
        q = pe.mark(q)
        need(V, q)
        v(V.tensor_tensor(gt[:, :, :], self.bank(4, 4 * AH).rearrange("p (t n) -> p t n", t=NT),
                          bif[:, :].unsqueeze(1).to_broadcast([P, NT, 2 * AH]), ALU.add))
        fg = gt[:, :, AH:2 * AH]
        v(V.scalar_tensor_tensor(l2[:, :, :], fg, -1.0, fg, ALU.mult, ALU.max))
        need(A, dve.now())
        q = act.mark(A.activation(l2[:, :, :], l2[:, :, :], ACT.Exp, scale=-1.0))
        need(A, q)
        q = act.mark(A.activation(l2[:, :, :], l2[:, :, :], ACT.Ln, bias=1.0))
        need(V, q)
        lfq = v(V.scalar_tensor_tensor(lf[:, :, :], fg, 0.0, l2[:, :, :], ALU.min, ALU.subtract))
        with p.fori("even_qk", 2) as i:
            need(M, self.behind("even_qk", "copied"))
            need(A, self.behind("even_qk", "convolved"))
            need(V, self.behind("even_qk", "convolved"))
            v(V.tensor_copy(cws[:, :, :], ecw[:, bass.ds(i * 8, 8), :]))
            for s in range(4):
                need(M, self.arrived[s].now())
                for n in range(2):
                    for k in range(KT):
                        q = M.matmul(self.bank(s, T, T * n), self.slots[:, s, k, n * P:(n + 1) * P],
                                     self.xt[:, k, :], start=(k == 0), stop=(k == KT - 1), skip_group_check=True)
                q = pe.mark(q)
                self.refill(s, i * 4 + (U_EIN + 4 + s), q)
                need(A, q)
                q = rawq = act.mark(A.activation(raw[:, 2 * s:2 * s + 2, 3:3 + T],
                                                 self.bank(s).rearrange("p (n t) -> p n t", n=2), ACT.Copy))
                need(V, q)
                last = [None] * 2
                for tap in range(4):
                    for n in range(2):
                        j = 2 * s + n
                        o = qk[:, bass.ds(i * 8 + j, 1), :]
                        src = raw[:, j:j + 1, tap:tap + T]
                        need(V, last[n])
                        if tap == 0:
                            last[n] = dve.mark(V.tensor_scalar(o, src, cws[:, j, 0:1], None, ALU.mult))
                        else:
                            last[n] = dve.mark(V.scalar_tensor_tensor(o, src, cws[:, j, tap:tap + 1], o,
                                                                      ALU.mult, ALU.add))
            need(A, last[1])
            o = qk[:, bass.ds(i * 8, 8), :]
            act.mark(A.activation(o, o, ACT.Silu))
            self.note("even_qk", "copied", rawq)
            self.note("even_qk", "convolved", last[1])

        qkq = act.now()
        VS, ZA, ZB, OS, US = range(5)
        need(M, lfq, rawq)
        for t in range(NT):
            for s in range(t + 1):
                q = M.matmul(self.bank(4, AH, t * AH), c["upto_all"] if s == t else c["ones"], lf[:, s, :],
                             start=(s == 0), stop=(s == t), skip_group_check=True)
        q = pe.mark(q)
        need(V, q)
        v(V.tensor_copy(bc[:, :, :], self.bank(4, 2 * AH).rearrange("p (t n) -> p t n", t=NT)))
        v(V.tensor_tensor(ai[:, :, :], gt[:, :, 0:AH], bc[:, :, :], ALU.subtract))
        abq = v(V.tensor_copy(ab[:, :, :, :], ai[:, :, :].unsqueeze(3).to_broadcast([P, NT, AH, P])))

        def keep_v(cg, b, q):
            need(A, q)
            return self.kept.mark(A.activation(pj[:, VS, :, cg * UC:(cg + 1) * UC],
                                         self.bank(b).rearrange("p (t n) -> p t n", t=NT), ACT.Copy))

        self.project("even_v", U_EIN + 8, 4, 1, self.xt, keep_v)
        need(M, abq)
        for h in range(AH):
            for t in range(NT):
                q = M.matmul(self.bank(6 + h // 2, P, (h % 2) * T + t * P), ab[:, t, h], c["ident"],
                             start=True, stop=True, skip_group_check=True)
        q = pe.mark(q)
        need(A, q)
        for b in range(2):
            aq = act.mark(A.activation(arow[:, 2 * b:2 * b + 2], self.bank(6 + b).rearrange("p (h s) -> p h s", h=2),
                                       ACT.Copy))
        need(M, qkq)
        for h in range(AH):
            for k in range(2):
                M.matmul(self.bank(4 + h // 2, T, (h % 2) * T), qk[:, 2 * h + k, P:2 * P], qk[:, 8 + 2 * h + k, :],
                         start=(k == 0), stop=(k == 1), skip_group_check=True)
        need(M, aq)
        for h in range(AH):
            for k in range(2):
                q = M.matmul(self.bank(6, P, h * P), qk[:, 2 * h + k, 0:P], qk[:, 8 + 2 * h + k, 0:P],
                             start=(k == 0), stop=(k == 1), skip_group_check=True)
        qkd = pe.mark(q)
        late = c["late"].rearrange("p (t s) -> p t s", t=NT)
        need(V, aq)
        for t in range(NT):
            S, w = (t + 1) * P, ww[t]
            v(V.tensor_tensor(w[:, :, :], arow[:, :, 0:S], late[:, t, 0:S].unsqueeze(1).to_broadcast([P, AH, S]),
                              ALU.subtract))
            v(V.tensor_reduce(mm[:, 0, t], w[:, :, :], AX, ALU.max))
            v(V.tensor_scalar(mm[:, 0, t], mm[:, 0, t], 0.0, None, ALU.max))
            v(V.tensor_scalar(mm[:, 1, t], mm[:, 0, t], -1.0, None, ALU.mult))
            v(V.tensor_tensor(mm[:, 3, t], mm[:, 1, t], bc[:, t], ALU.subtract))
            need(A, dve.now())
            act.mark(A.activation(mm[:, 3, t], mm[:, 3, t], ACT.Exp))
            for h in range(AH):
                eq = act.mark(A.activation(w[:, h], w[:, h], ACT.Exp, bias=mm[:, 1, t, h:h + 1]))
            need(V, eq, qkd)
            for h in range(AH):
                src = self.bank(4 + h // 2, T, (h % 2) * T) if t == 1 else self.bank(6, P, h * P)
                q = dve.mark(V.scalar_tensor_tensor(w[:, h], src, AD ** -0.5, w[:, h], ALU.mult, ALU.mult,
                                                    accum_out=mm[:, 2, t, h:h + 1]))
            need(V, q)
            v(V.scalar_tensor_tensor(mm[:, 4, t], mm[:, 2, t], -1.0, mm[:, 2, t], ALU.mult, ALU.max))
            v(V.tensor_tensor(mm[:, 4, t], mm[:, 4, t], mm[:, 3, t], ALU.max))
            v(V.reciprocal(mm[:, 4, t], mm[:, 4, t]))
        wq = dve.now()

        def keep(first, func):
            def evac(cg, b, q):
                need(A, q)
                return self.kept.mark(A.activation(
                    pj[:, first:first + 2].rearrange("p s t n -> p (s t) n")[
                        :, bass.ds((cg // 4) * 2, 2), bass.ds((cg % 4) * UC, UC)],
                    self.bank(b).rearrange("p (t n) -> p t n", t=NT), func))
            return evac

        self.project("even_z", U_EIN + 12, 8, 1, self.xt, keep(ZA, ACT.Silu))
        zq = self.kept.now()
        self.project("even_ou", U_EIN + 20, 8, 1, self.xt, keep(OS, ACT.Copy))
        kept = self.kept.now()
        need(M, wq, kept)
        for t, s, b in ((0, 0, 0), (1, 0, 1), (1, 1, 2)):
            for h in range(AH):
                q = M.transpose(self.bank(b, P, h * P), ww[t][:, h, s * P:(s + 1) * P], c["ident"])
            q = pe.mark(q)
            need(A, q)
            tq = act.mark(A.activation(wt[:, :, b], self.bank(b).rearrange("p (h j) -> p h j", h=AH), ACT.Copy))
            if b == 0:
                w0q = tq
        vq = []
        for t in range(NT):
            need(M, w0q if t == 0 else tq)
            for h in range(AH):
                for s in range(t + 1):
                    q = M.matmul(self.bank(4 + 2 * t + h // 2, AD, (h % 2) * AD), wt[:, h, t + s, :],
                                 pj[:, VS, s, h * AD:(h + 1) * AD], start=(s == 0), stop=(s == t),
                                 skip_group_check=True)
            vq.append(pe.mark(q))
        need(A, kept)
        sig = act.mark(A.activation(pj[:, OS], pj[:, OS], ACT.Sigmoid))
        need(V, sig)
        hq = []
        for t in range(NT):
            need(V, vq[t])
            og = pj[:, OS, t].rearrange("p (h d) -> p h d", h=AH)
            for h in range(AH):
                q = dve.mark(V.scalar_tensor_tensor(hn[:, t, h], self.bank(4 + 2 * t + h // 2, AD, (h % 2) * AD),
                                                    mm[:, 4, t, h:h + 1], og[:, h], ALU.mult, ALU.mult))
            hq.append(q)
        need(M, kept, vq[1], self.arrived[5].now(), self.small.now())
        win = c["window"].rearrange("p (g s t) -> p g s t", g=4, s=NT)
        pw = self.slots[:, 5].rearrange("p a b -> p (a b)").rearrange("p (g f n) -> p g f n", g=4, f=2)
        pT = al("pooled", [P, 4, T])
        zb = []
        for g in range(4):
            b = g % 2
            for f in range(2):
                for s in range(NT):
                    q = M.matmul(self.bank(b, T, f * T), pj[:, US, s, (2 * g + f) * P:(2 * g + f + 1) * P],
                                 win[:, g, s], start=(s == 0), stop=(s == NT - 1), skip_group_check=True)
            q = pe.mark(q)
            need(A, q)
            q = act.mark(A.activation(pT[:, 2 * b:2 * b + 2], self.bank(b).rearrange("p (f t) -> p f t", f=2), ACT.Copy))
            need(M, q)
            if g >= 2:
                need(M, zb[g - 2])
            for t in range(NT):
                for f in range(2):
                    q = M.matmul(self.bank(2 + b, UC, t * UC), pT[:, 2 * b + f, t * P:(t + 1) * P], pw[:, g, f],
                                 start=(f == 0), stop=(f == 1), skip_group_check=True)
            q = pe.mark(q)
            need(V, q, zq)
            cols = pj[:, ZB, :, g * UC:(g + 1) * UC]
            zb.append(dve.mark(V.tensor_tensor(
                cols, cols, self.bank(2 + b).rearrange("p (t n) -> p t n", t=NT), ALU.mult)))
        for t in range(NT):
            need(A, hq[t], wq, tq)
            for h in range(AH):
                q = act.mark(A.activation(w1[:, h], hn[:, t, h], ACT.Square, accum_out=mm[:, 5, t, h:h + 1]))
            need(A, q)
        q = act.mark(A.activation(mm[:, 5], mm[:, 5], ACT.Ln, scale=1.0 / AD, bias=self.col(0)))
        need(A, q)
        rq = act.mark(A.activation(mm[:, 5], mm[:, 5], ACT.Exp, scale=-0.5))
        for s in (4, 5):
            self.refill(s, U_CKV + s - 4, pe.now())
        need(V, rq, zq)
        for t in range(NT):
            za = pj[:, ZA, t].rearrange("p (h d) -> p h d", h=AH)
            for h in range(AH):
                q = dve.mark(V.scalar_tensor_tensor(za[:, h], hn[:, t, h], mm[:, 5, t, h:h + 1], za[:, h],
                                                    ALU.mult, ALU.mult))
        self.turn(pj[:, ZB], self.yt[:, 8:16], KT, [zb[-1], hq[-1]], [6, 7], fcol(F_POOL))
        q = self.turn(pj[:, ZA], self.yt[:, 0:8], KT, [dve.now()], [4, 5], fcol(F_HEAD))
        need(M, q)
        self.project("even_out", U_EOUT, 8, 2, self.yt, self.add_to_x)

    def odd(self):
        nc, I, p, need, c = self.nc, self.ins, self.p, self.need, self.c
        pe, act, dve = self.pe, self.act, self.dve
        A, V, G, M = nc.scalar, nc.vector, nc.gpsimd, nc.tensor
        self.fresh()
        al = self.alloc
        self.consts("late")
        wki = al("wki", [P, KT, 132])
        feat = al("feat", [P, FEATS])
        rb = al("rb", [BUCKETS, CH])
        st = al("st", [P, 4])
        self.load(wki[:, :, :], I["w_ki"])
        self.load(feat[:, :], I["feat"])
        loaded = self.load(rb[:, :], I["rel_bias_2"])
        fcol = lambda at: (lambda k: feat[:, at + k:at + k + 1])
        v = self.chain()
        pq = al("pq", [P, 2, NT, D])
        fb = al("fb", [CH, 2 * T])
        xn = al("xn", [P, NT, D])
        kk = al("kk", [P, NT, D])
        vv = al("vv", [P, NT, D])
        tb = [al(f"tb{t}", [P, CH, (t + 1) * P]) for t in range(NT)]
        q = self.norm_rows(self.x, xn, D, 0, st)
        need(V, q)
        for t in range(NT):
            q = dve.mark(V.tensor_scalar(xn[:, t], self.x[:, t], st[:, t:t + 1], None, ALU.mult))
        need(A, loaded)
        q = self.turn(xn, self.xt, KT, [q], [0, 1], fcol(F_ONORM))
        turned = q
        need(M, loaded)
        q = pe.mark(M.matmul(self.ps[0:CH, 7, :], rb[:, :], c["onehot"][0:BUCKETS, :], start=True, stop=True))
        need(A, q)
        q = act.mark(A.activation(fb[:, :], self.ps[0:CH, 7, :], ACT.Copy))
        need(nc.sync, q)
        wrote = self.scratch_done.mark(nc.sync.dma_start(self.bias_rows, fb[:, :]))
        need(nc.sync, wrote)
        for t in range(NT):
            biased = self.small.mark(nc.sync.dma_start(tb[t][:, :, :], self.bias_src(t)))
        need(M, turned, self.arrived[4].now(), self.arrived[5].now())
        for n in range(2):
            for k in range(KT):
                q = M.matmul(self.bank(5, T, n * T), self.slots[:, 5, k, n * P:(n + 1) * P], self.xt[:, k, :],
                             start=(k == 0), stop=(k == KT - 1), skip_group_check=True)
        for k in range(KT):
            M.matmul(self.bank(6, T), wki[:, k, 0:P], self.xt[:, k, :], start=(k == 0), stop=(k == KT - 1),
                     skip_group_check=True)
        for t in range(NT):
            for k in range(KT):
                q = M.matmul(self.bank(6, IH, T + t * IH), self.xt[:, k, t * P:(t + 1) * P], wki[:, k, P:P + IH],
                             start=(k == 0), stop=(k == KT - 1), skip_group_check=True)
        iq = pe.mark(q)
        for t in range(NT):
            for k in range(KT):
                q = M.matmul(self.bank(4, UC, t * UC), self.xt[:, k, t * P:(t + 1) * P], self.slots[:, 4, k, :],
                             start=(k == 0), stop=(k == KT - 1), skip_group_check=True)
        cq = pe.mark(q)
        for s in (4, 5):
            self.refill(s, U_UK + s - 4, cq)
        ck = al("ck", [P, NT, UC])
        ckt = al("ckt", [P, 2, T])
        qit = al("qit", [P, 2, T])
        kit = al("kit", [P, T])
        wi = al("wi", [P, NT, IH])
        s4 = al("s4", [P, 4])
        rl = al("rl", [P, IH, T])
        work = al("work", [P, T])
        best = al("best", [P, 8])
        mask = al("mask", [P, NT, T])
        need(A, iq)
        act.mark(A.activation(qit[:, :, :], self.bank(5).rearrange("p (k t) -> p k t", k=2), ACT.Copy))
        act.mark(A.activation(kit[:, :], self.bank(6, T), ACT.Copy))
        iq = act.mark(A.activation(wi[:, :, :], self.bank(6, NT * IH, T).rearrange("p (t n) -> p t n", t=NT),
                                   ACT.Copy, scale=IH ** -0.5))
        need(A, cq)
        cq = act.mark(A.activation(ck[:, :, :], self.bank(4).rearrange("p (t n) -> p t n", t=NT), ACT.Copy))
        pairs = ((5, 7), (4, 6))
        sq = []
        need(M, iq, cq)
        for t in range(NT):
            S = (t + 1) * P
            for h in range(IH):
                r = slice(CD * (h % 2), CD * (h % 2) + CD)
                q = M.matmul(self.bank(pairs[t][h % 2], S, (h // 2) * S), qit[r, h // 2, t * P:(t + 1) * P],
                             kit[r, 0:S], start=True, stop=True, skip_group_check=True)
            sq.append(pe.mark(q))
        late = c["late"].rearrange("p (t s) -> p t s", t=NT)
        masked = []
        for t in range(NT):
            S = (t + 1) * P
            need(A, sq[t], *masked)
            for h in range(IH):
                q = act.mark(A.activation(rl[:, h, 0:S], self.bank(pairs[t][h % 2], S, (h // 2) * S), ACT.Relu,
                                          scale=IDIM ** -0.5))
            need(V, q)
            wk, mk = work[:, 0:S], mask[:, t, 0:S]
            v(V.tensor_scalar(mk, rl[:, 0, 0:S], wi[:, t, 0:1], None, ALU.mult))
            for h in range(1, IH):
                q = v(V.scalar_tensor_tensor(mk, rl[:, h, 0:S], wi[:, t, h:h + 1], mk, ALU.mult, ALU.add))
            masked.append(q)
            v(V.tensor_tensor(wk, mk, late[:, t, 0:S], ALU.subtract))
            for r in range(SEL // 8):
                v(V.max(best[:, :], wk))
                v(V.match_replace(wk, best[:, :], wk, TAKEN))
            v(V.tensor_scalar(wk, wk, TAKEN / 2, -BIG, ALU.is_gt, ALU.mult))
            q = v(V.tensor_tensor(mk, wk, late[:, t, 0:S], ALU.subtract))
            need(G, q, biased)
            for g in range(4):
                o = tb[t][:, 4 * g:4 * g + 4, :]
                self.pool.mark(G.tensor_tensor(o, o, mk[:, ::-1].unsqueeze(1).to_broadcast([P, 4, S]), ALU.add))
        for t in range(NT):
            q = act.mark(A.activation(xn[:, 0, 0:UC], ck[:, t], ACT.Square, accum_out=s4[:, t:t + 1]))
            need(A, q)
        q = act.mark(A.activation(s4[:, 0:NT], s4[:, 0:NT], ACT.Ln, scale=1.0 / UC, bias=self.col(0)))
        need(A, q)
        q = act.mark(A.activation(s4[:, 0:NT], s4[:, 0:NT], ACT.Exp, scale=-0.5))
        need(A, q)
        for t in range(NT):
            cq = act.mark(A.activation(ck[:, t], ck[:, t], ACT.Copy, scale=s4[:, t:t + 1]))
        pqv = pq[:, :, :, :].rearrange("p s t n -> p (s t) n")

        def keep(cg, b, q):
            need(A, q)
            return self.kept.mark(A.activation(pqv[:, bass.ds((cg // 4) * 2, 2), bass.ds((cg % 4) * UC, UC)],
                                         self.bank(b).rearrange("p (t n) -> p t n", t=NT), ACT.Copy))

        self.project("odd_in", U_OIN, 8, 1, self.xt, keep)
        qT, kT = self.yt[:, 0:8], self.yt[:, 8:16]
        sh = al("sh", [P, 2, NT, CH])
        tv = self.xt[:, :, :].rearrange("p k t -> p (k t)").rearrange("p (t h d) -> p t h d", t=NT, h=CH)
        byh = lambda x: x.rearrange("p t (h d) -> p t h d", h=CH)

        def squares(n, src):
            v(V.tensor_tensor(tv, byh(src), byh(src), ALU.mult))
            v(V.tensor_reduce(sh[:, n], tv, AX, ALU.add))

        def expand(s, dst):
            w = self.slots[:, s].rearrange("p a b -> p (a b)").rearrange("p (f n) -> p f n", f=2)
            for t in range(NT):
                b0 = 2 * (s - 4) + 4 * t
                for b in range(2):
                    for f in range(2):
                        m = M.matmul(self.bank(b0 + b), ckt[:, f, t * P:(t + 1) * P],
                                     w[:, f, b * 512:(b + 1) * 512], start=(f == 0), stop=(f == 1),
                                     skip_group_check=True)
                m = pe.mark(m)
                need(A, m)
                q = act.mark(A.activation(dst[:, t].rearrange("p (b n) -> p b n", b=2), self.ps[:, b0:b0 + 2], ACT.Copy))
            return q

        need(M, act.now(), self.kept.now())
        need(V, act.now(), self.kept.now(), pe.now())
        squares(0, pq[:, 0])
        q = self.turn(ck, ckt, 2, [cq], [4], fcol(F_KV))
        zq = act.mark(A.activation(pq[:, 1], pq[:, 1], ACT.Silu))
        need(M, q, self.arrived[4].now(), self.arrived[5].now())
        q = expand(4, kk)
        need(V, q)
        squares(1, kk)
        need(A, dve.now())
        q = act.mark(A.activation(sh[:, :, :, :], sh[:, :, :, :], ACT.Ln, scale=1.0 / CD, bias=self.col(0)))
        need(A, q)
        q = act.mark(A.activation(sh[:, :, :, :], sh[:, :, :, :], ACT.Exp, scale=-0.5))
        need(V, q)
        scaled = []
        for n, src in ((0, pq[:, 0]), (1, kk)):
            for t in range(NT):
                sv = byh(src)[:, t]
                q = dve.mark(V.tensor_tensor(sv, sv, sh[:, n, t].unsqueeze(2).to_broadcast([P, CH, CD]), ALU.mult))
            scaled.append(q)
        expand(5, vv)
        need(M, act.now())
        self.turn(pq[:, 0], qT, KT, [scaled[0]], [4, 5], lambda k: feat[:, F_Q:F_Q + 1])
        self.turn(kk, kT, KT, [scaled[1]], [6, 7], lambda k: feat[:, F_K:F_K + 1])
        self.p.barrier()
        lgs = [al(f"lg{n}", [P, 4, T]) for n in range(2)]
        pt = al("weights", [P, 4, NT, P])
        mx = al("mx", [P, NT, CH])
        dn = al("dn", [P, NT, CH])
        out = xn
        read = {}

        def logits(n, t, g):
            S, lg = (t + 1) * P, lgs[n % 2]
            need(M, read.get("logits"))
            for j in range(4):
                h = 4 * g + j
                r = slice(CD * (h % 2), CD * (h % 2) + CD)
                q = M.matmul(self.bank(h % 2, S, (j // 2) * S), qT[r, h // 2, t * P:(t + 1) * P],
                             kT[r, h // 2, 0:S], start=True, stop=True, skip_group_check=True)
            q = pe.mark(q)
            need(V, q, read.get(f"turned{n % 2}"))
            for b in range(2):
                q = dve.mark(V.scalar_tensor_tensor(
                    lg[:, b::2, 0:S], self.bank(b, 2 * S).rearrange("p (h s) -> p h s", h=2), CD ** -0.5,
                    tb[t][:, 4 * g + b:4 * g + 4:2, ::-1], ALU.mult, ALU.add))
            read["logits"] = q
            need(V, q)
            m = mx[:, t, 4 * g:4 * g + 4]
            v(V.tensor_reduce(m, lg[:, :, 0:S], AX, ALU.max))
            return dve.mark(V.tensor_scalar(m, m, -1.0, None, ALU.mult))

        def weights(n, t, g, ready):
            S, lg = (t + 1) * P, lgs[n % 2]
            need(A, ready)
            for j in range(4):
                h = 4 * g + j
                q = act.mark(A.activation(lg[:, j, 0:S], lg[:, j, 0:S], ACT.Exp, bias=mx[:, t, h:h + 1],
                                          accum_out=dn[:, t, h:h + 1]))
            return q

        def values(n, t, g, ready):
            lg = lgs[n % 2]
            need(M, ready, read.get("weights"))
            for j in range(4):
                for s in range(t + 1):
                    q = M.transpose(self.bank(2 + j // 2, P, ((j % 2) * 2 + s) * P), lg[:, j, s * P:(s + 1) * P],
                                    c["ident"])
            q = pe.mark(q)
            read[f"turned{n % 2}"] = q
            need(A, q, read.get("products"))
            for b in range(2):
                q = act.mark(A.activation(pt[:, 2 * b:2 * b + 2, 0:t + 1], self.bank(2 + b).rearrange(
                    "p (h s j) -> p h s j", h=2, s=2)[:, :, 0:t + 1], ACT.Copy))
            read["weights"] = q
            need(M, q)
            for j in range(4):
                h = 4 * g + j
                for s in range(t + 1):
                    q = M.matmul(self.bank(4 + 2 * t + h // 8, CD, (h % 8) * CD), pt[:, j, s, :],
                                 vv[:, s, h * CD:(h + 1) * CD], start=(s == 0), stop=(s == t),
                                 skip_group_check=True)
            q = read["products"] = pe.mark(q)
            if g == 3:
                need(V, q, ready, zq)
                v(V.reciprocal(dn[:, t], dn[:, t]))
                v(V.tensor_tensor(out[:, t].rearrange("p (h d) -> p h d", h=CH),
                                  self.ps[:, 4 + 2 * t:6 + 2 * t].rearrange("p b (h d) -> p (b h) d", h=8),
                                  dn[:, t].unsqueeze(2).to_broadcast([P, CH, CD]), ALU.mult))
                v(V.tensor_tensor(out[:, t], out[:, t], pq[:, 1, t], ALU.mult))

        before = None
        for n in range(4 * NT):
            t, g = n // 4, n % 4
            ready = logits(n, t, g)
            if before:
                values(*before)
            before = (n, t, g, weights(n, t, g, ready))
        values(*before)
        q = self.turn(out, self.xt, KT, [dve.now()], [0, 1])
        need(M, q)
        self.project("odd_out", UNITS, 4, 1, self.xt, self.add_to_x)
        self.need(nc.sync, dve.now())
        o = self.stored.mark(nc.sync.dma_start(self.out.rearrange("a (n p) d -> p (a n) d", p=P), self.x[:, :, :]))
        self.need(nc.sync, o)

    def bias_src(self, t):
        return bass.AP(self.bias_rows.tensor, P, [[1, P], [2 * T, CH], [1, (t + 1) * P]])

    def add_to_x(self, cg, b, q):
        self.need(self.nc.vector, q)
        cols = self.x[:, :, bass.ds(cg * UC, UC)]
        return self.dve.mark(self.nc.vector.tensor_tensor(
            cols, cols, self.bank(b).rearrange("p (t n) -> p t n", t=NT), ALU.add))

    def note(self, loop, name, point):
        base = self.p.starts[point.line.name]
        self.p.found.setdefault("notes", {})[(loop, name)] = (point.line.name, point.value - base)
        self.last[(loop, name)] = point

    def behind(self, loop, name):
        if self.p.loop is None:
            return self.last.get((loop, name))
        got = self.p.per.get("notes", {}).get((loop, name))
        if got is None:
            return None
        line = next(l for l in self.p.lines if l.name == got[0])
        return Point(line, self.p.starts[line.name] + got[1] - self.p.loop.per[line.name], self.p.loop)


def pack_units(w, rows_of_tiles=None):
    K, N = w.shape
    return w.reshape(K // D, KT, P, N // UC, UC).transpose(0, 3, 2, 1, 4)


def layout(I):
    A = {}
    w = I["gdn_w_in"][0]
    kw = QKH * HD
    sec = {"q": w[:, 0:kw], "k": w[:, kw:2 * kw], "v": w[:, 2 * kw:2 * kw + VH * HD],
           "z": w[:, 2 * kw + VH * HD:2 * kw + 2 * VH * HD]}
    heads = []
    for h in range(QKH):
        parts = [np.concatenate([sec["q"][:, h * HD:(h + 1) * HD], sec["k"][:, h * HD:(h + 1) * HD]], 1),
                 sec["v"][:, h * UC:(h + 1) * UC], sec["z"][:, h * UC:(h + 1) * UC]]
        heads.append(np.stack([pack_units(q)[0, 0] for q in parts]))
    cols = lambda w: pack_units(w)[0]
    halves = lambda w: pack_units(w).transpose(1, 0, 2, 3, 4).reshape(-1, P, KT, UC)
    wide = lambda w: w.reshape(2, P, D).transpose(1, 0, 2).reshape(P, KT, UC)
    wg, wup = (I[n][0].reshape(EXPERTS, KT, P, HID).transpose(0, 2, 1, 3) for n in ("moe_w_gate", "moe_w_up"))
    wdn = I["moe_w_down"][0].reshape(EXPERTS, 2, P, D).transpose(0, 2, 1, 3).reshape(EXPERTS, P, KT, UC)
    e = I["e_w_in_2"][0]
    g0, e1 = 5 * D, 5 * D + 2 * AH
    o = I["o_w_in_2"][0]
    ck, ki = D, D + 512
    units = np.concatenate([
        np.concatenate(heads), halves(I["gdn_w_out"][0]),
        np.stack([wg, wup, wdn], 1).reshape(3 * EXPERTS, P, KT, UC),
        cols(I["pe_w_gate"][0]), wide(I["pe_w_proj"][0])[None],
        I["e_w_pool_2"][0].reshape(4, 2, P, 256).transpose(2, 0, 1, 3).reshape(1, P, KT, UC),
        cols(e[:, :3 * D]), cols(e[:, 4 * D:g0]), cols(e[:, e1 + D:]), cols(e[:, 3 * D:4 * D]), cols(e[:, e1:e1 + D]),
        halves(I["e_w_out_2"][0]),
        cols(o[:, :D]), cols(o[:, ki + 68:]), cols(I["o_w_out_2"][0]),
        wide(I["o_w_uk_2"][0])[None], wide(I["o_w_uv_2"][0])[None], cols(o[:, ck:ki])])
    assert len(units) == UNITS
    A["wu"] = units
    ktile = lambda w: w.reshape(KT, P, -1).transpose(1, 0, 2)
    A["w_route"] = ktile(np.concatenate([I["moe_w_group"][0], I["moe_w_router"][0]], 1))
    A["b_route"] = np.concatenate([I["moe_b_group"], I["moe_b_router"]], 1)
    A["w_if"] = ktile(e[:, g0:e1])
    A["w_ki"] = ktile(np.concatenate([o[:, ki:ki + 64], o[:, ki:ki + 68]], 1))
    A["pt"] = I["p"][0, 0].T.reshape(2, P, T).transpose(1, 0, 2)
    A["ecw"] = I["e_conv_2"][0].reshape(4, 16, P).transpose(2, 1, 0)
    feat = lambda v: v.reshape(-1, P).T
    A["feat"] = np.concatenate([feat(I["e_norm_2"][0]), feat(I["o_norm_2"][0]), feat(I["e_g_head_2"][0]),
                                feat(I["e_s_pool_2"][0]), feat(I["o_g_kv_2"][0]),
                                feat(np.tile(I["o_g_q_2"][0], 2)), feat(np.tile(I["o_g_k_2"][0], 2))], 1)
    A["wab"] = w[:, 2 * kw + 2 * VH * HD:].reshape(KT, P, 64).transpose(1, 0, 2)
    c = I["gdn_conv_w"][0]
    q, k, v = c[:, :kw], c[:, kw:2 * kw], c[:, 2 * kw:]
    cw = np.stack([q.reshape(TAPS, QKH, HD), k.reshape(TAPS, QKH, HD),
                   v.reshape(TAPS, QKH, 2, HD)[:, :, 0], v.reshape(TAPS, QKH, 2, HD)[:, :, 1]], 2)
    A["cw"] = cw.transpose(3, 1, 2, 0).reshape(P, QKH, 4 * TAPS)
    A["xt"] = I["x"][0].T.reshape(KT, P, T).transpose(1, 0, 2)
    return A


KEEP = ["x", "gdn_a_log", "gdn_dt_bias", "gdn_norm_w", "ln_g", "ln_b", "e_b_if_2", "rel_bias_2"]


def arrays_of(inputs):
    I = {k: np.asarray(v) for k, v in inputs.items()}
    A = layout(I)
    for k in KEEP:
        A[k] = I[k]
    for g, v in constants().items():
        A["c_" + g] = np.concatenate(list(v.values()), 1)
    return {k: np.ascontiguousarray(v) for k, v in A.items()}


def program(nc, shapes, per):
    ins = {k: nc.dram_tensor("in_" + k, s, F32, kind="ExternalInput").ap() for k, s in shapes.items()}
    out = nc.dram_tensor("out", (1, T, D), F32, kind="ExternalOutput").ap()
    return Build(nc, ins, out, per).p.found


def kernel(**inputs):
    import concourse.bacc as bacc
    from concourse.bass_utils import run_bass_kernel_spmd
    A = arrays_of(inputs)
    shapes = {k: v.shape for k, v in A.items()}
    counts = {}
    for _ in range(2):
        nc = bacc.Bacc("TRN2", target_bir_lowering=False, num_devices=1)
        counts = program(nc, shapes, counts)
    r = run_bass_kernel_spmd(nc, [{"in_" + k: v for k, v in A.items()}], core_ids=[0])
    return r.results[0]["out"]
```
